# Optimizing a Trainium2 kernel written in Bass

```python
import math
import jax
import jax.numpy as jnp
from jax import lax
import numpy as np

D_MODEL = 1024
BATCH = 1
SEQ = 128
DEPTH = 2
DEC_BATCH = 1
DEC_SEQ = 256
PAST_LEN = 128

GRID_W = 64
N_EVEN = (DEPTH + 1) // 2
N_ODD = DEPTH // 2
CHUNK = 128
Q_BLOCK = 128
RET_HEADS = 4
RET_DK = 128
RET_DV = 128
ML_HEADS = 4
ML_DK = 128
ML_DV = 128
GQA_HEADS = 8
GQA_KV_HEADS = 2
GQA_HD = 64
DIFF_HEADS = 4
DIFF_DH = 64
ROPE_THETA = 10000.0
PEER_HEADS = 8
N_KEYS = 128
N_EXPERTS = N_KEYS * N_KEYS
PK_DIM = 256
PK_TOPK = 16
PEER_BLOCK = 128
N_MOD = 6
ALPHA = (2 * DEPTH) ** 0.25
BETA = (8 * DEPTH) ** -0.25
LN_EPS = 1e-5
RMS_EPS = 1e-6
EVEN_WIDTHS = (RET_HEADS * RET_DK, RET_HEADS * RET_DK, RET_HEADS * RET_DV, RET_HEADS * RET_DV,
               ML_HEADS * ML_DK, ML_HEADS * ML_DK, ML_HEADS * ML_DV, ML_HEADS * ML_DV, 4 * ML_HEADS)
EVEN_IN = sum(EVEN_WIDTHS)
EVEN_MIX = RET_HEADS * RET_DV + ML_HEADS * ML_DV
ODD_WIDTHS = (GQA_HEADS * GQA_HD, GQA_KV_HEADS * GQA_HD, GQA_KV_HEADS * GQA_HD,
              DIFF_HEADS * 2 * DIFF_DH, DIFF_HEADS * 2 * DIFF_DH, DIFF_HEADS * 2 * DIFF_DH)
ODD_IN = sum(ODD_WIDTHS)
ODD_MIX = GQA_HEADS * GQA_HD + DIFF_HEADS * 2 * DIFF_DH

kernel_name = "hybrid_diffusion_retention_mlstm_gqa_diffattn_peer_step"

def _split(z, widths):
    out, start = [], 0
    for w in widths:
        out.append(z[..., start:start + w])
        start += w
    return out

def _layer_norm(x, g, b):
    xf = x.astype(jnp.float32)
    mu = jnp.mean(xf, -1, keepdims=True)
    var = jnp.mean(jnp.square(xf - mu), -1, keepdims=True)
    y = (xf - mu) * lax.rsqrt(var + LN_EPS)
    return (y * g.astype(jnp.float32) + b.astype(jnp.float32)).astype(x.dtype)

def _rms_norm(x, g):
    xf = x.astype(jnp.float32)
    y = xf * lax.rsqrt(jnp.mean(jnp.square(xf), -1, keepdims=True) + RMS_EPS)
    return (y * g.astype(jnp.float32)).astype(x.dtype)

def _head_norm(o, g, dtype):
    mu = jnp.mean(o, -1, keepdims=True)
    var = jnp.mean(jnp.square(o - mu), -1, keepdims=True)
    y = ((o - mu) * lax.rsqrt(var + LN_EPS)).reshape(o.shape[:2] + (-1,))
    return (y * g.astype(jnp.float32)).astype(dtype)

def _modulation(cond, w, b):
    m = jax.nn.silu(cond) @ w + b
    return [a[:, None, :] for a in jnp.split(m, N_MOD, axis=-1)]

def _modulate(x, shift, scale):
    return x * (1.0 + scale) + shift

def _axial_rope(x):
    n = x.shape[1]
    rows = n // GRID_W
    row = jnp.repeat(jnp.arange(rows, dtype=jnp.float32), GRID_W)
    col = jnp.tile(jnp.arange(GRID_W, dtype=jnp.float32), rows)
    half = x.shape[-1] // 2
    nf = half // 2
    inv = ROPE_THETA ** (-jnp.arange(nf, dtype=jnp.float32) / nf)

    def rot(xa, pos):
        ang = pos[:, None] * inv[None, :]
        cos = jnp.cos(ang)[None, :, None, :]
        sin = jnp.sin(ang)[None, :, None, :]
        x1 = xa[..., :nf].astype(jnp.float32)
        x2 = xa[..., nf:].astype(jnp.float32)
        return jnp.concatenate([x1 * cos - x2 * sin, x1 * sin + x2 * cos], axis=-1)

    return jnp.concatenate([rot(x[..., :half], row), rot(x[..., half:], col)], axis=-1).astype(x.dtype)

def _to_chunks(a):
    B, T = a.shape[:2]
    a = a.astype(jnp.float32).reshape((B, T // CHUNK, CHUNK) + a.shape[2:])
    return jnp.moveaxis(jnp.moveaxis(a, 1, 0), 3, 2)

def _from_chunks(o):
    n, B, H, L = o.shape[:4]
    return jnp.moveaxis(jnp.moveaxis(o, 2, 3), 0, 1).reshape((B, n * L, H) + o.shape[4:])

def _retention_scan(q, k, v, log_gamma, s0):
    idx = jnp.arange(CHUNK, dtype=jnp.float32)
    rel = idx[:, None] - idx[None, :]
    intra = jnp.where(rel >= 0, jnp.exp(jnp.maximum(rel, 0.0) * log_gamma[:, None, None]), 0.0)
    q_decay = jnp.exp((idx + 1.0) * log_gamma[:, None])[..., None]
    k_decay = jnp.exp((CHUNK - 1.0 - idx) * log_gamma[:, None])[..., None]
    c_decay = jnp.exp(CHUNK * log_gamma)[:, None, None]

    def step(s, inp):
        qc, kc, vc = inp
        att = jnp.einsum("bhld,bhmd->bhlm", qc, kc) * intra
        o = jnp.einsum("bhlm,bhme->bhle", att, vc) + jnp.einsum("bhld,bhde->bhle", qc, s) * q_decay
        s = s * c_decay + jnp.einsum("bhld,bhle->bhde", kc * k_decay, vc)
        return s, o

    s, o = lax.scan(step, s0.astype(jnp.float32), (_to_chunks(q), _to_chunks(k), _to_chunks(v)))
    return _from_chunks(o), s

def _mlstm_scan(q, k, v, log_i, log_f, c0, n0, m0):
    causal = jnp.tril(jnp.ones((CHUNK, CHUNK), dtype=bool))

    def step(carry, inp):
        c, n, m = carry
        qc, kc, vc, li, lf = inp
        b = jnp.cumsum(lf, axis=-1)
        a = b + m[..., None]
        d = jnp.where(causal, b[..., :, None] - b[..., None, :] + li[..., None, :], -jnp.inf)
        m_t = jnp.maximum(a, jnp.max(d, axis=-1))
        w_state = jnp.exp(a - m_t)
        w = jnp.einsum("bhld,bhmd->bhlm", qc, kc) * jnp.exp(d - m_t[..., None])
        num = jnp.einsum("bhlm,bhme->bhle", w, vc) + w_state[..., None] * jnp.einsum("bhld,bhde->bhle", qc, c)
        den = jnp.sum(w, axis=-1) + w_state * jnp.einsum("bhld,bhd->bhl", qc, n)
        h = num / jnp.maximum(jnp.abs(den), jnp.exp(-m_t))[..., None]
        b_last = b[..., -1]
        g = b_last[..., None] - b + li
        m_new = jnp.maximum(b_last + m, jnp.max(g, axis=-1))
        w_old = jnp.exp(b_last + m - m_new)
        w_in = jnp.exp(g - m_new[..., None])
        c = w_old[..., None, None] * c + jnp.einsum("bhl,bhld,bhle->bhde", w_in, kc, vc)
        n = w_old[..., None] * n + jnp.einsum("bhl,bhld->bhd", w_in, kc)
        return (c, n, m_new), h

    init = (c0.astype(jnp.float32), n0.astype(jnp.float32), m0.astype(jnp.float32))
    xs = (_to_chunks(q), _to_chunks(k), _to_chunks(v), _to_chunks(log_i), _to_chunks(log_f))
    (c, n, m), h = lax.scan(step, init, xs)
    return _from_chunks(h), c, n, m

def _even_mix(h, w_in, b_gate, ret_logit, ret_gn_g, ml_gn_g, w_out, s_ret, s_c, s_n, s_m):
    B, T, _ = h.shape
    rq, rk, rv, rg, mq, mk, mv, mo, zg = _split(h @ w_in, EVEN_WIDTHS)
    rq = rq.reshape(B, T, RET_HEADS, RET_DK)
    rk = rk.reshape(B, T, RET_HEADS, RET_DK) * RET_DK ** -0.5
    rv = rv.reshape(B, T, RET_HEADS, RET_DV)
    mq = mq.reshape(B, T, ML_HEADS, ML_DK)
    mk = mk.reshape(B, T, ML_HEADS, ML_DK) * ML_DK ** -0.5
    mv = mv.reshape(B, T, ML_HEADS, ML_DV)
    gates = (zg + b_gate).astype(jnp.float32).reshape(B, T, 4, ML_HEADS)
    li_f, lf_f = gates[:, :, 0], jax.nn.log_sigmoid(gates[:, :, 1])
    li_b, lf_b = gates[:, :, 2], jax.nn.log_sigmoid(gates[:, :, 3])
    log_gamma = jax.nn.log_sigmoid(ret_logit.astype(jnp.float32))

    def fl(a):
        return jnp.flip(a, axis=1)

    o_f, sr_f = _retention_scan(rq, rk, rv, log_gamma[0], s_ret[:, 0])
    o_b, sr_b = _retention_scan(fl(rq), fl(rk), fl(rv), log_gamma[1], s_ret[:, 1])
    h_f, c_f, n_f, m_f = _mlstm_scan(mq, mk, mv, li_f, lf_f, s_c[:, 0], s_n[:, 0], s_m[:, 0])
    h_b, c_b, n_b, m_b = _mlstm_scan(fl(mq), fl(mk), fl(mv), fl(li_b), fl(lf_b), s_c[:, 1], s_n[:, 1], s_m[:, 1])
    ret = _head_norm(o_f + fl(o_b), ret_gn_g, h.dtype) * jax.nn.silu(rg)
    o_gate = jax.nn.sigmoid(mo.astype(jnp.float32)).reshape(B, T, ML_HEADS, ML_DV)
    mls = _head_norm(o_gate * (h_f + fl(h_b)), ml_gn_g, h.dtype)
    y = jnp.concatenate([ret, mls], axis=-1) @ w_out
    states = (jnp.stack([sr_f, sr_b], axis=1), jnp.stack([c_f, c_b], axis=1),
              jnp.stack([n_f, n_b], axis=1), jnp.stack([m_f, m_b], axis=1))
    return y, states

def _q_blocks(q):
    B, T = q.shape[:2]
    return jnp.moveaxis(q.reshape((B, T // Q_BLOCK, Q_BLOCK) + q.shape[2:]), 1, 0)

def _from_q_blocks(o):
    nb, B, Q = o.shape[:3]
    return jnp.moveaxis(o, 0, 1).reshape((B, nb * Q) + o.shape[3:])

def _gqa_attend(q, k, v):
    B, T, H, d = q.shape
    G = H // GQA_KV_HEADS

    def one(qc):
        s = jnp.einsum("bqkgd,bskd->bkgqs", qc, k).astype(jnp.float32) * d ** -0.5
        p = jax.nn.softmax(s, axis=-1).astype(v.dtype)
        return jnp.einsum("bkgqs,bskd->bqkgd", p, v)

    o = lax.map(one, _q_blocks(q.reshape(B, T, GQA_KV_HEADS, G, d)))
    return _from_q_blocks(o).reshape(B, T, H, d)

def _diff_attend(q, k, v, lam):
    d = q.shape[-1]

    def one(qc):
        s = jnp.einsum("bqhcd,bshcd->bhcqs", qc, k).astype(jnp.float32) * d ** -0.5
        p = jax.nn.softmax(s, axis=-1)
        a = (p[:, :, 0] - lam * p[:, :, 1]).astype(v.dtype)
        return jnp.einsum("bhqs,bshe->bqhe", a, v)

    return _from_q_blocks(lax.map(one, _q_blocks(q)))

def _odd_mix(h, w_in, qn_g, kn_g, lam_p, subln_g, w_out, lam_init, ctx=None):
    B, T, _ = h.shape
    gq, gk, gv, dq, dk, dv = _split(h @ w_in, ODD_WIDTHS)
    gq = _rms_norm(gq.reshape(B, T, GQA_HEADS, GQA_HD), qn_g)
    gk = _rms_norm(gk.reshape(B, T, GQA_KV_HEADS, GQA_HD), kn_g)
    gv = gv.reshape(B, T, GQA_KV_HEADS, GQA_HD)
    dq = dq.reshape(B, T, DIFF_HEADS * 2, DIFF_DH)
    dk = dk.reshape(B, T, DIFF_HEADS * 2, DIFF_DH)
    dv = dv.reshape(B, T, DIFF_HEADS, 2 * DIFF_DH)
    if ctx is None:
        own = (gk, gv, dk.reshape(B, T, DIFF_HEADS, 2, DIFF_DH), dv)
        keys = own
    else:
        gq, gk, dq, dk = _axial_rope(gq), _axial_rope(gk), _axial_rope(dq), _axial_rope(dk)
        own = None
        lat = (gk, gv, dk.reshape(B, T, DIFF_HEADS, 2, DIFF_DH), dv)
        keys = [jnp.concatenate([a, b.astype(a.dtype)], axis=1) for a, b in zip(lat, ctx)]
    lp = lam_p.astype(jnp.float32)
    lam = jnp.exp(jnp.sum(lp[0] * lp[1])) - jnp.exp(jnp.sum(lp[2] * lp[3])) + lam_init
    o_g = _gqa_attend(gq, keys[0], keys[1]).reshape(B, T, GQA_HEADS * GQA_HD)
    o_d = _diff_attend(dq.reshape(B, T, DIFF_HEADS, 2, DIFF_DH), keys[2], keys[3], lam)
    o_d = (_rms_norm(o_d, subln_g) * (1.0 - lam_init)).reshape(B, T, DIFF_HEADS * 2 * DIFF_DH)
    y = jnp.concatenate([o_g, o_d], axis=-1) @ w_out
    return y, own

def _peer(h, w_q, sub_keys, u_tab, v_tab):
    B, T, D = h.shape
    N = B * T
    x = h.reshape(N, D)
    q = (x @ w_q).reshape(N, PEER_HEADS, 2, PK_DIM // 2)
    s = jnp.einsum("nhcd,ckd->nhck", q, sub_keys).astype(jnp.float32)
    s1, i1 = lax.top_k(s[:, :, 0], PK_TOPK)
    s2, i2 = lax.top_k(s[:, :, 1], PK_TOPK)
    cand_s = (s1[..., :, None] + s2[..., None, :]).reshape(N, PEER_HEADS, PK_TOPK * PK_TOPK)
    cand_i = (i1[..., :, None] * N_KEYS + i2[..., None, :]).reshape(N, PEER_HEADS, PK_TOPK * PK_TOPK)
    top_s, pos = lax.top_k(cand_s, PK_TOPK)
    idx = jnp.take_along_axis(cand_i, pos, axis=-1)
    gate = jax.nn.softmax(top_s, axis=-1).astype(h.dtype)
    nb = N // PEER_BLOCK

    def one(args):
        xb, ib, gb = args
        act = jax.nn.gelu(jnp.einsum("thkd,td->thk", u_tab[ib], xb)) * gb
        return jnp.einsum("thk,thkd->td", act, v_tab[ib])

    out = lax.map(one, (x.reshape(nb, PEER_BLOCK, D),
                        idx.reshape(nb, PEER_BLOCK, PEER_HEADS, PK_TOPK),
                        gate.reshape(nb, PEER_BLOCK, PEER_HEADS, PK_TOPK)))
    return out.reshape(B, T, D)

def setup_inputs(seed: int = 0) -> dict:
    key = jax.random.key(seed)
    ks = jax.random.split(key, 40)
    f32 = jnp.float32

    def nrm(i, shape, scale=1.0):
        return scale * jax.random.normal(ks[i], shape, f32)

    i_bias = nrm(17, (N_EVEN, 2, ML_HEADS), 0.1)
    f_bias = jnp.linspace(3.0, 6.0, ML_HEADS, dtype=f32) + nrm(18, (N_EVEN, 2, ML_HEADS), 0.1)
    even_b_gate = jnp.stack([i_bias, f_bias], axis=2).reshape(N_EVEN, 4 * ML_HEADS)
    ret_base = jnp.log(2.0 ** (5.0 + jnp.arange(RET_HEADS, dtype=f32)) - 1.0)
    return {
        "x_prompt": nrm(0, (BATCH, SEQ, D_MODEL)),
        "x_sample": nrm(1, (DEC_BATCH, DEC_SEQ, D_MODEL)),
        "state_ret": nrm(2, (DEC_BATCH, N_EVEN, 2, RET_HEADS, RET_DK, RET_DV), 0.5),
        "state_mlstm_C": nrm(3, (DEC_BATCH, N_EVEN, 2, ML_HEADS, ML_DK, ML_DV), 0.5),
        "state_mlstm_n": nrm(4, (DEC_BATCH, N_EVEN, 2, ML_HEADS, ML_DK), 0.5),
        "state_mlstm_m": nrm(5, (DEC_BATCH, N_EVEN, 2, ML_HEADS)),
        "cache_gqa_k": nrm(6, (DEC_BATCH, N_ODD, PAST_LEN, GQA_KV_HEADS, GQA_HD)),
        "cache_gqa_v": nrm(7, (DEC_BATCH, N_ODD, PAST_LEN, GQA_KV_HEADS, GQA_HD)),
        "cache_diff_k": nrm(8, (DEC_BATCH, N_ODD, PAST_LEN, DIFF_HEADS, 2, DIFF_DH)),
        "cache_diff_v": nrm(9, (DEC_BATCH, N_ODD, PAST_LEN, DIFF_HEADS, 2 * DIFF_DH)),
        "c": nrm(10, (DEC_BATCH, D_MODEL)),
        "c_ctx": nrm(11, (D_MODEL,)),
        "ada_w": nrm(12, (DEPTH, D_MODEL, N_MOD * D_MODEL), 0.5 * D_MODEL ** -0.5),
        "ada_b": nrm(13, (DEPTH, N_MOD * D_MODEL), 0.01),
        "ln_g": 1.0 + nrm(14, (DEPTH, 2, D_MODEL), 0.01),
        "ln_b": nrm(15, (DEPTH, 2, D_MODEL), 0.01),
        "even_w_in": nrm(16, (N_EVEN, D_MODEL, EVEN_IN), D_MODEL ** -0.5),
        "even_b_gate": even_b_gate,
        "ret_decay_logit": ret_base + nrm(19, (N_EVEN, 2, RET_HEADS), 0.1),
        "ret_gn_g": 1.0 + nrm(20, (N_EVEN, RET_HEADS * RET_DV), 0.01),
        "ml_gn_g": 1.0 + nrm(21, (N_EVEN, ML_HEADS * ML_DV), 0.01),
        "even_w_out": nrm(22, (N_EVEN, EVEN_MIX, D_MODEL), BETA * EVEN_MIX ** -0.5),
        "odd_w_in": nrm(23, (N_ODD, D_MODEL, ODD_IN), D_MODEL ** -0.5),
        "q_norm_g": 1.0 + nrm(24, (N_ODD, GQA_HD), 0.01),
        "k_norm_g": 1.0 + nrm(25, (N_ODD, GQA_HD), 0.01),
        "diff_lambda": nrm(26, (N_ODD, 4, DIFF_DH), 0.1),
        "diff_subln_g": 1.0 + nrm(27, (N_ODD, 2 * DIFF_DH), 0.01),
        "odd_w_out": nrm(28, (N_ODD, ODD_MIX, D_MODEL), BETA * ODD_MIX ** -0.5),
        "peer_w_q": nrm(29, (DEPTH, D_MODEL, PEER_HEADS * PK_DIM), D_MODEL ** -0.5),
        "peer_sub_keys": nrm(30, (DEPTH, 2, N_KEYS, PK_DIM // 2), (PK_DIM // 2) ** -0.5),
        "peer_u": nrm(31, (DEPTH, N_EXPERTS, D_MODEL), D_MODEL ** -0.5),
        "peer_v": nrm(32, (DEPTH, N_EXPERTS, D_MODEL), BETA),
    }

def reference(x_prompt, x_sample, state_ret, state_mlstm_C, state_mlstm_n, state_mlstm_m,
              cache_gqa_k, cache_gqa_v, cache_diff_k, cache_diff_v, c,
              c_ctx, ada_w, ada_b, ln_g, ln_b,
              even_w_in, even_b_gate, ret_decay_logit, ret_gn_g, ml_gn_g, even_w_out,
              odd_w_in, q_norm_g, k_norm_g, diff_lambda, diff_subln_g, odd_w_out,
              peer_w_q, peer_sub_keys, peer_u, peer_v):
    xp, xs = x_prompt, x_sample
    bp = xp.shape[0]
    f32 = jnp.float32
    new_ret, new_c, new_n, new_m = [], [], [], []
    new_gk, new_gv, new_dk, new_dv = [], [], [], []
    for l in range(DEPTH):
        mod_p = _modulation(c_ctx[None, :], ada_w[l], ada_b[l])
        mod_s = _modulation(c, ada_w[l], ada_b[l])
        hp = _modulate(xp, mod_p[0], mod_p[1])
        hs = _modulate(xs, mod_s[0], mod_s[1])
        j = l // 2
        if l % 2 == 0:
            zr = jnp.zeros((bp, 2, RET_HEADS, RET_DK, RET_DV), f32)
            zc = jnp.zeros((bp, 2, ML_HEADS, ML_DK, ML_DV), f32)
            zn = jnp.zeros((bp, 2, ML_HEADS, ML_DK), f32)
            zm = jnp.zeros((bp, 2, ML_HEADS), f32)
            ew = (even_w_in[j], even_b_gate[j], ret_decay_logit[j], ret_gn_g[j], ml_gn_g[j], even_w_out[j])
            out_p, (sr, sc, sn, sm) = _even_mix(hp, *ew, zr, zc, zn, zm)
            out_s, _ = _even_mix(hs, *ew, state_ret[:, j], state_mlstm_C[:, j], state_mlstm_n[:, j], state_mlstm_m[:, j])
            new_ret.append(sr)
            new_c.append(sc)
            new_n.append(sn)
            new_m.append(sm)
        else:
            lam_init = 0.8 - 0.6 * math.exp(-0.3 * l)
            ow = (odd_w_in[j], q_norm_g[j], k_norm_g[j], diff_lambda[j], diff_subln_g[j], odd_w_out[j], lam_init)
            out_p, (ck, cv, cdk, cdv) = _odd_mix(hp, *ow)
            out_s, _ = _odd_mix(hs, *ow, ctx=(cache_gqa_k[:, j], cache_gqa_v[:, j], cache_diff_k[:, j], cache_diff_v[:, j]))
            new_gk.append(ck)
            new_gv.append(cv)
            new_dk.append(cdk)
            new_dv.append(cdv)
        xp = _layer_norm(ALPHA * xp + mod_p[2] * out_p, ln_g[l, 0], ln_b[l, 0])
        xs = _layer_norm(ALPHA * xs + mod_s[2] * out_s, ln_g[l, 0], ln_b[l, 0])
        pw = (peer_w_q[l], peer_sub_keys[l], peer_u[l], peer_v[l])
        fp = _peer(_modulate(xp, mod_p[3], mod_p[4]), *pw)
        fs = _peer(_modulate(xs, mod_s[3], mod_s[4]), *pw)
        xp = _layer_norm(ALPHA * xp + mod_p[5] * fp, ln_g[l, 1], ln_b[l, 1])
        xs = _layer_norm(ALPHA * xs + mod_s[5] * fs, ln_g[l, 1], ln_b[l, 1])
    new_state_ret = jnp.stack(new_ret, axis=1)
    new_state_mlstm_C = jnp.stack(new_c, axis=1)
    new_state_mlstm_n = jnp.stack(new_n, axis=1)
    new_state_mlstm_m = jnp.stack(new_m, axis=1)
    new_cache_gqa_k = jnp.stack(new_gk, axis=1)
    new_cache_gqa_v = jnp.stack(new_gv, axis=1)
    new_cache_diff_k = jnp.stack(new_dk, axis=1)
    new_cache_diff_v = jnp.stack(new_dv, axis=1)
    return (xp, xs, new_state_ret, new_state_mlstm_C, new_state_mlstm_n, new_state_mlstm_m,
            new_cache_gqa_k, new_cache_gqa_v, new_cache_diff_k, new_cache_diff_v)


_drawn_inputs = setup_inputs


def setup_inputs(seed=0):
    import zlib

    import numpy as np

    out = dict(_drawn_inputs(seed))
    spreads = {}
    factors = {'state_ret': 3.637,
     'state_mlstm_n': 4.228,
     'state_mlstm_m': 3.263,
     'cache_gqa_k': 8.0,
     'cache_gqa_v': 8.0,
     'cache_diff_k': 3.635,
     'cache_diff_v': 3.314,
     'ret_gn_g': 8.0,
     'ml_gn_g': 8.0,
     'q_norm_g': 8.0,
     'k_norm_g': 5.865,
     'diff_lambda': 7.343,
     'diff_subln_g': 8.0}
    for name, (base, spread) in spreads.items():
        noise = np.random.default_rng([zlib.crc32(name.encode()), seed]).standard_normal(out[name].shape)
        drawn = base * np.exp(spread * noise) if base else spread * noise
        out[name] = jnp.asarray(drawn.astype(out[name].dtype))
    for name, factor in factors.items():
        out[name] = (out[name] * factor).astype(out[name].dtype)
    return out
```

```python
from contextlib import ExitStack
import math

import numpy as np

import concourse.bass as bass
from concourse import mybir
from concourse.alu_op_type import AluOpType as ALU

F32 = mybir.dt.float32
F32R = mybir.dt.float32r
BF16 = mybir.dt.bfloat16
U32 = mybir.dt.uint32
ACT = mybir.ActivationFunctionType
AX = mybir.AxisListType.X

P = 128
D = 1024
KB = D // P
TT = 3
T = TT * P
DEPTH = 2
N_MOD = 6
H = 4
HW = H * P
GQ_HEADS, KV_HEADS, HD = 8, 2, 64
ROPE_HEADS = 26
PH = 8
TOPK = 16
N_KEYS = 128
CH = 512
JC = 4
TG = 32
ALPHA = (2 * DEPTH) ** 0.25
LN_EPS = 1e-5
RMS_EPS = 1e-6
NEG = -3.0e38
LAM_INIT = 0.8 - 0.6 * math.exp(-0.3)
COND = (0, 1, 1)

C_IDENT, C_IOTA, C_KEEPF, C_KEEPB, C_RELF, C_RELB = (P * n for n in range(6))
C_IDX = 6 * P
C_SEL = C_IDX + 2
C_COS = C_SEL + 8 * P
C_SIN = C_COS + 2 * 32
C_ALL = C_SIN + 2 * 32


class Steps:

    def __init__(self, eng, sem):
        self.eng, self.sem, self.n = eng, sem, 0

    def mark(self, ins):
        self.n += 1
        ins.then_inc(self.sem, 1)

    def wait(self):
        self.eng.wait_ge(self.sem, self.n)

    def seq(self, ins):
        self.mark(ins)
        self.wait()


def build(nc, I, O):
    top = ExitStack()
    names = {}
    taken_sems = []

    def renew_semaphores():
        nc.clear_and_free_semaphores(list(taken_sems))
        taken_sems.clear()
        nc.all_engine_barrier()

    def unique(name):
        names[name] = names.get(name, 0) + 1
        return f"{name}_{names[name]}"

    def sb(st, name, shape, dt=F32):
        return st.enter_context(nc.sbuf_tensor(unique(name), shape, dt))

    def ps(st, name, shape, dt=F32):
        return st.enter_context(nc.psum_tensor(unique(name), shape, dt))

    def sem(st, name):
        s = nc.alloc_semaphore(unique(name))
        taken_sems.append(s)
        return s

    with top:
        X = sb(top, "X", [P, TT, D])
        CST = sb(top, "CST", [P, C_ALL])
        MOD = sb(top, "MOD", [P, DEPTH, N_MOD * KB, 2])
        GATE = sb(top, "GATE", [P, 2, D])
        WD = nc.dram_tensor("spread_gates", [P, T // TG, N_KEYS, TG], F32).ap()
        ident = CST[:, C_IDENT:C_IDENT + P]
        iota = CST[:, C_IOTA:C_IOTA + P]

        def modulation():
            with ExitStack() as st:
                SLOTS, BODY, NCH = 3, 6, DEPTH * N_MOD * D // CH
                W = sb(st, "ada_w_ring", [P, SLOTS, KB, CH])
                CT = sb(st, "cond_t", [P, KB, 2])
                E = sb(st, "cond_e", [P, KB, 2])
                B = sb(st, "ada_b_t", [P, DEPTH * N_MOD * KB])
                ROW = sb(st, "mod_rows", [2, BODY, CH])
                PR = ps(st, "mod_row_ps", [P, 2, CH])
                PM = ps(st, "mod_ps", [P, DEPTH * N_MOD * KB * 2])
                w_in = [sem(st, f"ada_w_in{s}") for s in range(SLOTS)]
                small_in, w_used, e_done, v_step, cond_ready, row_ready, turned = (
                    sem(st, n) for n in ("small_in", "ada_w_used", "exp_done", "v_step", "cond_ready", "row_ready", "turned"))
                PER = CH // P * 2
                block = st.enter_context(nc.Block())

                @block.sync
                def _(sp):
                    for s in range(SLOTS):
                        sp.dma_start(W[:, s], I["ada_w"][s]).then_inc(w_in[s], 16)
                    with sp.Fori(1, NCH // SLOTS) as it:
                        for s in range(SLOTS):
                            sp.wait_ge(w_used, it * SLOTS + (s + 1 - SLOTS))
                            sp.dma_start(W[:, s], I["ada_w"][bass.ds(it * SLOTS + s, 1)].rearrange("a p k n -> p (a k) n")).then_inc(w_in[s], 16)

                @block.scalar
                def _(act):
                    act.dma_start(CT[:, :, :], I["cond_t"]).then_inc(small_in, 16)
                    act.dma_start(B[:, :], I["ada_b_t"]).then_inc(small_in, 16)
                    act.dma_start(CST[:, :], I["consts"]).then_inc(small_in, 16)
                    for t in range(TT):
                        act.dma_start(X[:, t, :], I["x"][t]).then_inc(small_in, 16)
                    act.wait_ge(small_in, 96)
                    act.activation(E[:, :, :], CT[:, :, :], ACT.Exp, scale=-1.0).then_inc(e_done, 1)
                    with act.Fori(0, NCH // BODY) as it:
                        for s in range(BODY):
                            act.wait_ge(w_used, it * BODY + (s + 1))
                            if s == 0:
                                act.wait_ge(turned, it * BODY)
                            act.activation(ROW[:, s, :], PR[0:2, s % 2, :], ACT.Copy).then_inc(row_ready, 1)

                @block.tensor
                def _(pe):
                    pe.wait_ge(cond_ready, 1)

                    def turn(it, s):
                        pe.wait_ge(row_ready, it * BODY + (s + 1))
                        for c in range(CH // P):
                            mm = pe.matmul(PM[:, bass.ds(it * (BODY * PER) + (s * PER + c * 2), 2)],
                                           ROW[:, s, c * P:(c + 1) * P], CST[0:2, C_IDENT:C_IDENT + 2], start=True, stop=True)
                        mm.then_inc(turned, 1)

                    with pe.Fori(0, NCH // BODY) as it:
                        for s in range(BODY):
                            pe.wait_ge(w_in[s % SLOTS], it * (16 * BODY // SLOTS) + 16 * (s // SLOTS + 1))
                            for k in range(KB):
                                mm = pe.matmul(PR[0:2, s % 2, :], CT[:, k, :], W[:, s % SLOTS, k, :],
                                               start=(k == 0), stop=(k == KB - 1))
                            mm.then_inc(w_used, 1)
                            if s:
                                turn(it, s - 1)
                        turn(it, BODY - 1)

                @block.vector
                def _(dve):
                    v = Steps(dve, v_step)
                    dve.wait_ge(e_done, 1)
                    v.seq(dve.tensor_scalar_add(E[:, :, :], E[:, :, :], 1.0))
                    v.seq(dve.reciprocal(E[:, :, :], E[:, :, :]))
                    dve.tensor_tensor(CT[:, :, :], CT[:, :, :], E[:, :, :], ALU.mult).then_inc(cond_ready, 1)
                    dve.wait_ge(turned, NCH)
                    v.seq(dve.tensor_tensor(MOD[:, :, :, :].rearrange("p l c j -> p (l c) j"),
                                            PM[:, :].rearrange("p (c j) -> p c j", j=2),
                                            B[:, :].unsqueeze(2).broadcast_to([P, DEPTH * N_MOD * KB, 2]), ALU.add))
                    for part in (1, 4):
                        for l in range(DEPTH):
                            m = MOD[:, l, part * KB:(part + 1) * KB, :]
                            v.mark(dve.tensor_scalar_add(m, m, 1.0))
                    v.wait()

        def transpose_modulate(HT, l, first, split=None):
            with ExitStack() as st:
                PT = ps(st, "xt_ps", [P, 4, CH])
                PG = ps(st, "gate_ps", [P, 2, 2, CH])
                COLS = sb(st, "gate_cols", [P, KB, 2, P])
                turned, act_took, dve_took, gate_done, cols, gate_took = (
                    sem(st, n) for n in ("turned", "act_took", "dve_took", "gate_done", "gate_cols_ready", "gate_took"))
                lo_done = sem(st, "lo_done")
                block = st.enter_context(nc.Block())

                def mod(part, kb, cond):
                    return MOD[:, l, part * KB + kb, cond:cond + 1]

                @block.tensor
                def _(pe):
                    for kb in range(KB):
                        if kb >= 4:
                            pe.wait_ge(act_took if kb % 2 == 0 else dve_took, kb // 2 - 1)
                        for t in range(TT):
                            mm = pe.transpose(PT[:, kb % 4, t * P:(t + 1) * P], X[:, t, kb * P:(kb + 1) * P], ident)
                        mm.then_inc(turned, 1)
                    pe.wait_ge(cols, 1)
                    for c in range(2):
                        for kb in range(KB):
                            mm = pe.matmul(PG[:, c, kb // 4, (kb % 4) * P:(kb % 4 + 1) * P], COLS[:, kb, c, :], ident,
                                           start=True, stop=True)
                    mm.then_inc(gate_done, 1)

                @block.gpsimd
                def _(pool):
                    m = MOD[:, l, (first + 2) * KB:(first + 3) * KB, :]
                    pool.tensor_copy(COLS[:, :, :, :], m.unsqueeze(3).broadcast_to([P, KB, 2, P])).then_inc(cols, 1)

                @block.scalar
                def _(act):
                    for kb in range(0, KB, 2):
                        act.wait_ge(turned, kb + 1)
                        act.activation(HT[:, kb, 0:P], PT[:, kb % 4, 0:P], ACT.Identity, scale=mod(first + 1, kb, 0),
                                       bias=mod(first, kb, 0))
                        act.activation(HT[:, kb, P:T], PT[:, kb % 4, P:T], ACT.Identity, scale=mod(first + 1, kb, 1),
                                       bias=mod(first, kb, 1)).then_inc(act_took, 1)
                    act.wait_ge(gate_done, 1)
                    for c in range(2):
                        act.activation(GATE[:, c, :], PG[:, c].rearrange("p a n -> p (a n)"), ACT.Copy).then_inc(gate_took, 1)

                @block.vector
                def _(dve):
                    for kb in range(1, KB, 2):
                        dve.wait_ge(turned, kb + 1)
                        dve.tensor_scalar(HT[:, kb, 0:P], PT[:, kb % 4, 0:P], mod(first + 1, kb, 0), mod(first, kb, 0),
                                          ALU.mult, ALU.add)
                        dve.tensor_scalar(HT[:, kb, P:T], PT[:, kb % 4, P:T], mod(first + 1, kb, 1), mod(first, kb, 1),
                                          ALU.mult, ALU.add).then_inc(dve_took, 1)
                    if split:
                        dve.wait_ge(dve_took, KB // 2)
                        dve.wait_ge(act_took, KB // 2)
                        dve.tensor_copy(split[0][:, :, :], HT[:, :, :]).then_inc(lo_done, 1)
                        dve.wait_ge(lo_done, 1)
                        dve.tensor_tensor(split[1][:, :, :], HT[:, :, :], split[0][:, :, :].bitcast(F32),
                                          ALU.subtract).then_inc(lo_done, 1)

        def spread(row, n):
            return row.broadcast_to([P, n])

        def even_project(HT, QKT, RV, RG, MVA, MO, LI, FF, RT):
            DT, QD, KD, CD = RT
            with ExitStack() as st:
                SLOTS, NCH = 4, 8
                W = sb(st, "even_w_ring", [P, SLOTS, KB, CH])
                GW = sb(st, "gate_w", [P, KB, P])
                GB = sb(st, "gate_b", [P, 1])
                LG = sb(st, "log_gamma", [P, 4, 2 * H])
                EX = sb(st, "decay_exp", [P, 2 * H, P])
                TMP = sb(st, "logit_tmp", [P, 2 * H])
                SG = sb(st, "sigmoid", [P, 2, CH])
                PJ = ps(st, "proj_ps", [P, 4, CH])
                PG = ps(st, "gates_ps", [P, CH])
                w_in = [sem(st, f"even_w_in{s}") for s in range(SLOTS)]
                gate_in, item_done, item_taken, zeroed, gates_done, logit_in, a_step, v_step, lg_ready, ex_done, sig_done, rg_in, ones_done = (
                    sem(st, n) for n in ("gate_in", "item_done", "item_taken", "zeroed", "gates_done",
                                         "logit_in", "a_step", "v_step", "lg_ready", "ex_done", "sig_done", "rg_in", "ones_done"))
                block = st.enter_context(nc.Block())

                @block.sync
                def _(sp):
                    for n in range(NCH):
                        if n >= SLOTS:
                            sp.wait_ge(item_done, 4 * (n - SLOTS + 1))
                        sp.dma_start(W[:, n % SLOTS], I["even_w"][n]).then_inc(w_in[n % SLOTS], 16)

                @block.gpsimd
                def _(pool):
                    pool.memset(GW[:, :, :], 0.0).then_inc(zeroed, 1)
                    pool.memset(GB[:, :], 0.0).then_inc(zeroed, 1)
                    pool.memset(MVA[:, :, :, P:P + 1], 1.0).then_inc(ones_done, 1)
                    pool.wait_ge(zeroed, 2)
                    for kind, at in enumerate((0, 64, 32, 96)):
                        pool.dma_start(GW[:, :, at:at + H], I["even_w_gate"][kind]).then_inc(gate_in, 16)
                        pool.dma_start(GB[at:at + H, :], I["even_b_gate"][kind]).then_inc(gate_in, 16)
                    pool.wait_ge(ones_done, 1)

                @block.tensor
                def _(pe):
                    for n in range(NCH):
                        pe.wait_ge(w_in[n % SLOTS], 16 * (n // SLOTS + 1))
                        for i in range(4 if n < 4 else TT):
                            item = 4 * n + i if n < 4 else 16 + TT * (n - 4) + i
                            if item >= 4:
                                pe.wait_ge(item_taken, item - 3)
                            for k in range(KB):
                                if n < 4:
                                    mm = pe.matmul(PJ[:, item % 4, 0:T], W[:, n % SLOTS, k, i * P:(i + 1) * P], HT[:, k, :],
                                                   start=(k == 0), stop=(k == KB - 1))
                                else:
                                    mm = pe.matmul(PJ[:, item % 4, :], HT[:, k, i * P:(i + 1) * P], W[:, n % SLOTS, k, :],
                                                   start=(k == 0), stop=(k == KB - 1))
                            mm.then_inc(item_done, 1)
                    pe.wait_ge(gate_in, 8 * 16)
                    for k in range(KB):
                        mm = pe.matmul(PG[:, 0:T], GW[:, k, :], HT[:, k, :], start=(k == 0), stop=(k == KB - 1))
                    mm.then_inc(gates_done, 1)

                @block.scalar
                def _(act):
                    a = Steps(act, a_step)
                    act.dma_start(LG[:, 0, :], spread(I["ret_logit"], 2 * H)).then_inc(logit_in, 16)
                    act.wait_ge(logit_in, 16)
                    a.seq(act.activation(TMP[:, :], LG[:, 0, :], ACT.Abs))
                    a.seq(act.activation(TMP[:, :], TMP[:, :], ACT.Exp, scale=-1.0))
                    a.seq(act.activation(TMP[:, :], TMP[:, :], ACT.Ln, bias=1.0))
                    act.wait_ge(lg_ready, 1)
                    act.wait_ge(v_step, 2)
                    for n in range(2 * H):
                        lg, nlg, lg128 = LG[:, 1, n:n + 1], LG[:, 2, n:n + 1], LG[:, 3, n:n + 1]
                        rel = CST[:, C_RELF:C_RELF + P] if n < H else CST[:, C_RELB:C_RELB + P]
                        act.activation(EX[:, n, :], rel, ACT.Exp, scale=lg)
                        act.activation(QD[:, n, :], iota, ACT.Exp, scale=lg if n < H else nlg, bias=lg if n < H else lg128)
                        act.activation(KD[:, n:n + 1], CST[:, C_IDX + (n < H):C_IDX + (n < H) + 1], ACT.Exp, scale=lg)
                    act.activation(CD[:, :], LG[:, 3, :], ACT.Exp).then_inc(ex_done, 1)
                    for item in range(28):
                        act.wait_ge(item_done, item + 1)
                        if item < 16:
                            act.activation(QKT[:, item, :], PJ[:, item % 4, 0:T], ACT.Copy,
                                           scale=P ** -0.5 if item // 4 % 2 else 1.0).then_inc(item_taken, 1)
                            continue
                        what, t = divmod(item - 16, TT)
                        src = PJ[:, item % 4, :]
                        if what == 0:
                            act.activation(RV[:, t, :, :].rearrange("p h e -> p (h e)"), src, ACT.Copy).then_inc(item_taken, 1)
                        elif what == 1:
                            act.activation(RG[:, t, :], src, ACT.Copy).then_inc(rg_in, 1)
                            if t >= 2:
                                act.wait_ge(sig_done, t - 1)
                            act.activation(SG[:, t % 2, :], src, ACT.Sigmoid).then_inc(item_taken, 1)
                        elif what == 2:
                            act.activation(MVA[:, t, :, 0:P], src.rearrange("p (h e) -> p h e", h=H), ACT.Copy).then_inc(item_taken, 1)
                        else:
                            act.activation(MO[:, t, :], src, ACT.Sigmoid).then_inc(item_taken, 1)
                    act.wait_ge(gates_done, 1)
                    a.mark(act.activation(LI[:, :], PG[0:64, 0:T], ACT.Identity, bias=GB[0:64, :]))
                    a.mark(act.activation(FF[:, :], PG[64:P, 0:T], ACT.Identity, bias=GB[64:P, :]))
                    a.wait()

                @block.vector
                def _(dve):
                    v = Steps(dve, v_step)
                    dve.wait_ge(a_step, 3)
                    v.seq(dve.scalar_tensor_tensor(LG[:, 1, :], LG[:, 0, :], 0.0, TMP[:, :], ALU.min, ALU.subtract))
                    v.mark(dve.tensor_scalar_mul(LG[:, 2, :], LG[:, 1, :], -1.0))
                    dve.tensor_scalar_mul(LG[:, 3, :], LG[:, 1, :], float(P)).then_inc(lg_ready, 1)
                    v.wait()
                    dve.wait_ge(ex_done, 1)
                    for n in range(2 * H):
                        keep = CST[:, C_KEEPF:C_KEEPF + P] if n < H else CST[:, C_KEEPB:C_KEEPB + P]
                        v.mark(dve.tensor_tensor(EX[:, n, :], EX[:, n, :], keep, ALU.mult))
                    v.wait()
                    v.seq(dve.tensor_tensor(DT[:, :, :], EX[:, 0:H, :], EX[:, H:2 * H, :], ALU.add))
                    for t in range(TT):
                        dve.wait_ge(rg_in, t + 1)
                        dve.wait_ge(item_taken, 20 + t)
                        dve.tensor_tensor(RG[:, t, :], RG[:, t, :], SG[:, t % 2, :], ALU.mult).then_inc(sig_done, 1)
                    dve.wait_ge(sig_done, TT)

        def retention(QKT, RV, MIX, RT):
            DT, QD, KD, CD = RT
            with ExitStack() as st:
                S0 = sb(st, "state0", [P, 2, H, P])
                SU = sb(st, "state1", [P, 2, H, P])
                NS = sb(st, "prompt_state", [P, 2, H, P])
                AT = sb(st, "att_t", [P, 2, TT, P])
                QF = sb(st, "q_decayed", [P, 2, 2, 2, P])
                KR = sb(st, "k_decayed", [P, 2, 4, P])
                PA = ps(st, "att_ps", [P, 2, CH])
                PK = ps(st, "k_rows_ps", [P, 2, CH])
                PS = ps(st, "state_ps", [P, 2, CH])
                PO = ps(st, "out_ps", [P, 2, CH])
                s_in, att_done, att_t, k_done, k_rows, st_done, st_taken, o_done, o_taken, q_dec, out_st = (
                    sem(st, n) for n in ("state_in", "att_done", "att_t_ready", "k_turned", "k_rows_ready", "state_done",
                                         "state_taken", "o_done", "o_taken", "q_decayed_ready", "state_out"))
                block = st.enter_context(nc.Block())
                KINDS = ((0, 0), (0, 1), (1, 0), (2, 1))

                @block.sync
                def _(sp):
                    sp.dma_start(S0[:, :, :, :], I["state_ret"]).then_inc(s_in, 16)
                    sp.wait_ge(st_taken, H)
                    sp.dma_start(O["new_ret"], NS[:, :, :, :]).then_inc(out_st, 16)
                    sp.wait_ge(out_st, 16)

                @block.tensor
                def _(pe):
                    def begin(h):
                        if h >= 2:
                            pe.wait_ge(att_t, h - 1)
                            pe.wait_ge(k_rows, h - 1)
                        for t in range(TT):
                            mm = pe.matmul(PA[:, h % 2, t * P:(t + 1) * P], QKT[:, H + h, t * P:(t + 1) * P],
                                           QKT[:, h, t * P:(t + 1) * P], start=True, stop=True)
                        mm.then_inc(att_done, 1)
                        for t in range(TT):
                            mm = pe.transpose(PK[:, h % 2, t * P:(t + 1) * P], QKT[:, H + h, t * P:(t + 1) * P], ident)
                        mm.then_inc(k_done, 1)

                    begin(0)
                    begin(1)
                    for h in range(H):
                        pe.wait_ge(k_rows, h + 1)
                        if h >= 2:
                            pe.wait_ge(st_taken, h - 1)
                            pe.wait_ge(o_taken, h - 1)
                        for n, (t, d) in enumerate(KINDS):
                            mm = pe.matmul(PS[:, h % 2, n * P:(n + 1) * P], KR[:, h % 2, n, :], RV[:, t, h, :], start=True, stop=True)
                        mm.then_inc(st_done, 1)
                        pe.wait_ge(att_t, h + 1)
                        pe.wait_ge(q_dec, h + 1)
                        pe.wait_ge(st_taken, h + 1)
                        for t in range(TT):
                            o = PO[:, h % 2, t * P:(t + 1) * P]
                            mm = pe.matmul(o, AT[:, h % 2, t, :], RV[:, t, h, :], start=True, stop=(t == 0))
                            if t:
                                fwd, bwd = (S0, SU) if t == 1 else (SU, S0)
                                pe.matmul(o, QF[:, h % 2, 0, t - 1, :], fwd[:, 0, h, :], start=False, stop=False)
                                mm = pe.matmul(o, QF[:, h % 2, 1, t - 1, :], bwd[:, 1, h, :], start=False, stop=True)
                        mm.then_inc(o_done, 1)
                        if h + 2 < H:
                            begin(h + 2)

                @block.scalar
                def _(act):
                    def rows(h):
                        act.wait_ge(k_done, h + 1)
                        if h >= 2:
                            act.wait_ge(st_done, h - 1)
                        for n, (t, d) in enumerate(KINDS):
                            ins = act.activation(KR[:, h % 2, n, :], PK[:, h % 2, t * P:(t + 1) * P], ACT.Copy,
                                                 scale=KD[:, d * H + h:d * H + h + 1])
                        ins.then_inc(k_rows, 1)

                    rows(0)
                    rows(1)
                    for h in range(H):
                        act.wait_ge(o_done, h + 1)
                        act.activation(MIX[:, :, h, :], PO[:, h % 2, 0:T].rearrange("p (t e) -> p t e", t=TT),
                                       ACT.Copy).then_inc(o_taken, 1)
                        if h + 2 < H:
                            rows(h + 2)
                    act.wait_ge(o_taken, H)

                @block.vector
                def _(dve):
                    def begin(h):
                        dve.wait_ge(att_done, h + 1)
                        if h >= 2:
                            dve.wait_ge(o_done, h - 1)
                        dve.tensor_tensor(AT[:, h % 2, :, :], PA[:, h % 2, 0:T].rearrange("p (t l) -> p t l", t=TT),
                                          DT[:, h:h + 1, :].broadcast_to([P, TT, P]), ALU.mult).then_inc(att_t, 1)
                        for d in range(2):
                            ins = dve.tensor_tensor(QF[:, h % 2, d, :, :], QKT[:, h, P:T].rearrange("p (t l) -> p t l", t=2),
                                                    QD[:, d * H + h:d * H + h + 1, :].broadcast_to([P, 2, P]), ALU.mult)
                        ins.then_inc(q_dec, 1)

                    begin(0)
                    begin(1)
                    dve.wait_ge(s_in, 16)
                    for h in range(H):
                        dve.wait_ge(st_done, h + 1)
                        dve.tensor_copy(NS[:, :, h, :], PS[:, h % 2, 0:2 * P].rearrange("p (d e) -> p d e", d=2))
                        for d in range(2):
                            ins = dve.scalar_tensor_tensor(SU[:, d, h, :], S0[:, d, h, :], CD[:, d * H + h:d * H + h + 1],
                                                           PS[:, h % 2, (2 + d) * P:(3 + d) * P], ALU.mult, ALU.add)
                        ins.then_inc(st_taken, 1)
                        if h + 2 < H:
                            begin(h + 2)
                    dve.wait_ge(st_taken, H)

        def norm_rows(dve, v, sqrt_in, sqrt_out, x_ready, f, t, LN, S, n):
            x = X[:, t, :]
            v.seq(dve.tensor_tensor(S[0][:, :], f, GATE[:, COND[t], :], ALU.mult))
            v.seq(dve.scalar_tensor_tensor(x, x, ALPHA, S[0][:, :], ALU.mult, ALU.add))
            for i in range(2):
                v.mark(dve.bn_stats(S[1][:, i, :], x[:, i * CH:(i + 1) * CH]))
            v.wait()
            v.seq(dve.bn_aggr(S[2][:, t, 0:2], S[1][:, :, :].rearrange("p a b -> p (a b)")))
            dve.tensor_scalar_add(S[2][:, t, 2:3], S[2][:, t, 1:2], LN_EPS).then_inc(sqrt_in, 1)
            dve.wait_ge(sqrt_out, n)
            v.seq(dve.reciprocal(S[2][:, t, 2:3], S[2][:, t, 2:3]))
            v.seq(dve.tensor_scalar(x, x, S[2][:, t, 0:1], S[2][:, t, 2:3], ALU.subtract, ALU.mult))
            v.seq(dve.tensor_tensor(x, x, LN[:, 0, :], ALU.mult))
            dve.tensor_tensor(x, x, LN[:, 1, :], ALU.add).then_inc(x_ready, 1)

        def norm_root(act, sqrt_in, sqrt_out, S, t, n):
            act.wait_ge(sqrt_in, n)
            act.activation(S[2][:, t, 2:3], S[2][:, t, 2:3], ACT.Sqrt).then_inc(sqrt_out, 1)

        def norm_tiles(st):
            return (sb(st, "ln_tmp", [P, D]), sb(st, "ln_stats", [P, 2, 6]), sb(st, "ln_moments", [P, TT, 3]))

        def out_project(MIX, MT, wout, l, RG=None):
            with ExitStack() as st:
                W = sb(st, "w_out", [P, 2, KB, CH])
                LN = sb(st, "ln_rows", [P, 2, D])
                S = norm_tiles(st)
                GN = sb(st, "gn_row", [P, 2 * HW]) if RG is not None else None
                HS = sb(st, "head_stats", [P, TT * 2 * H, 6])
                HM = sb(st, "head_moments", [P, TT * 2 * H, 2])
                HR = sb(st, "head_root", [P, TT * 2 * H])
                PF = ps(st, "f_ps", [P, TT, 2, CH])
                PT = ps(st, "mix_t_ps", [P, 2, CH])
                x_ready = sem(st, "x_ready")
                (w_in, row_in, v_step, root_in, root_out, hr_in, hr_out, mix_ready, turned, taken, f_done) = (
                    sem(st, n) for n in ("w_out_in", "rows_in", "v_step", "root_in", "root_out", "hr_in", "hr_out",
                                         "mix_ready", "turned", "taken", "f_done"))
                block = st.enter_context(nc.Block())

                @block.sync
                def _(sp):
                    for n in range(2):
                        sp.dma_start(W[:, n], wout[n]).then_inc(w_in, 16)
                    sp.dma_start(LN[:, 0, :], spread(I["ln_g"][l, 0:1, :], D)).then_inc(row_in, 16)
                    sp.dma_start(LN[:, 1, :], spread(I["ln_b"][l, 0:1, :], D)).then_inc(row_in, 16)

                @block.tensor
                def _(pe):
                    for t in range(TT):
                        if RG is not None:
                            pe.wait_ge(mix_ready, t + 1)
                        for half in range(2):
                            n = 2 * t + half
                            if n >= 2:
                                pe.wait_ge(taken, n - 1)
                            for k in range(4):
                                mm = pe.transpose(PT[:, n % 2, k * P:(k + 1) * P], MIX[:, t, 4 * half + k, :], ident)
                            mm.then_inc(turned, 1)
                        pe.wait_ge(taken, 2 * t + 2)
                        pe.wait_ge(w_in, 32)
                        for n in range(2):
                            for k in range(KB):
                                mm = pe.matmul(PF[:, t, n, :], MT[:, k, t * P:(t + 1) * P], W[:, n, k, :],
                                               start=(k == 0), stop=(k == KB - 1))
                        mm.then_inc(f_done, 1)

                @block.scalar
                def _(act):
                    if RG is not None:
                        act.dma_start(GN[:, :], spread(I["gn_g"], 2 * HW)).then_inc(row_in, 16)
                        for t in range(TT):
                            act.wait_ge(hr_in, t + 1)
                            r = HR[:, t * 2 * H:(t + 1) * 2 * H]
                            act.activation(r, r, ACT.Sqrt).then_inc(hr_out, 1)
                    for n in range(2 * TT):
                        t, half = divmod(n, 2)
                        act.wait_ge(turned, n + 1)
                        act.activation(MT[:, 4 * half:4 * half + 4, t * P:(t + 1) * P],
                                       PT[:, n % 2, :].rearrange("p (k l) -> p k l", k=4), ACT.Copy).then_inc(taken, 1)
                    for t in range(TT):
                        norm_root(act, root_in, root_out, S, t, t + 1)

                @block.vector
                def _(dve):
                    v = Steps(dve, v_step)
                    for t in range(TT if RG is not None else 0):
                        a, b = t * 2 * H, (t + 1) * 2 * H
                        for h in range(2 * H):
                            v.mark(dve.bn_stats(HS[:, a + h, :], MIX[:, t, h, :]))
                        v.wait()
                        for h in range(2 * H):
                            v.mark(dve.bn_aggr(HM[:, a + h, :], HS[:, a + h, :]))
                        v.wait()
                        dve.tensor_scalar_add(HR[:, a:b], HM[:, a:b, 1], LN_EPS).then_inc(hr_in, 1)
                        dve.wait_ge(hr_out, t + 1)
                        v.seq(dve.reciprocal(HR[:, a:b], HR[:, a:b]))
                        for h in range(2 * H):
                            m = MIX[:, t, h, :]
                            v.mark(dve.tensor_scalar(m, m, HM[:, a + h, 0:1], HR[:, a + h:a + h + 1], ALU.subtract, ALU.mult))
                        v.wait()
                        dve.wait_ge(row_in, 48)
                        m = MIX[:, t, :, :].rearrange("p h e -> p (h e)")
                        v.seq(dve.tensor_tensor(m, m, GN[:, :], ALU.mult))
                        dve.tensor_tensor(m[:, 0:HW], m[:, 0:HW], RG[:, t, :], ALU.mult).then_inc(mix_ready, 1)
                    dve.wait_ge(row_in, 32 if RG is None else 48)
                    for t in range(TT):
                        dve.wait_ge(f_done, t + 1)
                        norm_rows(dve, v, root_in, root_out, x_ready, PF[:, t].rearrange("p a n -> p (a n)"), t, LN, S, t + 1)
                    dve.wait_ge(x_ready, TT)

        def peer_select(l, HT, GI):
            with ExitStack() as st:
                NQ, NC = 2 * PH, 112
                W = sb(st, "peer_wq", [P, 4, KB, CH])
                KEY = sb(st, "keys_t", [P, 2, N_KEYS])
                QT = sb(st, "q_t", [P, 2, T])
                S = sb(st, "scores", [P, 2, TT, N_KEYS])
                V = sb(st, "key_top", [P, TT, NQ, TOPK])
                IX = sb(st, "key_at", [P, TT, NQ, TOPK], U32)
                IB = sb(st, "key_at_b", [P, NQ, TOPK], BF16)
                CA = sb(st, "cand", [P, PH, NC])
                CB = sb(st, "cand_rest", [P, PH, NC])
                TV = sb(st, "top_v", [P, PH, TOPK])
                TP = sb(st, "top_at", [P, PH, TOPK], U32)
                DI = sb(st, "digits", [P, 4, PH * TOPK], U32)
                HI = sb(st, "is_rest", [P, PH * TOPK])
                DF = sb(st, "digit_diff", [P, 2, PH * TOPK])
                AB = sb(st, "digit_b", [P, 2, PH * TOPK], BF16)
                IO = sb(st, "iota_b", [P, TOPK], BF16)
                EQ = sb(st, "is_digit", [P, PH * TOPK, TOPK], BF16)
                GS = sb(st, "picked", [P, 2, 3, PH * TOPK])
                SUM = sb(st, "gate_sum", [P, PH])
                PJ = ps(st, "q_ps", [P, 4, CH])
                PS = ps(st, "score_ps", [P, 2, CH])
                PT = ps(st, "pick_ps", [P, 2, CH])
                (w_in, key_in, q_done, q_taken, s_done, s_taken, v_step, e_in, e_out, picked, turned, gi_done) = (
                    sem(st, n) for n in ("w_in", "key_in", "q_done", "q_taken", "s_done", "s_taken", "v_step", "e_in", "e_out",
                                         "picked", "turned", "gi_done"))
                w_ins = [w_in] + [sem(st, f"w_in{n}") for n in range(1, 4)]
                block = st.enter_context(nc.Block())

                @block.sync
                def _(sp):
                    for n in range(4):
                        sp.dma_start(W[:, n], I["peer_w_q"][l, n]).then_inc(w_ins[n], 16)
                    sp.dma_start(KEY[:, :, :], I["peer_keys"][l]).then_inc(key_in, 16)

                @block.tensor
                def _(pe):
                    def scores(n):
                        pe.wait_ge(q_taken, n + 1)
                        if n >= 2:
                            pe.wait_ge(s_taken, n - 1)
                        for t in range(TT):
                            mm = pe.matmul(PS[:, n % 2, t * P:(t + 1) * P], QT[:, n % 2, t * P:(t + 1) * P], KEY[:, n % 2, :],
                                           start=True, stop=True)
                        mm.then_inc(s_done, 1)

                    for n in range(NQ):
                        if n % 4 == 0:
                            pe.wait_ge(w_ins[n // 4], 16)
                        if n >= 4:
                            pe.wait_ge(q_taken, n - 3)
                        for k in range(KB):
                            mm = pe.matmul(PJ[:, n % 4, 0:T], W[:, n // 4, k, (n % 4) * P:(n % 4 + 1) * P], HT[:, k, :],
                                           start=(k == 0), stop=(k == KB - 1))
                        mm.then_inc(q_done, 1)
                        if n == 0:
                            pe.wait_ge(key_in, 16)
                        else:
                            scores(n - 1)
                    scores(NQ - 1)
                    for t in range(TT):
                        pe.wait_ge(picked, t + 1)
                        if t >= 2:
                            pe.wait_ge(gi_done, t - 1)
                        for kind in range(3):
                            mm = pe.transpose(PT[:, t % 2, kind * P:(kind + 1) * P], GS[:, t % 2, kind, :], ident)
                        mm.then_inc(turned, 1)

                @block.scalar
                def _(act):
                    for n in range(NQ):
                        act.wait_ge(q_done, n + 1)
                        if n >= 2:
                            act.wait_ge(s_done, n - 1)
                        act.activation(QT[:, n % 2, :], PJ[:, n % 4, 0:T], ACT.Copy).then_inc(q_taken, 1)
                    for t in range(TT):
                        act.wait_ge(e_in, t + 1)
                        act.activation(TV[:, :, :], TV[:, :, :], ACT.Exp).then_inc(e_out, 1)
                        act.wait_ge(turned, t + 1)
                        act.activation(GI[:, :, t * P:(t + 1) * P], PT[:, t % 2, 0:3 * P].rearrange("p (k t) -> p k t", k=3),
                                       ACT.Copy).then_inc(gi_done, 1)
                    act.wait_ge(gi_done, TT)

                @block.vector
                def _(dve):
                    v = Steps(dve, v_step)
                    v.seq(dve.tensor_copy(IO[:, :], iota[:, 0:TOPK]))

                    def top16(many):
                        for x, rest, top, at in many:
                            v.mark(dve.max(top[:, 0:8], x))
                        v.wait()
                        for x, rest, top, at in many:
                            v.mark(dve.max_index(at[:, 0:8], top[:, 0:8], x))
                        for x, rest, top, at in many:
                            v.mark(dve.match_replace(rest, top[:, 0:8], x, NEG))
                        v.wait()
                        for x, rest, top, at in many:
                            v.mark(dve.max(top[:, 8:16], rest))
                        v.wait()
                        for x, rest, top, at in many:
                            v.mark(dve.max_index(at[:, 8:16], top[:, 8:16], rest))
                        v.wait()

                    for n in range(NQ):
                        dve.wait_ge(s_done, n + 1)
                        dve.tensor_copy(S[:, 0, :, :], PS[:, n % 2, 0:T].rearrange("p (t k) -> p t k", t=TT)).then_inc(s_taken, 1)
                        dve.wait_ge(s_taken, n + 1)
                        top16([(S[:, 0, t, :], S[:, 1, t, :], V[:, t, n, :], IX[:, t, n, :]) for t in range(TT)])
                    for t in range(TT):
                        v1, v2 = V[:, t, 0:NQ:2, :], V[:, t, 1:NQ:2, :]
                        v.mark(dve.tensor_copy(IB[:, :, :], IX[:, t, :, :]))
                        v.mark(dve.tensor_tensor(CA[:, :, 0:64].rearrange("p h (a b) -> p h a b", a=4),
                                                 v1[:, :, 0:4].unsqueeze(3).broadcast_to([P, PH, 4, 16]),
                                                 v2.unsqueeze(2).broadcast_to([P, PH, 4, 16]), ALU.add))
                        v.mark(dve.tensor_tensor(CA[:, :, 64:NC].rearrange("p h (a b) -> p h a b", a=12),
                                                 v1[:, :, 4:16].unsqueeze(3).broadcast_to([P, PH, 12, 4]),
                                                 v2[:, :, 0:4].unsqueeze(2).broadcast_to([P, PH, 12, 4]), ALU.add))
                        v.wait()
                        top16([(CA[:, h, :], CB[:, h, :], TV[:, h, :], TP[:, h, :]) for h in range(PH)])
                        g = GS[:, t % 2, 0, :].rearrange("p (h k) -> p h k", h=PH)
                        v.seq(dve.tensor_copy(SUM[:, :], TV[:, :, 0]))
                        dve.tensor_tensor(TV[:, :, :], TV[:, :, :], SUM[:, :].unsqueeze(2).broadcast_to([P, PH, TOPK]),
                                          ALU.subtract).then_inc(e_in, 1)
                        tp = TP[:, :, :].rearrange("p h k -> p (h k)")
                        v.mark(dve.tensor_single_scalar(DI[:, 0, :], tp, 4, ALU.logical_shift_right))
                        v.mark(dve.tensor_single_scalar(DI[:, 1, :], tp, 15, ALU.bitwise_and))
                        v.mark(dve.tensor_single_scalar(DI[:, 2, :], tp, 2, ALU.logical_shift_right))
                        v.mark(dve.tensor_single_scalar(DI[:, 3, :], tp, 3, ALU.bitwise_and))
                        v.mark(dve.tensor_scalar(HI[:, :], tp, 64.0, None, ALU.is_ge))
                        v.wait()
                        v.mark(dve.scalar_tensor_tensor(DF[:, 0, :], DI[:, 2, :], -12.0, DI[:, 0, :], ALU.add, ALU.subtract))
                        v.mark(dve.tensor_tensor(DF[:, 1, :], DI[:, 3, :], DI[:, 1, :], ALU.subtract))
                        v.wait()
                        v.seq(dve.tensor_tensor(DF[:, :, :], DF[:, :, :], HI[:, :].unsqueeze(1).broadcast_to([P, 2, PH * TOPK]), ALU.mult))
                        v.seq(dve.tensor_tensor(AB[:, :, :], DF[:, :, :], DI[:, 0:2, :], ALU.add))
                        if t >= 2:
                            dve.wait_ge(turned, t - 1)
                        for c in range(2):
                            v.seq(dve.tensor_tensor(EQ[:, :, :], AB[:, c, :].unsqueeze(2).broadcast_to([P, PH * TOPK, TOPK]),
                                                    IO[:, :].unsqueeze(1).broadcast_to([P, PH * TOPK, TOPK]), ALU.is_equal))
                            eq = EQ[:, :, :].rearrange("p (h k) a -> p h k a", h=PH)
                            v.seq(dve.tensor_tensor(eq, eq, IB[:, c:NQ:2, :].unsqueeze(2).broadcast_to([P, PH, TOPK, TOPK]), ALU.mult))
                            v.seq(dve.tensor_reduce(GS[:, t % 2, 1 + c, :], EQ[:, :, :], mybir.AxisListType.X, ALU.add))
                        dve.wait_ge(e_out, t + 1)
                        v.seq(dve.tensor_reduce(SUM[:, :], TV[:, :, :], mybir.AxisListType.X, ALU.add))
                        v.seq(dve.reciprocal(SUM[:, :], SUM[:, :]))
                        dve.tensor_tensor(g, TV[:, :, :], SUM[:, :].unsqueeze(2).broadcast_to([P, PH, TOPK]),
                                          ALU.mult).then_inc(picked, 1)
                        dve.wait_ge(picked, t + 1)

        def peer_gates(GI, WD):
            with ExitStack() as st:
                QUADS = 2 * TG // 4
                TURNS = T // (2 * TG)
                RB = 4
                LT = sb(st, "first_one_hot", [P, RB, 4, P])
                RT = sb(st, "second_gated", [P, RB, 4, P])
                WS = sb(st, "spread", [P, 2, P, TG])
                PW = ps(st, "spread_ps", [P, 4, CH])
                lr_ready, w_done, w_taken = (sem(st, n) for n in ("lr_ready", "w_done", "w_taken"))
                w_out = [sem(st, f"w_stored{n}") for n in range(2)]
                block = st.enter_context(nc.Block())

                @block.sync
                def _(sp):
                    with sp.Fori(0, TURNS) as it:
                        for g in range(2):
                            sp.wait_ge(w_taken, it * QUADS + (g + 1) * (QUADS // 2))
                            sp.dma_start(WD[:, bass.ds(it * 2 + g, 1)].rearrange("p a j t -> p (a j t)"),
                                         WS[:, g].rearrange("p j t -> p (j t)")).then_inc(w_out[g], 16)
                    for g in range(2):
                        sp.wait_ge(w_out[g], 16 * TURNS)

                @block.vector
                def _(dve):
                    def quad(it, q, n0):
                        if n0:
                            dve.wait_ge(w_done, it * QUADS + (q - RB + 1))
                        for k in range(4):
                            tok = it * (2 * TG) + (4 * q + k)
                            dve.tensor_scalar(LT[:, (q % RB), k, :], iota, GI[:, 1, bass.ds(tok, 1)], None, ALU.is_equal)
                            ins = dve.tensor_scalar(RT[:, (q % RB), k, :], iota, GI[:, 2, bass.ds(tok, 1)],
                                                    GI[:, 0, bass.ds(tok, 1)], ALU.is_equal, ALU.mult)
                        ins.then_inc(lr_ready, 1)

                    for q in range(QUADS):
                        quad(0, q, q >= RB)
                    with dve.Fori(1, TURNS) as it:
                        for q in range(QUADS):
                            quad(it, q, True)

                @block.tensor
                def _(pe):
                    def quad(it, q, bank_wait):
                        pe.wait_ge(lr_ready, it * QUADS + (q + 1))
                        if bank_wait:
                            pe.wait_ge(w_taken, it * QUADS + (q - 3))
                        for k in range(4):
                            mm = pe.matmul(PW[:, q % 4, k * P:(k + 1) * P], LT[:, q % RB, k, :], RT[:, q % RB, k, :],
                                           start=True, stop=True)
                        mm.then_inc(w_done, 1)

                    for q in range(QUADS):
                        quad(0, q, q >= 4)
                    with pe.Fori(1, TURNS) as it:
                        for q in range(QUADS):
                            quad(it, q, True)

                @block.scalar
                def _(act):
                    def quad(it, q, store_wait):
                        if store_wait and q % (QUADS // 2) == 0:
                            act.wait_ge(w_out[q // (QUADS // 2)], it * 16)
                        act.wait_ge(w_done, it * QUADS + (q + 1))
                        g, k = divmod(q, QUADS // 2)
                        act.activation(WS[:, g, :, 4 * k:4 * k + 4].rearrange("p j t -> p t j"),
                                       PW[:, q % 4, :].rearrange("p (t j) -> p t j", t=4), ACT.Copy).then_inc(w_taken, 1)

                    for q in range(QUADS):
                        quad(0, q, False)
                    with act.Fori(1, TURNS) as it:
                        for q in range(QUADS):
                            quad(it, q, True)

        def peer_experts(l, HH, HL, WD, out=None):
            with ExitStack() as st:
                NCHK, BODY = N_KEYS // JC, 2 * JC
                TURNS = N_KEYS // BODY
                U = sb(st, "u_ring", [P, 2, JC, KB * P])
                V = sb(st, "v_ring", [P, 2, JC, D])
                W = sb(st, "w_ring", [P, 2, T // TG, JC * TG])
                UH, UL = (sb(st, n, [P, 2, KB * P], F32R) for n in ("u_hi", "u_lo"))
                VH, VL = (sb(st, n, [P, 2, D], F32R) for n in ("v_hi", "v_lo"))
                G = sb(st, "gelu", [P, 2, T])
                A = sb(st, "act", [P, 2, T])
                AH, AL = (sb(st, n, [P, 2, T], F32R) for n in ("act_hi", "act_lo"))
                LN = sb(st, "ln_rows", [P, 2, D])
                S = norm_tiles(st)
                PO = ps(st, "out_ps", [P, TT, 2, CH])
                PH_ = ps(st, "hidden_ps", [P, 2, CH])
                u_in, v_in, w_in = ([sem(st, f"{n}{s}") for s in range(2)] for n in ("u_in", "v_in", "w_in"))
                x_ready = sem(st, "x_ready")
                (row_in, v_step, uh, ul, vh, vl, h_done, g_done, a_done, o_done, root_in, root_out, x_out) = (
                    sem(st, n) for n in ("row_in", "v_step", "uh_ready", "ul_ready", "vh_ready", "vl_ready", "h_done", "g_done",
                                         "a_done", "o_done", "root_in", "root_out", "x_out"))
                block = st.enter_context(nc.Block())
                LAST = TURNS - 1

                def turns(eng, step):
                    for jj in range(BODY):
                        step(0, jj, True, False)
                    with eng.Fori(1, LAST) as it:
                        for jj in range(BODY):
                            step(it, jj, False, False)
                    for jj in range(BODY):
                        step(LAST, jj, False, True)

                @block.sync
                def _(sp):
                    def load(it, s, wait):
                        if wait:
                            sp.wait_ge(ul, it * BODY + (JC * (s - 1)))
                        sp.dma_start(U[:, s].rearrange("p j n -> p (j n)"), I["peer_u"][l, bass.ds(it * 2 + s, 1)].rearrange("c p j k i -> p (c j k i)")).then_inc(u_in[s], 16)
                        if wait:
                            sp.wait_ge(vl, it * BODY + (JC * (s - 1)))
                        sp.dma_start(V[:, s].rearrange("p j n -> p (j n)"), I["peer_v"][l, bass.ds(it * 2 + s, 1)].rearrange("c p j d -> p (c j d)")).then_inc(v_in[s], 16)
                        if wait:
                            sp.wait_ge(a_done, it * BODY + (JC * (s - 1)))
                        sp.dma_start(W[:, s], WD[:, :, bass.ds(it * BODY + JC * s, JC), :].rearrange("p g j t -> p g (j t)")).then_inc(w_in[s], 16)

                    load(0, 0, False)
                    load(0, 1, False)
                    with sp.Fori(1, TURNS) as it:
                        load(it, 0, True)
                        load(it, 1, True)
                    sp.dma_start(LN[:, 0, :], spread(I["ln_g"][l, 1:2, :], D)).then_inc(row_in, 16)
                    sp.dma_start(LN[:, 1, :], spread(I["ln_b"][l, 1:2, :], D)).then_inc(row_in, 16)
                    if out is not None:
                        for t in range(TT):
                            sp.wait_ge(x_ready, t + 1)
                            sp.dma_start(out[t], X[:, t, :]).then_inc(x_out, 16)
                        sp.wait_ge(x_out, 16 * TT)

                @block.tensor
                def _(pe):
                    def hidden(it, jj):
                        b = jj % 2
                        pe.wait_ge(uh, it * BODY + (jj + 1))
                        pe.wait_ge(ul, it * BODY + (jj + 1))
                        for k in range(KB):
                            for n, (u, x) in enumerate(((UH, HH), (UH, HL), (UL, HH))):
                                mm = pe.matmul(PH_[:, b, 0:T], u[:, b, k * P:(k + 1) * P], x[:, k, :],
                                               start=(k == 0 and n == 0), stop=(k == KB - 1 and n == 2))
                        mm.then_inc(h_done, 1)

                    def step(it, jj, first, last):
                        if not (last and jj == BODY - 1):
                            if not first or jj >= 1:
                                pe.wait_ge(g_done, it * BODY + jj)
                            hidden(it, jj + 1)
                        b = jj % 2
                        pe.wait_ge(a_done, it * BODY + (jj + 1))
                        pe.wait_ge(vl, it * BODY + (jj + 1))
                        for t in range(TT):
                            for c in range(2):
                                for n, (a, x) in enumerate(((AH, VH), (AH, VL), (AL, VH))):
                                    mm = pe.matmul(PO[:, t, c, :], a[:, b, t * P:(t + 1) * P], x[:, b, c * CH:(c + 1) * CH],
                                                   start=(first and jj == 0 and n == 0), stop=(last and jj == BODY - 1 and n == 2),
                                                   skip_group_check=True)
                        mm.then_inc(o_done, 1)

                    hidden(0, 0)
                    turns(pe, step)

                @block.scalar
                def _(act):
                    def u_part(it, jj):
                        s = jj // JC % 2
                        if jj % JC == 0:
                            act.wait_ge(u_in[s], it * 16 + 16 * (jj // BODY + 1))
                        act.activation(UH[:, jj % 2, :], U[:, s, jj % JC, :], ACT.Copy).then_inc(uh, 1)

                    def v_part(it, jj):
                        s = jj // JC % 2
                        if jj % JC == 0:
                            act.wait_ge(v_in[s], it * 16 + 16 * (jj // BODY + 1))
                        act.activation(VH[:, jj % 2, :], V[:, s, jj % JC, :], ACT.Copy).then_inc(vh, 1)

                    def step(it, jj, first, last):
                        act.wait_ge(h_done, it * BODY + (jj + 1))
                        if not first or jj >= 2:
                            act.wait_ge(a_done, it * BODY + (jj - 1))
                        act.activation(G[:, jj % 2, :], PH_[:, jj % 2, 0:T], ACT.Gelu_apprx_tanh).then_inc(g_done, 1)
                        if not last or jj + 2 < BODY:
                            u_part(it, jj + 2)
                        if not last or jj + 1 < BODY:
                            if not first or jj >= 1:
                                act.wait_ge(o_done, it * BODY + jj)
                            v_part(it, jj + 1)

                    u_part(0, 0)
                    u_part(0, 1)
                    v_part(0, 0)
                    turns(act, step)
                    for t in range(TT):
                        norm_root(act, root_in, root_out, S, t, t + 1)

                @block.vector
                def _(dve):
                    v = Steps(dve, v_step)

                    def u_part(it, jj):
                        dve.wait_ge(uh, it * BODY + (jj + 1))
                        dve.tensor_tensor(UL[:, jj % 2, :], U[:, jj // JC % 2, jj % JC, :], UH[:, jj % 2, :].bitcast(F32),
                                          ALU.subtract).then_inc(ul, 1)

                    def v_part(it, jj):
                        dve.wait_ge(vh, it * BODY + (jj + 1))
                        dve.tensor_tensor(VL[:, jj % 2, :], V[:, jj // JC % 2, jj % JC, :], VH[:, jj % 2, :].bitcast(F32),
                                          ALU.subtract).then_inc(vl, 1)

                    def step(it, jj, first, last):
                        b = jj % 2
                        dve.wait_ge(g_done, it * BODY + (jj + 1))
                        if jj % JC == 0:
                            dve.wait_ge(w_in[jj // JC], it * 16 + 16)
                        if not first or jj >= 2:
                            dve.wait_ge(o_done, it * BODY + (jj - 1))
                        dve.tensor_tensor(A[:, b, :].rearrange("p (g t) -> p g t", t=TG), G[:, b, :].rearrange("p (g t) -> p g t", t=TG),
                                          W[:, jj // JC, :, (jj % JC) * TG:(jj % JC + 1) * TG], ALU.mult).then_inc(v_step, 1)
                        dve.wait_ge(v_step, it * (2 * BODY) + (2 * jj + 1))
                        dve.tensor_copy(AH[:, b, :], A[:, b, :]).then_inc(v_step, 1)
                        dve.wait_ge(v_step, it * (2 * BODY) + (2 * jj + 2))
                        dve.tensor_tensor(AL[:, b, :], A[:, b, :], AH[:, b, :].bitcast(F32), ALU.subtract).then_inc(a_done, 1)
                        if not last or jj + 2 < BODY:
                            u_part(it, jj + 2)
                        if not last or jj + 1 < BODY:
                            v_part(it, jj + 1)

                    u_part(0, 0)
                    u_part(0, 1)
                    v_part(0, 0)
                    turns(dve, step)
                    v.n = 2 * N_KEYS
                    dve.wait_ge(row_in, 32)
                    dve.wait_ge(o_done, N_KEYS)
                    for t in range(TT):
                        norm_rows(dve, v, root_in, root_out, x_ready, PO[:, t].rearrange("p a n -> p (a n)"), t, LN, S, t + 1)
                    dve.wait_ge(x_ready, TT)

        def peer(l, out=None):
            with ExitStack() as st:
                HH = sb(st, "h_hi", [P, KB, T], F32R)
                HL = sb(st, "h_lo", [P, KB, T], F32R)
                GI = sb(st, "picks", [P, 3, T])
                with ExitStack() as inner:
                    HT = sb(inner, "HT", [P, KB, T])
                    transpose_modulate(HT, l, 3, (HH, HL))
                    peer_select(l, HT, GI)
                peer_gates(GI, WD)
                peer_experts(l, HH, HL, WD, out)

        def odd_project(HT, Z, GS):
            with ExitStack() as st:
                NW, NCH = 384, 6
                NN = GQ_HEADS + KV_HEADS
                W = sb(st, "odd_w", [P, NCH, KB, NW])
                QG = sb(st, "qk_gain", [P, 2 * HD])
                SQ = sb(st, "squares", [P, NN, HD])
                MS = sb(st, "mean_square", [P, TT, NN])
                RO = sb(st, "rotated", [P, 4, ROPE_HEADS, 32])
                PJ = ps(st, "proj_ps", [P, 4, CH])
                w_in = [sem(st, f"odd_w_in{n}") for n in range(NCH)]
                g_in, done, taken, v_step, root_in, root_out, rows_ready, out_st = (
                    sem(st, n) for n in ("gain_in", "proj_done", "proj_taken", "v_step", "root_in", "root_out", "rows_ready", "rows_out"))
                block = st.enter_context(nc.Block())
                ORDER = (0, 1, 2)

                @block.sync
                def _(sp):
                    for n in range(NCH):
                        sp.dma_start(W[:, n], I["odd_w"][n]).then_inc(w_in[n], 16)
                    sp.wait_ge(rows_ready, 1)
                    sp.dma_start(O["new_gk"], Z[:, 0, 512:640]).then_inc(out_st, 16)
                    sp.dma_start(O["new_dk"], Z[:, 0, 1152:1664]).then_inc(out_st, 16)
                    sp.dma_start(O["new_gv"], Z[:, 0, 1664:1792]).then_inc(out_st, 16)
                    sp.dma_start(O["new_dv"], Z[:, 0, 1792:2304]).then_inc(out_st, 16)
                    sp.wait_ge(out_st, 64)

                @block.tensor
                def _(pe):
                    for i, t in enumerate(ORDER):
                        for n in range(NCH):
                            item = i * NCH + n
                            pe.wait_ge(w_in[n], 16)
                            if item >= 4:
                                pe.wait_ge(taken, item - 3)
                            for k in range(KB):
                                mm = pe.matmul(PJ[:, item % 4, 0:NW], HT[:, k, t * P:(t + 1) * P], W[:, n, k, :],
                                               start=(k == 0), stop=(k == KB - 1))
                            mm.then_inc(done, 1)

                @block.scalar
                def _(act):
                    act.dma_start(QG[:, :], spread(I["qk_norm_g"], 2 * HD)).then_inc(g_in, 16)
                    for i, t in enumerate(ORDER):
                        for n in range(NCH):
                            item = i * NCH + n
                            act.wait_ge(done, item + 1)
                            act.activation(Z[:, t, n * NW:(n + 1) * NW], PJ[:, item % 4, 0:NW], ACT.Copy).then_inc(taken, 1)
                        act.wait_ge(root_in, i + 1)
                        act.activation(MS[:, t, :], MS[:, t, :], ACT.Sqrt).then_inc(root_out, 1)

                @block.vector
                def _(dve):
                    v = Steps(dve, v_step)
                    dve.wait_ge(g_in, 16)
                    for i, t in enumerate(ORDER):
                        z = Z[:, t, 0:NN * HD].rearrange("p (h e) -> p h e", h=NN)
                        dve.wait_ge(taken, i * NCH + 2)
                        v.seq(dve.tensor_tensor(SQ[:, :, :], z, z, ALU.mult))
                        v.seq(dve.tensor_reduce(MS[:, t, :], SQ[:, :, :], AX, ALU.add))
                        dve.tensor_scalar(MS[:, t, :], MS[:, t, :], 1.0 / HD, RMS_EPS, ALU.mult, ALU.add).then_inc(root_in, 1)
                        dve.wait_ge(root_out, i + 1)
                        v.seq(dve.reciprocal(MS[:, t, :], MS[:, t, :]))
                        v.seq(dve.tensor_tensor(z, z, MS[:, t, :].unsqueeze(2).broadcast_to([P, NN, HD]), ALU.mult))
                        for a, b, g in ((0, GQ_HEADS, 0), (GQ_HEADS, NN, 1)):
                            v.mark(dve.tensor_tensor(z[:, a:b, :], z[:, a:b, :],
                                                     QG[:, g * HD:(g + 1) * HD].unsqueeze(1).broadcast_to([P, b - a, HD]), ALU.mult))
                        v.wait()
                        dve.wait_ge(taken, (i + 1) * NCH)
                        if t:
                            x = Z[:, t, 0:ROPE_HEADS * HD].rearrange("p (h a n f) -> p h a n f", h=ROPE_HEADS, a=2, n=2)
                            o = (t - 1) * 32
                            cos, sin = (CST[:, c + o:c + o + 32].rearrange("p (a f) -> p a f", a=2).unsqueeze(1)
                                        .broadcast_to([P, ROPE_HEADS, 2, 16]) for c in (C_COS, C_SIN))
                            r = [RO[:, k].rearrange("p h (a f) -> p h a f", a=2) for k in range(4)]
                            for k, (half, table) in enumerate(((0, cos), (1, sin), (0, sin), (1, cos))):
                                v.mark(dve.tensor_tensor(r[k], x[:, :, :, half, :], table, ALU.mult))
                            v.wait()
                            v.mark(dve.tensor_tensor(x[:, :, :, 0, :], r[0], r[1], ALU.subtract))
                            v.mark(dve.tensor_tensor(x[:, :, :, 1, :], r[2], r[3], ALU.add))
                            v.wait()
                        for g in range(2):
                            ins = dve.tensor_copy(GS[:, t, g * HD:(g + 1) * HD], Z[:, t, 512 + (1 - g) * HD:512 + (2 - g) * HD])
                            if g == 0:
                                v.mark(ins)
                        ins.then_inc(rows_ready, 1)
                        dve.wait_ge(rows_ready, i + 1)

        def attend(Z, GS, MIX):
            with ExitStack() as st:
                QT = sb(st, "q_t", [P, 8, T])
                KT = sb(st, "k_t", [P, 6, 4 * P])
                CK = sb(st, "ctx_k", [P, 6, P])
                CV = sb(st, "ctx_v", [P, 5 * P])
                E = sb(st, "exp_s", [P, 2, 2, 3 * P])
                ET = sb(st, "exp_t", [P, 2, 2, 3 * P])
                MX = sb(st, "row_max", [P, 2, 2])
                SU = sb(st, "row_sum", [P, 2, 2])
                TMP = sb(st, "diff_tmp", [P, 2, P])
                LB = sb(st, "lambda_rows", [P, 4 * HD])
                NL = sb(st, "minus_lambda", [P, 4])
                SG = sb(st, "subln_gain", [P, P])
                SQ = sb(st, "squares", [P, TT, H, P])
                MS = sb(st, "mean_square", [P, TT, H])
                PS = ps(st, "score_ps", [P, 2, 2, CH])
                PT = ps(st, "exp_t_ps", [P, 2, CH])
                PO = ps(st, "o_ps", [P, 2, CH])
                (c_in, l_in, v_step, turned, turn_taken, l_sum, l_exp, s_done, m_ready, e_done, t_done, t_taken, o_done, o_taken,
                 root_in, root_out, neg_l, swapped) = (
                    sem(st, n) for n in ("cache_in", "lambda_in", "v_step", "turned", "turn_taken", "l_sum", "l_exp", "s_done",
                                         "m_ready", "e_done", "t_done", "t_taken", "o_done", "o_taken", "root_in", "root_out", "neg_l", "swapped"))
                block = st.enter_context(nc.Block())
                UNITS = [(t, u) for t in (0, 1, 2) for u in range(8)]
                TURNS = ([(QT[:, b, :], [Z[:, t, b * P:(b + 1) * P] for t in range(TT)]) for b in range(4)]
                         + [(QT[:, 4 + b, :], [Z[:, t, 640 + b * P:640 + (b + 1) * P] for t in range(TT)]) for b in range(4)]
                         + [(KT[:, 0, :], [Z[:, t, 512:640] for t in range(TT)] + [CK[:, 0, :]])]
                         + [(KT[:, 1, :], [GS[:, t, :] for t in range(TT)] + [CK[:, 1, :]])]
                         + [(KT[:, 2 + b, :], [Z[:, t, 1152 + b * P:1152 + (b + 1) * P] for t in range(TT)] + [CK[:, 2 + b, :]])
                            for b in range(4)])

                def banks(n):
                    return PS[:, n // 2 % 2, n % 2, :]

                @block.sync
                def _(sp):
                    sp.dma_start(CK[:, 0, :], I["cache_gk"]).then_inc(c_in, 16)
                    for g in range(2):
                        sp.dma_start(CK[:, 1, g * HD:(g + 1) * HD], I["cache_gk"][:, (1 - g) * HD:(2 - g) * HD]).then_inc(c_in, 16)
                    sp.dma_start(CK[:, 2:6, :].rearrange("p b n -> p (b n)"), I["cache_dk"]).then_inc(c_in, 16)
                    sp.dma_start(CV[:, 0:P], I["cache_gv"]).then_inc(c_in, 16)
                    sp.dma_start(CV[:, P:5 * P], I["cache_dv"]).then_inc(c_in, 16)
                    sp.dma_start(LB[:, :], spread(I["diff_lambda"], 4 * HD)).then_inc(l_in, 16)
                    sp.dma_start(SG[:, :], spread(I["diff_subln_g"], P)).then_inc(l_in, 16)

                @block.tensor
                def _(pe):
                    for n, (dst, src) in enumerate(TURNS):
                        if n >= 4:
                            pe.wait_ge(turn_taken, n - 3)
                        if n == 8:
                            pe.wait_ge(c_in, 96)
                        for k, x in enumerate(src):
                            mm = pe.transpose(banks(n)[:, k * P:(k + 1) * P], x, ident)
                        mm.then_inc(turned, 1)
                    pe.wait_ge(turn_taken, len(TURNS))

                    def scores(n):
                        t, u = UNITS[n]
                        a, b = (0, P) if t == 0 else (P, 4 * P)
                        if n >= 2:
                            pe.wait_ge(e_done, n - 1)
                        for c in range(2):
                            r = slice(c * HD, (c + 1) * HD)
                            kb = (0 if u // 2 == c else 1) if u < 4 else 2 + u - 4
                            mm = pe.matmul(PS[:, n % 2, c, 0:b - a], QT[r, u, t * P:(t + 1) * P], KT[r, kb, a:b], start=True, stop=True)
                        mm.then_inc(s_done, 1)

                    scores(0)
                    for n, (t, u) in enumerate(UNITS):
                        if n + 1 < len(UNITS):
                            scores(n + 1)
                        m = 1 if t == 0 else 3
                        pe.wait_ge(e_done, n + 1)
                        if n >= 1:
                            pe.wait_ge(t_taken, n)
                        for c in range(2):
                            for i in range(m):
                                mm = pe.transpose(PT[:, c, i * P:(i + 1) * P], E[:, n % 2, c, i * P:(i + 1) * P], ident)
                        mm.then_inc(t_done, 1)
                        pe.wait_ge(t_taken, n + 1)
                        if n >= 2:
                            pe.wait_ge(o_taken, n - 1)
                        for c in range(2):
                            w = HD if u < 4 else P
                            for i in range(m):
                                off = (u // 2) * HD if u < 4 else P + (u - 4) * P
                                src = Z[:, 0, 1664 + off:1664 + off + w] if t == 0 else (
                                    Z[:, 1 + i, 1664 + off:1664 + off + w] if i < 2 else CV[:, off:off + w])
                                mm = pe.matmul(PO[:, n % 2, c * P:c * P + w], ET[:, n % 2, c, i * P:(i + 1) * P], src,
                                               start=(i == 0), stop=(i == m - 1))
                        mm.then_inc(o_done, 1)

                @block.scalar
                def _(act):
                    for n, (dst, src) in enumerate(TURNS):
                        act.wait_ge(turned, n + 1)
                        act.activation(dst, banks(n)[:, 0:len(src) * P], ACT.Copy).then_inc(turn_taken, 1)
                    act.wait_ge(l_sum, 1)
                    act.activation(NL[:, 0:2], NL[:, 0:2], ACT.Exp).then_inc(l_exp, 1)

                    def exps(n):
                        t, u = UNITS[n]
                        m = P if t == 0 else 3 * P
                        act.wait_ge(m_ready, n + 1)
                        if n >= 2:
                            act.wait_ge(t_done, n - 1)
                            act.wait_ge(o_taken, n - 1)
                        for c in range(2):
                            ins = act.activation(E[:, n % 2, c, 0:m], PS[:, n % 2, c, 0:m], ACT.Exp, scale=HD ** -0.5,
                                                 bias=MX[:, n % 2, c:c + 1], accum_out=SU[:, n % 2, c:c + 1])
                        ins.then_inc(e_done, 1)

                    exps(0)
                    for n, (t, u) in enumerate(UNITS):
                        if n + 1 < len(UNITS):
                            exps(n + 1)
                        m = P if t == 0 else 3 * P
                        act.wait_ge(t_done, n + 1)
                        if n >= 2:
                            act.wait_ge(o_done, n - 1)
                        act.activation(ET[:, n % 2, :, 0:m], PT[:, :, 0:m], ACT.Copy).then_inc(t_taken, 1)
                    act.wait_ge(root_in, 1)
                    act.activation(MS[:, :, :], MS[:, :, :], ACT.Sqrt).then_inc(root_out, 1)

                @block.vector
                def _(dve):
                    v = Steps(dve, v_step)
                    dve.wait_ge(l_in, 32)
                    l = LB[:, :].rearrange("p (a b e) -> p a b e", a=2, b=2)
                    v.seq(dve.tensor_tensor(TMP[:, 0, :].rearrange("p (a e) -> p a e", a=2), l[:, :, 0, :], l[:, :, 1, :], ALU.mult))
                    dve.tensor_reduce(NL[:, 0:2], TMP[:, 0, :].rearrange("p (a e) -> p a e", a=2), AX, ALU.add).then_inc(l_sum, 1)
                    dve.wait_ge(l_exp, 1)
                    v.seq(dve.tensor_tensor(NL[:, 2:3], NL[:, 1:2], NL[:, 0:1], ALU.subtract))
                    v.seq(dve.tensor_scalar_add(NL[:, 2:3], NL[:, 2:3], -LAM_INIT))
                    dve.wait_ge(turn_taken, len(TURNS))

                    def maxes(n):
                        t, u = UNITS[n]
                        m = P if t == 0 else 3 * P
                        dve.wait_ge(s_done, n + 1)
                        if n >= 2:
                            dve.wait_ge(e_done, n - 1)
                        v.seq(dve.tensor_reduce(MX[:, n % 2, :], PS[:, n % 2, :, 0:m], AX, ALU.max))
                        dve.tensor_scalar_mul(MX[:, n % 2, :], MX[:, n % 2, :], -HD ** -0.5).then_inc(m_ready, 1)

                    maxes(0)
                    for n, (t, u) in enumerate(UNITS):
                        if n + 1 < len(UNITS):
                            maxes(n + 1)
                        b = n % 2
                        dve.wait_ge(e_done, n + 1)
                        v.seq(dve.reciprocal(SU[:, b, :], SU[:, b, :]))
                        if u >= 4:
                            v.seq(dve.tensor_tensor(SU[:, b, 1:2], SU[:, b, 1:2], NL[:, 2:3], ALU.mult))
                        dve.wait_ge(o_done, n + 1)
                        if u < 4:
                            v.mark(dve.tensor_scalar(MIX[:, t, u, 0:HD], PO[:, b, 0:HD], SU[:, b, 0:1], None, ALU.mult))
                            dve.tensor_scalar(MIX[:, t, u, HD:P], PO[:, b, P:P + HD], SU[:, b, 1:2], None, ALU.mult).then_inc(o_taken, 1)
                        else:
                            v.seq(dve.tensor_scalar(TMP[:, b, :], PO[:, b, P:2 * P], SU[:, b, 1:2], None, ALU.mult))
                            dve.scalar_tensor_tensor(MIX[:, t, u, :], PO[:, b, 0:P], SU[:, b, 0:1], TMP[:, b, :],
                                                     ALU.mult, ALU.add).then_inc(o_taken, 1)
                    dve.wait_ge(o_taken, len(UNITS))
                    for t in range(TT):
                        v.mark(dve.tensor_tensor(SQ[:, t], MIX[:, t, 4:8, :], MIX[:, t, 4:8, :], ALU.mult))
                    v.wait()
                    v.seq(dve.tensor_reduce(MS[:, :, :], SQ[:, :, :, :], AX, ALU.add))
                    dve.tensor_scalar(MS[:, :, :], MS[:, :, :], 1.0 / P, RMS_EPS, ALU.mult, ALU.add).then_inc(root_in, 1)
                    dve.wait_ge(root_out, 1)
                    v.seq(dve.reciprocal(MS[:, :, :], MS[:, :, :]))
                    v.seq(dve.tensor_scalar_mul(SG[:, :], SG[:, :], 1.0 - LAM_INIT))
                    for t in range(TT):
                        v.seq(dve.tensor_tensor(MIX[:, t, 4:8, :], MIX[:, t, 4:8, :], MS[:, t, :].unsqueeze(2).broadcast_to([P, H, P]), ALU.mult))
                        v.seq(dve.tensor_tensor(MIX[:, t, 4:8, :], MIX[:, t, 4:8, :], SG[:, :].unsqueeze(1).broadcast_to([P, H, P]), ALU.mult))

        def mlstm(QKT, MVA, MO, LI, FF, MIX):
            with ExitStack() as st:
                R = 64
                C0 = sb(st, "mstate0", [P, 2, H, P + 1])
                CU = sb(st, "mstate1", [P, 2, H, P + 1])
                NC = sb(st, "prompt_mstate", [P, 2, H, P + 1])
                LF, BB, CR, NM, EM = (sb(st, n, [R, T]) for n in ("log_f", "b_sum", "c_rows", "m_rows", "exp_m_rows"))
                MM = sb(st, "run_max", [R, T])
                ONE = sb(st, "ones", [R, P])
                SM = sb(st, "m_ends", [R, TT, 2])
                M0 = sb(st, "m0", [R, 1])
                COL = sb(st, "cols", [P, 2, TT, R])
                MC = sb(st, "m_cols", [P, 2 * H, TT, 2])
                WIN = sb(st, "w_in", [P, 4, H])
                WOLD = sb(st, "w_old", [P, 2, H])
                AM = sb(st, "att_masked", [P, 2, H, TT, P])
                EE = sb(st, "exp_w", [P, TT, 2, H, P])
                QS = sb(st, "q_scaled", [P, 2, 2, H, P])
                KW = sb(st, "k_weighed", [P, 2, 4, P])
                DEN = sb(st, "den", [P, 2, 2])
                HB = sb(st, "h_tmp", [P, 2, P])
                PB = ps(st, "m_ps", [P, 2, CH])
                PA = ps(st, "att_ps", [P, CH])
                PK = ps(st, "k_ps", [P, CH])
                PC = ps(st, "c_ps", [P, 2, CH])
                PN = ps(st, "num_ps", [P, 2, CH])
                (s_in, m_in, zeroed, a_step, v_step, absf, ln_done, c_ready, m_ready, em_ready, cols_done, small_done,
                 cols_ready, small_ready, mb_done, mb_taken, e_sub, e_exp, att_done, att_taken, kt_done, k_rows, win_sub, win_exp,
                 wt_ready, q_sub, q_exp, q_ready, cu_done, cu_taken, num_done, num_taken, out_st) = (
                    sem(st, n) for n in (
                        "state_in", "m_in", "zeroed", "a_step", "v_step", "absf", "ln_done", "c_ready", "m_ready", "em_ready",
                        "cols_done", "small_done", "cols_ready", "small_ready", "mb_done", "mb_taken", "e_sub", "e_exp",
                        "att_done", "att_taken", "kt_done", "k_rows", "win_sub", "win_exp", "wt_ready", "q_sub", "q_exp",
                        "q_ready", "cu_done", "cu_taken", "num_done", "num_taken", "out_st"))
                block = st.enter_context(nc.Block())
                KINDS = ((0, 0), (0, 1), (1, 0), (2, 1))
                UNITS = [(t, d) for t in range(TT) for d in range(2)]
                scale_in = [(t, d) for t, d in UNITS if t]

                @block.sync
                def _(sp):
                    sp.dma_start(C0[:, :, :, :], I["state_mlstm"]).then_inc(s_in, 16)
                    sp.wait_ge(zeroed, 1)
                    for d in range(2):
                        sp.dma_start(M0[32 * d:32 * d + H, :], I["state_m"][d]).then_inc(m_in, 16)
                    sp.wait_ge(m_ready, 1)
                    sp.dma_start(O["new_m"][0], NM[0:H, P - 1:P]).then_inc(out_st, 16)
                    sp.dma_start(O["new_m"][1], NM[32:32 + H, 0:1]).then_inc(out_st, 16)
                    sp.wait_ge(cu_taken, H)
                    sp.dma_start(O["new_mlstm"], NC[:, :, :, :]).then_inc(out_st, 16)
                    sp.wait_ge(out_st, 48)

                @block.gpsimd
                def _(pool):
                    pool.memset(M0[:, :], 0.0).then_inc(zeroed, 1)
                    pool.memset(ONE[:, :], 1.0).then_inc(zeroed, 1)
                    pool.memset(MM[:, :], 0.0).then_inc(zeroed, 1)
                    pool.memset(BB[:, :], 0.0).then_inc(zeroed, 1)
                    pool.memset(SM[:, :, :], 0.0).then_inc(zeroed, 1)

                @block.tensor
                def _(pe):
                    pe.wait_ge(m_ready, 1)
                    pe.wait_ge(em_ready, 1)
                    for n, src in enumerate((CR, EM)):
                        for t in range(TT):
                            mm = pe.transpose(PK[:, (n * TT + t) * R:(n * TT + t + 1) * R], src[:, t * P:(t + 1) * P],
                                              CST[0:R, C_IDENT:C_IDENT + R])
                    mm.then_inc(cols_done, 1)
                    for n in range(2 * H):
                        mm = pe.matmul(PA[:, n * 6:(n + 1) * 6], CST[0:R, C_SEL + n * P:C_SEL + (n + 1) * P],
                                       SM[:, :, :].rearrange("p t j -> p (t j)"), start=True, stop=True)
                    mm.then_inc(small_done, 1)
                    for u, (t, d) in enumerate(UNITS):
                        if u >= 2:
                            pe.wait_ge(mb_taken, u - 1)
                        for h in range(H):
                            n = d * H + h
                            mm = pe.matmul(PB[:, u % 2, h * P:(h + 1) * P], CST[0:R, C_SEL + n * P:C_SEL + (n + 1) * P],
                                           MM[:, t * P:(t + 1) * P], start=True, stop=True)
                        mm.then_inc(mb_done, 1)
                    pe.wait_ge(small_ready, 1)
                    for h in range(H):
                        if h:
                            pe.wait_ge(att_taken, h)
                        for t in range(TT):
                            mm = pe.matmul(PA[:, t * P:(t + 1) * P], QKT[:, 3 * H + h, t * P:(t + 1) * P],
                                           QKT[:, 2 * H + h, t * P:(t + 1) * P], start=True, stop=True)
                        mm.then_inc(att_done, 1)
                    pe.wait_ge(cols_ready, 1)
                    pe.wait_ge(s_in, 16)
                    for h in range(H):
                        if h:
                            pe.wait_ge(k_rows, h)
                            pe.wait_ge(cu_taken, h)
                        for t in range(TT):
                            mm = pe.transpose(PK[:, t * P:(t + 1) * P], QKT[:, 3 * H + h, t * P:(t + 1) * P], ident)
                        mm.then_inc(kt_done, 1)
                        pe.wait_ge(k_rows, h + 1)
                        for n, (t, d) in enumerate(KINDS):
                            mm = pe.matmul(PC[:, n // 2, n % 2 * (P + 1):(n % 2 + 1) * (P + 1)], KW[:, h % 2, n, :],
                                           MVA[:, t, h, :], start=True, stop=True)
                        mm.then_inc(cu_done, 1)
                    pe.wait_ge(cu_taken, H)
                    pe.wait_ge(wt_ready, 6)
                    pe.wait_ge(q_ready, 4)
                    for n in range(TT * H):
                        t, h = divmod(n, H)
                        if n >= 2:
                            pe.wait_ge(num_taken, n - 1)
                        for d in range(2):
                            o = PN[:, n % 2, d * 256:d * 256 + P + 1]
                            mm = pe.matmul(o, EE[:, t, d, h, :], MVA[:, t, h, :], start=True, stop=(t == 0))
                            if t:
                                c = C0 if (t == 1) == (d == 0) else CU
                                mm = pe.matmul(o, QS[:, t - 1, d, h, :], c[:, d, h, :], start=False, stop=True)
                        mm.then_inc(num_done, 1)

                @block.scalar
                def _(act):
                    a = Steps(act, a_step)
                    a.seq(act.activation(LF[:, :], FF[:, :], ACT.Abs))
                    a.seq(act.activation(LF[:, :], LF[:, :], ACT.Exp, scale=-1.0))
                    act.activation(LF[:, :], LF[:, :], ACT.Ln, bias=1.0).then_inc(ln_done, 1)
                    act.wait_ge(m_ready, 1)
                    act.activation(EM[:, :], NM[:, :], ACT.Exp, scale=-1.0).then_inc(em_ready, 1)
                    act.wait_ge(win_sub, 6)
                    a.mark(act.activation(WOLD[:, :, :], WOLD[:, :, :], ACT.Exp))
                    act.activation(WIN[:, :, :], WIN[:, :, :], ACT.Exp).then_inc(win_exp, 1)
                    a.wait()
                    u4 = 0
                    for u, (t, d) in enumerate(UNITS):
                        if t:
                            act.wait_ge(q_sub, u4 + 1)
                            q = QS[:, t - 1, d, :, :]
                            act.activation(q, q, ACT.Exp, scale=-1.0).then_inc(q_exp, 1)
                            u4 += 1
                        act.wait_ge(e_sub, u + 1)
                        e = EE[:, t, d, :, :]
                        act.activation(e, e, ACT.Exp, scale=-1.0).then_inc(e_exp, 1)
                    act.wait_ge(win_exp, 1)
                    for h in range(H):
                        act.wait_ge(kt_done, h + 1)
                        if h >= 2:
                            act.wait_ge(cu_done, h - 1)
                        for n, (t, d) in enumerate(KINDS):
                            ins = act.activation(KW[:, h % 2, n, :], PK[:, t * P:(t + 1) * P], ACT.Copy, scale=WIN[:, n, h:h + 1])
                        ins.then_inc(k_rows, 1)

                @block.vector
                def _(dve):
                    v = Steps(dve, v_step)
                    dve.wait_ge(ln_done, 1)
                    v.seq(dve.scalar_tensor_tensor(LF[:, :], FF[:, :], 0.0, LF[:, :], ALU.min, ALU.subtract))
                    dve.wait_ge(zeroed, 5)
                    dve.wait_ge(m_in, 32)

                    def rows(x, t, d):
                        a = x[32 * d:32 * d + H, t * P:(t + 1) * P]
                        return a[:, ::-1] if d else a

                    for t, d in UNITS:
                        v.mark(dve.tensor_tensor_scan(rows(BB, t, d), ONE[32 * d:32 * d + H, :], rows(LF, t, d), 0.0, ALU.mult, ALU.add))
                    v.wait()
                    v.seq(dve.tensor_tensor(CR[:, :], LI[:, :], BB[:, :], ALU.subtract))
                    for t, d in ((0, 0), (0, 1), (1, 0), (2, 1), (2, 0), (1, 1)):
                        r = slice(32 * d, 32 * d + H)
                        last = lambda x, t: x[r, t * P + (0 if d else P - 1):t * P + (1 if d else P)]
                        if t:
                            first = (t == 1) == (d == 0)
                            before = 3 - t
                            v.seq(dve.tensor_copy(SM[r, t, 1:2], M0[r, :]) if first else
                                  dve.tensor_tensor(SM[r, t, 1:2], last(BB, before), last(MM, before), ALU.add))
                        v.seq(dve.tensor_tensor_scan(rows(MM, t, d), rows(CR, t, d), rows(CR, t, d), SM[r, t, 1:2], ALU.max, ALU.max))
                        v.mark(dve.tensor_copy(SM[r, t, 0:1], last(MM, t)))
                    v.wait()
                    dve.tensor_tensor(NM[:, :], BB[:, :], MM[:, :], ALU.add).then_inc(m_ready, 1)
                    dve.wait_ge(cols_done, 1)
                    dve.tensor_copy(COL[:, :, :, :], PK[:, 0:6 * R].rearrange("p (n t r) -> p n t r", n=2, t=TT)).then_inc(cols_ready, 1)
                    dve.wait_ge(small_done, 1)
                    dve.tensor_copy(MC[:, :, :, :], PA[:, 0:48].rearrange("p (n t j) -> p n t j", n=2 * H, t=TT)).then_inc(small_ready, 1)
                    dve.wait_ge(cols_ready, 1)
                    dve.wait_ge(small_ready, 1)
                    for j, (t, d) in enumerate(KINDS[2:]):
                        m = MC[:, d * H:(d + 1) * H, t, :]
                        dve.tensor_tensor(WOLD[:, j, :], m[:, :, 1], m[:, :, 0], ALU.subtract).then_inc(win_sub, 1)
                    for n, (t, d) in enumerate(KINDS):
                        dve.tensor_tensor(WIN[:, n, :], COL[:, 0, t, 32 * d:32 * d + H], MC[:, d * H:(d + 1) * H, t, 0],
                                          ALU.subtract).then_inc(win_sub, 1)
                    for u, (t, d) in enumerate(UNITS):
                        dve.wait_ge(mb_done, u + 1)
                        mb = PB[:, u % 2, :].rearrange("p (h l) -> p h l", h=H)
                        if t:
                            dve.tensor_tensor(QS[:, t - 1, d, :, :], mb, MC[:, d * H:(d + 1) * H, t, 1:2].broadcast_to([P, H, P]),
                                              ALU.subtract).then_inc(q_sub, 1)
                        e = EE[:, t, d, :, :]
                        dve.tensor_tensor(e, mb, COL[:, 0, t, 32 * d:32 * d + H].unsqueeze(2).broadcast_to([P, H, P]),
                                          ALU.subtract).then_inc(mb_taken, 1)
                        dve.wait_ge(mb_taken, u + 1)
                        dve.tensor_scalar_max(e, e, 0.0).then_inc(e_sub, 1)
                    for h in range(H):
                        dve.wait_ge(att_done, h + 1)
                        for d in range(2):
                            keep = CST[:, (C_KEEPB if d else C_KEEPF):(C_KEEPB if d else C_KEEPF) + P]
                            ins = dve.tensor_tensor(AM[:, d, h, :, :], PA[:, 0:T].rearrange("p (t l) -> p t l", t=TT),
                                                    keep.unsqueeze(1).broadcast_to([P, TT, P]), ALU.mult)
                        ins.then_inc(att_taken, 1)
                    dve.wait_ge(att_taken, H)
                    for u, (t, d) in enumerate(UNITS):
                        dve.wait_ge(e_exp, u + 1)
                        e = EE[:, t, d, :, :]
                        dve.tensor_tensor(e, e, AM[:, d, :, t, :], ALU.mult).then_inc(wt_ready, 1)
                    for n, (t, d) in enumerate(scale_in):
                        dve.wait_ge(q_exp, n + 1)
                        q = QS[:, t - 1, d, :, :]
                        dve.tensor_tensor(q, q, QKT[:, 2 * H:3 * H, t * P:(t + 1) * P], ALU.mult).then_inc(q_ready, 1)
                    dve.wait_ge(win_exp, 1)
                    dve.wait_ge(a_step, 3)
                    dve.wait_ge(s_in, 16)
                    for h in range(H):
                        dve.wait_ge(cu_done, h + 1)
                        dve.tensor_copy(NC[:, :, h, :], PC[:, 0, 0:2 * (P + 1)].rearrange("p (d e) -> p d e", d=2))
                        for d in range(2):
                            ins = dve.scalar_tensor_tensor(CU[:, d, h, :], C0[:, d, h, :], WOLD[:, d, h:h + 1],
                                                           PC[:, 1, d * (P + 1):(d + 1) * (P + 1)], ALU.mult, ALU.add)
                        ins.then_inc(cu_taken, 1)
                    for n in range(TT * H):
                        t, h = divmod(n, H)
                        b = n % 2
                        dve.wait_ge(num_done, n + 1)
                        num = PN[:, b, :].rearrange("p (d e) -> p d e", d=2)
                        v.seq(dve.scalar_tensor_tensor(DEN[:, b, :], num[:, :, P], -1.0, COL[:, 1, t, h:h + 33:32], ALU.mult, ALU.max))
                        v.seq(dve.tensor_tensor(DEN[:, b, :], num[:, :, P], DEN[:, b, :], ALU.max))
                        v.seq(dve.reciprocal(DEN[:, b, :], DEN[:, b, :]))
                        v.seq(dve.tensor_scalar(HB[:, b, :], num[:, 0, 0:P], DEN[:, b, 0:1], None, ALU.mult))
                        dve.scalar_tensor_tensor(HB[:, b, :], num[:, 1, 0:P], DEN[:, b, 1:2], HB[:, b, :],
                                                 ALU.mult, ALU.add).then_inc(num_taken, 1)
                        dve.wait_ge(num_taken, n + 1)
                        v.mark(dve.tensor_tensor(MIX[:, t, H + h, :], HB[:, b, :], MO[:, t, h * P:(h + 1) * P], ALU.mult))
                    v.wait()

        modulation()
        with ExitStack() as ev:
            HT = sb(ev, "HT", [P, KB, T])
            transpose_modulate(HT, 0, 0)
            QKT = sb(ev, "qk_t", [P, 4 * H, T])
            RV = sb(ev, "ret_v", [P, TT, H, P])
            RG = sb(ev, "ret_gate", [P, TT, HW])
            MVA = sb(ev, "ml_v", [P, TT, H, P + 1])
            MO = sb(ev, "ml_gate", [P, TT, HW])
            LI = sb(ev, "log_i", [64, T])
            FF = sb(ev, "forget", [64, T])
            RT = (sb(ev, "ret_dt", [P, H, P]), sb(ev, "ret_qd", [P, 2 * H, P]), sb(ev, "ret_kd", [P, 2 * H]),
                  sb(ev, "ret_cd", [P, 2 * H]))
            even_project(HT, QKT, RV, RG, MVA, MO, LI, FF, RT)
            MIX = sb(ev, "mix", [P, TT, 2 * H, P])
            retention(QKT, RV, MIX, RT)
            mlstm(QKT, MVA, MO, LI, FF, MIX)
            out_project(MIX, HT, I["even_w_out"], 0, RG)
        peer(0)
        renew_semaphores()
        with ExitStack() as od:
            HT = sb(od, "HT", [P, KB, T])
            Z = sb(od, "odd_rows", [P, TT, 2304])
            GS = sb(od, "gk_swapped", [P, TT, P])
            MIX = sb(od, "mix", [P, TT, 2 * H, P])
            transpose_modulate(HT, 1, 0)
            odd_project(HT, Z, GS)
            attend(Z, GS, MIX)
            out_project(MIX, HT, I["odd_w_out"], 1)
        peer(1, O["y"])


def constants():
    c = np.zeros((P, C_ALL), np.float32)
    i = np.arange(P, dtype=np.float32)
    c[:, C_IDENT:C_IDENT + P] = np.eye(P)
    c[:, C_IOTA:C_IOTA + P] = i
    rel = i[None, :] - i[:, None]
    c[:, C_KEEPF:C_KEEPF + P] = rel >= 0
    c[:, C_KEEPB:C_KEEPB + P] = rel <= 0
    c[:, C_RELF:C_RELF + P] = np.maximum(rel, 0)
    c[:, C_RELB:C_RELB + P] = np.maximum(-rel, 0)
    c[:, C_IDX] = i
    c[:, C_IDX + 1] = P - 1 - i
    for n in range(8):
        c[32 * (n // H) + n % H, C_SEL + n * P:C_SEL + (n + 1) * P] = 1
    nf = HD // 4
    inv = (np.float32(10000.0) ** (-np.arange(nf, dtype=np.float32) / np.float32(nf))).astype(np.float32)
    pos = np.arange(2 * P)
    for t in range(2):
        at = pos[t * P:(t + 1) * P]
        for axis, where in enumerate((at // 64, at % 64)):
            ang = where.astype(np.float32)[:, None] * inv[None, :]
            o = t * 32 + axis * nf
            c[:, C_COS + o:C_COS + o + nf] = np.cos(ang)
            c[:, C_SIN + o:C_SIN + o + nf] = np.sin(ang)
    return c


def chunked(w, n=CH):
    k, cols = w.shape
    return np.ascontiguousarray(w.reshape(k // P, P, cols // n, n).transpose(2, 1, 0, 3))


def layout(**a):
    a = {k: np.asarray(v) for k, v in a.items()}
    w = a["even_w_in"][0]
    part = [w[:, n * HW:(n + 1) * HW] for n in range(8)]
    wo = a["odd_w_in"][0]
    gq, gk, gv, dq, dk, dv = np.split(wo, np.cumsum([512, 128, 128, 512, 512]), axis=1)
    cols = lambda v: np.ascontiguousarray(v.reshape(-1, P).T)
    d = {
        "x": np.concatenate([a["x_prompt"].reshape(1, P, D), a["x_sample"].reshape(2, P, D)]),
        "consts": constants(),
        "cond_t": np.ascontiguousarray(np.stack([cols(a["c_ctx"]), cols(a["c"][0])], axis=2)),
        "ada_w": np.concatenate([chunked(a["ada_w"][l]) for l in range(DEPTH)]),
        "ada_b_t": cols(a["ada_b"].reshape(-1)),
        "ln_g": a["ln_g"], "ln_b": a["ln_b"],
        "even_w": chunked(np.concatenate([part[n] for n in (0, 1, 4, 5, 2, 3, 6, 7)], axis=1)),
        "even_w_gate": np.ascontiguousarray(w[:, 8 * HW:].reshape(KB, P, 4, H).transpose(2, 1, 0, 3)),
        "even_b_gate": a["even_b_gate"].reshape(4, H, 1),
        "ret_logit": a["ret_decay_logit"].reshape(1, 2 * H),
        "gn_g": np.concatenate([a["ret_gn_g"], a["ml_gn_g"]]).reshape(1, 2 * HW),
        "even_w_out": chunked(a["even_w_out"][0]),
        "state_ret": np.ascontiguousarray(a["state_ret"][0, 0].transpose(2, 0, 1, 3)),
        "state_mlstm": np.ascontiguousarray(np.concatenate(
            [a["state_mlstm_C"][0, 0], a["state_mlstm_n"][0, 0][..., None]], axis=-1).transpose(2, 0, 1, 3)),
        "state_m": a["state_mlstm_m"].reshape(2, H, 1),
        "odd_w": chunked(np.concatenate([gq, gk, dq, dk, gv, dv], axis=1), 384),
        "qk_norm_g": np.stack([a["q_norm_g"][0], a["k_norm_g"][0]]).reshape(1, 2 * HD),
        "diff_lambda": a["diff_lambda"].reshape(1, 4 * HD),
        "diff_subln_g": a["diff_subln_g"].reshape(1, P),
        "odd_w_out": chunked(a["odd_w_out"][0]),
        "cache_gk": a["cache_gqa_k"].reshape(P, P), "cache_gv": a["cache_gqa_v"].reshape(P, P),
        "cache_dk": a["cache_diff_k"].reshape(P, HW), "cache_dv": a["cache_diff_v"].reshape(P, HW),
        "peer_w_q": np.stack([chunked(a["peer_w_q"][l]) for l in range(DEPTH)]),
        "peer_keys": np.ascontiguousarray(a["peer_sub_keys"].transpose(0, 3, 1, 2)),
        "peer_u": np.ascontiguousarray(a["peer_u"].reshape(DEPTH, N_KEYS, N_KEYS // JC, JC, KB, P)
                                       .transpose(0, 2, 5, 3, 4, 1)),
        "peer_v": np.ascontiguousarray(a["peer_v"].reshape(DEPTH, N_KEYS, N_KEYS // JC, JC, D)
                                       .transpose(0, 2, 1, 3, 4)),
    }
    return {k: np.ascontiguousarray(v) for k, v in d.items()}


OUTS = {
    "y": (TT, P, D),
    "new_ret": (P, 2, H, P),
    "new_mlstm": (P, 2, H, P + 1),
    "new_m": (2, H, 1),
    "new_gk": (P, P), "new_gv": (P, P), "new_dk": (P, HW), "new_dv": (P, HW),
}


def kernel(**inputs):
    import concourse.bacc as bacc
    from concourse.bass_utils import run_bass_kernel_spmd

    nc = bacc.Bacc("TRN2", target_bir_lowering=False, num_devices=1)
    arrays = layout(**inputs)
    I = {n: nc.dram_tensor(f"in_{n}", v.shape, mybir.dt.from_np(v.dtype), kind="ExternalInput").ap()
         for n, v in arrays.items()}
    O = {n: nc.dram_tensor(f"out_{n}", s, F32, kind="ExternalOutput").ap() for n, s in OUTS.items()}
    build(nc, I, O)
    r = run_bass_kernel_spmd(nc, [{f"in_{n}": v for n, v in arrays.items()}], core_ids=[0]).results[0]
    got = {n: r[f"out_{n}"] for n in OUTS}
    state = lambda s: s.transpose(1, 2, 0, 3)[None, None]
    return (got["y"][0:1], got["y"][1:3].reshape(1, 2 * P, D), state(got["new_ret"]),
            state(got["new_mlstm"][..., :P]), state(got["new_mlstm"])[..., P], got["new_m"].reshape(1, 1, 2, H),
            got["new_gk"].reshape(1, 1, P, KV_HEADS, HD), got["new_gv"].reshape(1, 1, P, KV_HEADS, HD),
            got["new_dk"].reshape(1, 1, P, H, 2, HD), got["new_dv"].reshape(1, 1, P, H, P))
```

```python
from contextlib import ExitStack
import math

import numpy as np

import concourse.bass as bass
from concourse import mybir
from concourse.alu_op_type import AluOpType as ALU

F32 = mybir.dt.float32
F32R = mybir.dt.float32r
BF16 = mybir.dt.bfloat16
U32 = mybir.dt.uint32
ACT = mybir.ActivationFunctionType
AX = mybir.AxisListType.X

P = 128
D = 1024
KB = D // P
TT = 3
T = TT * P
DEPTH = 2
N_MOD = 6
H = 4
HW = H * P
GQ_HEADS, KV_HEADS, HD = 8, 2, 64
ROPE_HEADS = 26
PH = 8
TOPK = 16
N_KEYS = 128
CH = 512
JC = 4
ADA_CH = N_MOD * D // CH
ADA_COLS = CH // P * 2
TG = 32
ALPHA = (2 * DEPTH) ** 0.25
LN_EPS = 1e-5
RMS_EPS = 1e-6
NEG = -3.0e38
LAM_INIT = 0.8 - 0.6 * math.exp(-0.3)
COND = (0, 1, 1)

C_IDENT, C_IOTA, C_KEEPF, C_KEEPB, C_RELF, C_RELB = (P * n for n in range(6))
C_IDX = 6 * P
C_SEL = C_IDX + 2
C_COS = C_SEL + 8 * P
C_SIN = C_COS + 2 * 32
C_ALL = C_SIN + 2 * 32


class Steps:

    def __init__(self, eng, sem):
        self.eng, self.sem, self.n = eng, sem, 0

    def mark(self, ins):
        self.n += 1
        ins.then_inc(self.sem, 1)

    def wait(self):
        self.eng.wait_ge(self.sem, self.n)

    def seq(self, ins):
        self.mark(ins)
        self.wait()


def build(nc, I, O):
    top = ExitStack()
    names = {}
    taken_sems = []

    def renew_semaphores():
        nc.clear_and_free_semaphores(list(taken_sems))
        taken_sems.clear()
        nc.all_engine_barrier()

    def unique(name):
        names[name] = names.get(name, 0) + 1
        return f"{name}_{names[name]}"

    def sb(st, name, shape, dt=F32):
        return st.enter_context(nc.sbuf_tensor(unique(name), shape, dt))

    def ps(st, name, shape, dt=F32):
        return st.enter_context(nc.psum_tensor(unique(name), shape, dt))

    def sem(st, name):
        s = nc.alloc_semaphore(unique(name))
        taken_sems.append(s)
        return s

    with top:
        X = sb(top, "X", [P, TT, D])
        CST = sb(top, "CST", [P, C_ALL])
        MOD = sb(top, "MOD", [P, DEPTH, N_MOD * KB, 2])
        CT = sb(top, "cond_t", [P, KB, 2])
        B = sb(top, "ada_b_t", [P, DEPTH * N_MOD * KB])
        GATE = sb(top, "GATE", [P, 2, D])
        WD = nc.dram_tensor("spread_gates", [P, T // TG, N_KEYS, TG], F32).ap()
        ident = CST[:, C_IDENT:C_IDENT + P]
        iota = CST[:, C_IOTA:C_IOTA + P]

        def finish_modulation(dve, v, l, PM):
            v.seq(dve.tensor_tensor(MOD[:, l, :, :], PM[:, :].rearrange("p (c j) -> p c j", j=2),
                                    B[:, l * N_MOD * KB:(l + 1) * N_MOD * KB].unsqueeze(2).broadcast_to([P, N_MOD * KB, 2]), ALU.add))
            for part in (1, 4):
                m = MOD[:, l, part * KB:(part + 1) * KB, :]
                v.mark(dve.tensor_scalar_add(m, m, 1.0))
            v.wait()

        def modulation(l):
            with ExitStack() as st:
                SLOTS, BODY, NCH = 3, 6, ADA_CH
                W = sb(st, "ada_w_ring", [P, SLOTS, KB, CH])
                E = sb(st, "cond_e", [P, KB, 2])
                ROW = sb(st, "mod_rows", [2, BODY, CH])
                PR = ps(st, "mod_row_ps", [P, 2, CH])
                PM = ps(st, "mod_ps", [P, N_MOD * KB * 2])
                w_in = [sem(st, f"ada_w_in{s}") for s in range(SLOTS)]
                small_in, rest_in, w_used, e_done, v_step, cond_ready, row_ready, turned = (
                    sem(st, n) for n in ("small_in", "rest_in", "ada_w_used", "exp_done", "v_step", "cond_ready", "row_ready", "turned"))
                block = st.enter_context(nc.Block())

                @block.sync
                def _(sp):
                    sp.dma_start(CT[:, :, :], I["cond_t"]).then_inc(small_in, 16)
                    for s in range(SLOTS):
                        sp.dma_start(W[:, s], I["ada_w"][s]).then_inc(w_in[s], 16)
                    with sp.Fori(1, NCH // SLOTS) as it:
                        for s in range(SLOTS):
                            sp.wait_ge(w_used, it * SLOTS + (s + 1 - SLOTS))
                            sp.dma_start(W[:, s], I["ada_w"][bass.ds(it * SLOTS + s, 1)].rearrange("a p k n -> p (a k) n")).then_inc(w_in[s], 16)

                @block.scalar
                def _(act):
                    act.wait_ge(small_in, 16)
                    act.activation(E[:, :, :], CT[:, :, :], ACT.Exp, scale=-1.0).then_inc(e_done, 1)
                    act.dma_start(CST[:, :], I["consts"]).then_inc(rest_in, 16)
                    act.dma_start(B[:, :], I["ada_b_t"]).then_inc(rest_in, 16)
                    for t in range(TT):
                        act.dma_start(X[:, t, :], I["x"][t]).then_inc(rest_in, 16)
                    with act.Fori(0, NCH // BODY) as it:
                        for s in range(BODY):
                            act.wait_ge(w_used, it * BODY + (s + 1))
                            if s == 0:
                                act.wait_ge(turned, it * BODY)
                            act.activation(ROW[:, s, :], PR[0:2, s % 2, :], ACT.Copy).then_inc(row_ready, 1)

                @block.tensor
                def _(pe):
                    pe.wait_ge(cond_ready, 1)

                    def turn(it, s):
                        if s == 0:
                            pe.wait_ge(rest_in, 16 * (2 + TT))
                        pe.wait_ge(row_ready, it * BODY + (s + 1))
                        for c in range(CH // P):
                            mm = pe.matmul(PM[:, bass.ds(it * (BODY * ADA_COLS) + (s * ADA_COLS + c * 2), 2)],
                                           ROW[:, s, c * P:(c + 1) * P], CST[0:2, C_IDENT:C_IDENT + 2], start=True, stop=True)
                        mm.then_inc(turned, 1)

                    with pe.Fori(0, NCH // BODY) as it:
                        for s in range(BODY):
                            pe.wait_ge(w_in[s % SLOTS], it * (16 * BODY // SLOTS) + 16 * (s // SLOTS + 1))
                            for k in range(KB):
                                mm = pe.matmul(PR[0:2, s % 2, :], CT[:, k, :], W[:, s % SLOTS, k, :],
                                               start=(k == 0), stop=(k == KB - 1))
                            mm.then_inc(w_used, 1)
                            if s:
                                turn(it, s - 1)
                        turn(it, BODY - 1)

                @block.vector
                def _(dve):
                    v = Steps(dve, v_step)
                    dve.wait_ge(e_done, 1)
                    v.seq(dve.tensor_scalar_add(E[:, :, :], E[:, :, :], 1.0))
                    v.seq(dve.reciprocal(E[:, :, :], E[:, :, :]))
                    dve.tensor_tensor(CT[:, :, :], CT[:, :, :], E[:, :, :], ALU.mult).then_inc(cond_ready, 1)
                    dve.wait_ge(turned, NCH)
                    finish_modulation(dve, v, l, PM)

        def load_ahead(sp, loads):
            for to, source, landed in loads:
                sp.dma_start(to, source).then_inc(landed, 16)

        def transpose_modulate(HT, l, first, split=None, ahead=()):
            with ExitStack() as st:
                PT = ps(st, "xt_ps", [P, 4, CH])
                PG = ps(st, "gate_ps", [P, 2, 2, CH])
                COLS = sb(st, "gate_cols", [P, KB, 2, P])
                turned, act_took, dve_took, gate_done, cols, gate_took = (
                    sem(st, n) for n in ("turned", "act_took", "dve_took", "gate_done", "gate_cols_ready", "gate_took"))
                lo_done = sem(st, "lo_done")
                block = st.enter_context(nc.Block())

                def mod(part, kb, cond):
                    return MOD[:, l, part * KB + kb, cond:cond + 1]

                @block.sync
                def _(sp):
                    load_ahead(sp, ahead)

                @block.tensor
                def _(pe):
                    for kb in range(KB):
                        if kb >= 4:
                            pe.wait_ge(act_took if kb % 2 == 0 else dve_took, kb // 2 - 1)
                        for t in range(TT):
                            mm = pe.transpose(PT[:, kb % 4, t * P:(t + 1) * P], X[:, t, kb * P:(kb + 1) * P], ident)
                        mm.then_inc(turned, 1)
                    pe.wait_ge(cols, 1)
                    for c in range(2):
                        for kb in range(KB):
                            mm = pe.matmul(PG[:, c, kb // 4, (kb % 4) * P:(kb % 4 + 1) * P], COLS[:, kb, c, :], ident,
                                           start=True, stop=True)
                    mm.then_inc(gate_done, 1)

                @block.gpsimd
                def _(pool):
                    m = MOD[:, l, (first + 2) * KB:(first + 3) * KB, :]
                    pool.tensor_copy(COLS[:, :, :, :], m.unsqueeze(3).broadcast_to([P, KB, 2, P])).then_inc(cols, 1)

                @block.scalar
                def _(act):
                    for kb in range(0, KB, 2):
                        act.wait_ge(turned, kb + 1)
                        act.activation(HT[:, kb, 0:P], PT[:, kb % 4, 0:P], ACT.Identity, scale=mod(first + 1, kb, 0),
                                       bias=mod(first, kb, 0))
                        act.activation(HT[:, kb, P:T], PT[:, kb % 4, P:T], ACT.Identity, scale=mod(first + 1, kb, 1),
                                       bias=mod(first, kb, 1)).then_inc(act_took, 1)
                    act.wait_ge(gate_done, 1)
                    for c in range(2):
                        act.activation(GATE[:, c, :], PG[:, c].rearrange("p a n -> p (a n)"), ACT.Copy).then_inc(gate_took, 1)

                @block.vector
                def _(dve):
                    for kb in range(1, KB, 2):
                        dve.wait_ge(turned, kb + 1)
                        dve.tensor_scalar(HT[:, kb, 0:P], PT[:, kb % 4, 0:P], mod(first + 1, kb, 0), mod(first, kb, 0),
                                          ALU.mult, ALU.add)
                        dve.tensor_scalar(HT[:, kb, P:T], PT[:, kb % 4, P:T], mod(first + 1, kb, 1), mod(first, kb, 1),
                                          ALU.mult, ALU.add).then_inc(dve_took, 1)
                    if split:
                        dve.wait_ge(dve_took, KB // 2)
                        dve.wait_ge(act_took, KB // 2)
                        dve.tensor_copy(split[0][:, :, :], HT[:, :, :]).then_inc(lo_done, 1)
                        dve.wait_ge(lo_done, 1)
                        dve.tensor_tensor(split[1][:, :, :], HT[:, :, :], split[0][:, :, :].bitcast(F32),
                                          ALU.subtract).then_inc(lo_done, 1)

        def spread(row, n):
            return row.broadcast_to([P, n])

        def even_project(HT, W, w_in, QKT, RV, RG, MVA, MO, LI, FF, RT):
            DT, QD, KD, CD = RT
            with ExitStack() as st:
                SLOTS, NCH = len(w_in), 8
                GW = sb(st, "gate_w", [P, KB, P])
                GB = sb(st, "gate_b", [P, 1])
                LG = sb(st, "log_gamma", [P, 4, 2 * H])
                EX = sb(st, "decay_exp", [P, 2 * H, P])
                TMP = sb(st, "logit_tmp", [P, 2 * H])
                SG = sb(st, "sigmoid", [P, 2, CH])
                PJ = ps(st, "proj_ps", [P, 4, CH])
                PG = ps(st, "gates_ps", [P, CH])
                gate_in, item_done, item_taken, zeroed, gates_done, logit_in, a_step, v_step, lg_ready, ex_done, sig_done, rg_in, ones_done = (
                    sem(st, n) for n in ("gate_in", "item_done", "item_taken", "zeroed", "gates_done",
                                         "logit_in", "a_step", "v_step", "lg_ready", "ex_done", "sig_done", "rg_in", "ones_done"))
                block = st.enter_context(nc.Block())

                @block.sync
                def _(sp):
                    for n in range(SLOTS, NCH):
                        sp.wait_ge(item_done, 4 * (n - SLOTS + 1))
                        sp.dma_start(W[:, n % SLOTS], I["even_w"][n]).then_inc(w_in[n % SLOTS], 16)

                @block.gpsimd
                def _(pool):
                    pool.memset(GW[:, :, :], 0.0).then_inc(zeroed, 1)
                    pool.memset(GB[:, :], 0.0).then_inc(zeroed, 1)
                    pool.memset(MVA[:, :, :, P:P + 1], 1.0).then_inc(ones_done, 1)
                    pool.wait_ge(zeroed, 2)
                    for kind, at in enumerate((0, 64, 32, 96)):
                        pool.dma_start(GW[:, :, at:at + H], I["even_w_gate"][kind]).then_inc(gate_in, 16)
                        pool.dma_start(GB[at:at + H, :], I["even_b_gate"][kind]).then_inc(gate_in, 16)
                    pool.wait_ge(ones_done, 1)

                @block.tensor
                def _(pe):
                    for n in range(NCH):
                        pe.wait_ge(w_in[n % SLOTS], 16 * (n // SLOTS + 1))
                        for i in range(4 if n < 4 else TT):
                            item = 4 * n + i if n < 4 else 16 + TT * (n - 4) + i
                            if item >= 4:
                                pe.wait_ge(item_taken, item - 3)
                            for k in range(KB):
                                if n < 4:
                                    mm = pe.matmul(PJ[:, item % 4, 0:T], W[:, n % SLOTS, k, i * P:(i + 1) * P], HT[:, k, :],
                                                   start=(k == 0), stop=(k == KB - 1))
                                else:
                                    mm = pe.matmul(PJ[:, item % 4, :], HT[:, k, i * P:(i + 1) * P], W[:, n % SLOTS, k, :],
                                                   start=(k == 0), stop=(k == KB - 1))
                            mm.then_inc(item_done, 1)
                    pe.wait_ge(gate_in, 8 * 16)
                    for k in range(KB):
                        mm = pe.matmul(PG[:, 0:T], GW[:, k, :], HT[:, k, :], start=(k == 0), stop=(k == KB - 1))
                    mm.then_inc(gates_done, 1)

                @block.scalar
                def _(act):
                    a = Steps(act, a_step)
                    act.dma_start(LG[:, 0, :], spread(I["ret_logit"], 2 * H)).then_inc(logit_in, 16)
                    act.wait_ge(logit_in, 16)
                    a.seq(act.activation(TMP[:, :], LG[:, 0, :], ACT.Abs))
                    a.seq(act.activation(TMP[:, :], TMP[:, :], ACT.Exp, scale=-1.0))
                    a.seq(act.activation(TMP[:, :], TMP[:, :], ACT.Ln, bias=1.0))
                    act.wait_ge(lg_ready, 1)
                    act.wait_ge(v_step, 2)
                    for n in range(2 * H):
                        lg, nlg, lg128 = LG[:, 1, n:n + 1], LG[:, 2, n:n + 1], LG[:, 3, n:n + 1]
                        rel = CST[:, C_RELF:C_RELF + P] if n < H else CST[:, C_RELB:C_RELB + P]
                        act.activation(EX[:, n, :], rel, ACT.Exp, scale=lg)
                        act.activation(QD[:, n, :], iota, ACT.Exp, scale=lg if n < H else nlg, bias=lg if n < H else lg128)
                        act.activation(KD[:, n:n + 1], CST[:, C_IDX + (n < H):C_IDX + (n < H) + 1], ACT.Exp, scale=lg)
                    act.activation(CD[:, :], LG[:, 3, :], ACT.Exp).then_inc(ex_done, 1)
                    for item in range(28):
                        act.wait_ge(item_done, item + 1)
                        if item < 16:
                            act.activation(QKT[:, item, :], PJ[:, item % 4, 0:T], ACT.Copy,
                                           scale=P ** -0.5 if item // 4 % 2 else 1.0).then_inc(item_taken, 1)
                            continue
                        what, t = divmod(item - 16, TT)
                        src = PJ[:, item % 4, :]
                        if what == 0:
                            act.activation(RV[:, t, :, :].rearrange("p h e -> p (h e)"), src, ACT.Copy).then_inc(item_taken, 1)
                        elif what == 1:
                            act.activation(RG[:, t, :], src, ACT.Copy).then_inc(rg_in, 1)
                            if t >= 2:
                                act.wait_ge(sig_done, t - 1)
                            act.activation(SG[:, t % 2, :], src, ACT.Sigmoid).then_inc(item_taken, 1)
                        elif what == 2:
                            act.activation(MVA[:, t, :, 0:P], src.rearrange("p (h e) -> p h e", h=H), ACT.Copy).then_inc(item_taken, 1)
                        else:
                            act.activation(MO[:, t, :], src, ACT.Sigmoid).then_inc(item_taken, 1)
                    act.wait_ge(gates_done, 1)
                    a.mark(act.activation(LI[:, :], PG[0:64, 0:T], ACT.Identity, bias=GB[0:64, :]))
                    a.mark(act.activation(FF[:, :], PG[64:P, 0:T], ACT.Identity, bias=GB[64:P, :]))
                    a.wait()

                @block.vector
                def _(dve):
                    v = Steps(dve, v_step)
                    dve.wait_ge(a_step, 3)
                    v.seq(dve.scalar_tensor_tensor(LG[:, 1, :], LG[:, 0, :], 0.0, TMP[:, :], ALU.min, ALU.subtract))
                    v.mark(dve.tensor_scalar_mul(LG[:, 2, :], LG[:, 1, :], -1.0))
                    dve.tensor_scalar_mul(LG[:, 3, :], LG[:, 1, :], float(P)).then_inc(lg_ready, 1)
                    v.wait()
                    dve.wait_ge(ex_done, 1)
                    for n in range(2 * H):
                        keep = CST[:, C_KEEPF:C_KEEPF + P] if n < H else CST[:, C_KEEPB:C_KEEPB + P]
                        v.mark(dve.tensor_tensor(EX[:, n, :], EX[:, n, :], keep, ALU.mult))
                    v.wait()
                    v.seq(dve.tensor_tensor(DT[:, :, :], EX[:, 0:H, :], EX[:, H:2 * H, :], ALU.add))
                    for t in range(TT):
                        dve.wait_ge(rg_in, t + 1)
                        dve.wait_ge(item_taken, 20 + t)
                        dve.tensor_tensor(RG[:, t, :], RG[:, t, :], SG[:, t % 2, :], ALU.mult).then_inc(sig_done, 1)
                    dve.wait_ge(sig_done, TT)

        def retention(QKT, RV, MIX, RT):
            DT, QD, KD, CD = RT
            with ExitStack() as st:
                S0 = sb(st, "state0", [P, 2, H, P])
                SU = sb(st, "state1", [P, 2, H, P])
                NS = sb(st, "prompt_state", [P, 2, H, P])
                AT = sb(st, "att_t", [P, 2, TT, P])
                QF = sb(st, "q_decayed", [P, 2, 2, 2, P])
                KR = sb(st, "k_decayed", [P, 2, 4, P])
                PA = ps(st, "att_ps", [P, 2, CH])
                PK = ps(st, "k_rows_ps", [P, 2, CH])
                PS = ps(st, "state_ps", [P, 2, CH])
                PO = ps(st, "out_ps", [P, 2, CH])
                s_in, att_done, att_t, k_done, k_rows, st_done, st_taken, o_done, o_taken, q_dec, out_st = (
                    sem(st, n) for n in ("state_in", "att_done", "att_t_ready", "k_turned", "k_rows_ready", "state_done",
                                         "state_taken", "o_done", "o_taken", "q_decayed_ready", "state_out"))
                block = st.enter_context(nc.Block())
                KINDS = ((0, 0), (0, 1), (1, 0), (2, 1))

                @block.sync
                def _(sp):
                    sp.dma_start(S0[:, :, :, :], I["state_ret"]).then_inc(s_in, 16)
                    sp.wait_ge(st_taken, H)
                    sp.dma_start(O["new_ret"], NS[:, :, :, :]).then_inc(out_st, 16)
                    sp.wait_ge(out_st, 16)

                @block.tensor
                def _(pe):
                    def begin(h):
                        if h >= 2:
                            pe.wait_ge(att_t, h - 1)
                            pe.wait_ge(k_rows, h - 1)
                        for t in range(TT):
                            mm = pe.matmul(PA[:, h % 2, t * P:(t + 1) * P], QKT[:, H + h, t * P:(t + 1) * P],
                                           QKT[:, h, t * P:(t + 1) * P], start=True, stop=True)
                        mm.then_inc(att_done, 1)
                        for t in range(TT):
                            mm = pe.transpose(PK[:, h % 2, t * P:(t + 1) * P], QKT[:, H + h, t * P:(t + 1) * P], ident)
                        mm.then_inc(k_done, 1)

                    begin(0)
                    begin(1)
                    for h in range(H):
                        pe.wait_ge(k_rows, h + 1)
                        if h >= 2:
                            pe.wait_ge(st_taken, h - 1)
                            pe.wait_ge(o_taken, h - 1)
                        for n, (t, d) in enumerate(KINDS):
                            mm = pe.matmul(PS[:, h % 2, n * P:(n + 1) * P], KR[:, h % 2, n, :], RV[:, t, h, :], start=True, stop=True)
                        mm.then_inc(st_done, 1)
                        pe.wait_ge(att_t, h + 1)
                        pe.wait_ge(q_dec, h + 1)
                        pe.wait_ge(st_taken, h + 1)
                        for t in range(TT):
                            o = PO[:, h % 2, t * P:(t + 1) * P]
                            mm = pe.matmul(o, AT[:, h % 2, t, :], RV[:, t, h, :], start=True, stop=(t == 0))
                            if t:
                                fwd, bwd = (S0, SU) if t == 1 else (SU, S0)
                                pe.matmul(o, QF[:, h % 2, 0, t - 1, :], fwd[:, 0, h, :], start=False, stop=False)
                                mm = pe.matmul(o, QF[:, h % 2, 1, t - 1, :], bwd[:, 1, h, :], start=False, stop=True)
                        mm.then_inc(o_done, 1)
                        if h + 2 < H:
                            begin(h + 2)

                @block.scalar
                def _(act):
                    def rows(h):
                        act.wait_ge(k_done, h + 1)
                        if h >= 2:
                            act.wait_ge(st_done, h - 1)
                        for n, (t, d) in enumerate(KINDS):
                            ins = act.activation(KR[:, h % 2, n, :], PK[:, h % 2, t * P:(t + 1) * P], ACT.Copy,
                                                 scale=KD[:, d * H + h:d * H + h + 1])
                        ins.then_inc(k_rows, 1)

                    rows(0)
                    rows(1)
                    for h in range(H):
                        act.wait_ge(o_done, h + 1)
                        act.activation(MIX[:, :, h, :], PO[:, h % 2, 0:T].rearrange("p (t e) -> p t e", t=TT),
                                       ACT.Copy).then_inc(o_taken, 1)
                        if h + 2 < H:
                            rows(h + 2)
                    act.wait_ge(o_taken, H)

                @block.vector
                def _(dve):
                    def begin(h):
                        dve.wait_ge(att_done, h + 1)
                        if h >= 2:
                            dve.wait_ge(o_done, h - 1)
                        dve.tensor_tensor(AT[:, h % 2, :, :], PA[:, h % 2, 0:T].rearrange("p (t l) -> p t l", t=TT),
                                          DT[:, h:h + 1, :].broadcast_to([P, TT, P]), ALU.mult).then_inc(att_t, 1)
                        for d in range(2):
                            ins = dve.tensor_tensor(QF[:, h % 2, d, :, :], QKT[:, h, P:T].rearrange("p (t l) -> p t l", t=2),
                                                    QD[:, d * H + h:d * H + h + 1, :].broadcast_to([P, 2, P]), ALU.mult)
                        ins.then_inc(q_dec, 1)

                    begin(0)
                    begin(1)
                    dve.wait_ge(s_in, 16)
                    for h in range(H):
                        dve.wait_ge(st_done, h + 1)
                        dve.tensor_copy(NS[:, :, h, :], PS[:, h % 2, 0:2 * P].rearrange("p (d e) -> p d e", d=2))
                        for d in range(2):
                            ins = dve.scalar_tensor_tensor(SU[:, d, h, :], S0[:, d, h, :], CD[:, d * H + h:d * H + h + 1],
                                                           PS[:, h % 2, (2 + d) * P:(3 + d) * P], ALU.mult, ALU.add)
                        ins.then_inc(st_taken, 1)
                        if h + 2 < H:
                            begin(h + 2)
                    dve.wait_ge(st_taken, H)

        def norm_rows(dve, v, sqrt_in, sqrt_out, x_ready, f, t, LN, S, n):
            x = X[:, t, :]
            v.seq(dve.tensor_tensor(S[0][:, :], f, GATE[:, COND[t], :], ALU.mult))
            v.seq(dve.scalar_tensor_tensor(x, x, ALPHA, S[0][:, :], ALU.mult, ALU.add))
            for i in range(2):
                v.mark(dve.bn_stats(S[1][:, i, :], x[:, i * CH:(i + 1) * CH]))
            v.wait()
            v.seq(dve.bn_aggr(S[2][:, t, 0:2], S[1][:, :, :].rearrange("p a b -> p (a b)")))
            dve.tensor_scalar_add(S[2][:, t, 2:3], S[2][:, t, 1:2], LN_EPS).then_inc(sqrt_in, 1)
            dve.wait_ge(sqrt_out, n)
            v.seq(dve.reciprocal(S[2][:, t, 2:3], S[2][:, t, 2:3]))
            v.seq(dve.tensor_scalar(x, x, S[2][:, t, 0:1], S[2][:, t, 2:3], ALU.subtract, ALU.mult))
            v.seq(dve.tensor_tensor(x, x, LN[:, 0, :], ALU.mult))
            dve.tensor_tensor(x, x, LN[:, 1, :], ALU.add).then_inc(x_ready, 1)

        def norm_root(act, sqrt_in, sqrt_out, S, t, n):
            act.wait_ge(sqrt_in, n)
            act.activation(S[2][:, t, 2:3], S[2][:, t, 2:3], ACT.Sqrt).then_inc(sqrt_out, 1)

        def norm_tiles(st):
            return (sb(st, "ln_tmp", [P, D]), sb(st, "ln_stats", [P, 2, 6]), sb(st, "ln_moments", [P, TT, 3]))

        def out_project(MIX, MT, W, w_in, l, RG=None):
            with ExitStack() as st:
                LN = sb(st, "ln_rows", [P, 2, D])
                S = norm_tiles(st)
                GN = sb(st, "gn_row", [P, 2 * HW]) if RG is not None else None
                HS = sb(st, "head_stats", [P, TT * 2 * H, 6])
                HM = sb(st, "head_moments", [P, TT * 2 * H, 2])
                HR = sb(st, "head_root", [P, TT * 2 * H])
                PF = ps(st, "f_ps", [P, TT, 2, CH])
                PT = ps(st, "mix_t_ps", [P, 2, CH])
                x_ready = sem(st, "x_ready")
                (row_in, v_step, root_in, root_out, hr_in, hr_out, mix_ready, turned, taken, f_done) = (
                    sem(st, n) for n in ("rows_in", "v_step", "root_in", "root_out", "hr_in", "hr_out",
                                         "mix_ready", "turned", "taken", "f_done"))
                block = st.enter_context(nc.Block())

                @block.sync
                def _(sp):
                    sp.dma_start(LN[:, 0, :], spread(I["ln_g"][l, 0:1, :], D)).then_inc(row_in, 16)
                    sp.dma_start(LN[:, 1, :], spread(I["ln_b"][l, 0:1, :], D)).then_inc(row_in, 16)

                @block.tensor
                def _(pe):
                    for t in range(TT):
                        if RG is not None:
                            pe.wait_ge(mix_ready, t + 1)
                        for half in range(2):
                            n = 2 * t + half
                            if n >= 2:
                                pe.wait_ge(taken, n - 1)
                            for k in range(4):
                                mm = pe.transpose(PT[:, n % 2, k * P:(k + 1) * P], MIX[:, t, 4 * half + k, :], ident)
                            mm.then_inc(turned, 1)
                        pe.wait_ge(taken, 2 * t + 2)
                        pe.wait_ge(w_in, 32)
                        for n in range(2):
                            for k in range(KB):
                                mm = pe.matmul(PF[:, t, n, :], MT[:, k, t * P:(t + 1) * P], W[:, n, k, :],
                                               start=(k == 0), stop=(k == KB - 1))
                        mm.then_inc(f_done, 1)

                @block.scalar
                def _(act):
                    if RG is not None:
                        act.dma_start(GN[:, :], spread(I["gn_g"], 2 * HW)).then_inc(row_in, 16)
                        for t in range(TT):
                            act.wait_ge(hr_in, t + 1)
                            r = HR[:, t * 2 * H:(t + 1) * 2 * H]
                            act.activation(r, r, ACT.Sqrt).then_inc(hr_out, 1)
                    for n in range(2 * TT):
                        t, half = divmod(n, 2)
                        act.wait_ge(turned, n + 1)
                        act.activation(MT[:, 4 * half:4 * half + 4, t * P:(t + 1) * P],
                                       PT[:, n % 2, :].rearrange("p (k l) -> p k l", k=4), ACT.Copy).then_inc(taken, 1)
                    for t in range(TT):
                        norm_root(act, root_in, root_out, S, t, t + 1)

                @block.vector
                def _(dve):
                    v = Steps(dve, v_step)
                    for t in range(TT if RG is not None else 0):
                        a, b = t * 2 * H, (t + 1) * 2 * H
                        for h in range(2 * H):
                            v.mark(dve.bn_stats(HS[:, a + h, :], MIX[:, t, h, :]))
                        v.wait()
                        for h in range(2 * H):
                            v.mark(dve.bn_aggr(HM[:, a + h, :], HS[:, a + h, :]))
                        v.wait()
                        dve.tensor_scalar_add(HR[:, a:b], HM[:, a:b, 1], LN_EPS).then_inc(hr_in, 1)
                        dve.wait_ge(hr_out, t + 1)
                        v.seq(dve.reciprocal(HR[:, a:b], HR[:, a:b]))
                        for h in range(2 * H):
                            m = MIX[:, t, h, :]
                            v.mark(dve.tensor_scalar(m, m, HM[:, a + h, 0:1], HR[:, a + h:a + h + 1], ALU.subtract, ALU.mult))
                        v.wait()
                        dve.wait_ge(row_in, 48)
                        m = MIX[:, t, :, :].rearrange("p h e -> p (h e)")
                        v.seq(dve.tensor_tensor(m, m, GN[:, :], ALU.mult))
                        dve.tensor_tensor(m[:, 0:HW], m[:, 0:HW], RG[:, t, :], ALU.mult).then_inc(mix_ready, 1)
                    dve.wait_ge(row_in, 32 if RG is None else 48)
                    for t in range(TT):
                        dve.wait_ge(f_done, t + 1)
                        norm_rows(dve, v, root_in, root_out, x_ready, PF[:, t].rearrange("p a n -> p (a n)"), t, LN, S, t + 1)
                    dve.wait_ge(x_ready, TT)

        def peer_select(HT, W, w_in, KEY, key_in, GI):
            with ExitStack() as st:
                NQ, NC = 2 * PH, 112
                QT = sb(st, "q_t", [P, 2, 4, P])
                S = sb(st, "scores", [P, 2, 4, N_KEYS])
                SR = sb(st, "scores_rest", [P, 4, N_KEYS])
                V = sb(st, "key_top", [P, TT, NQ, TOPK])
                IX = sb(st, "key_at", [P, TT, NQ, TOPK], U32)
                IB = sb(st, "key_at_b", [P, NQ, TOPK], BF16)
                CA = sb(st, "cand", [P, PH, NC])
                CB = sb(st, "cand_rest", [P, PH, NC])
                TV = sb(st, "top_v", [P, PH, TOPK])
                TP = sb(st, "top_at", [P, PH, TOPK], U32)
                DI = sb(st, "digits", [P, 4, PH * TOPK], U32)
                HI = sb(st, "is_rest", [P, PH * TOPK])
                DF = sb(st, "digit_diff", [P, 2, PH * TOPK])
                AB = sb(st, "digit_b", [P, 2, PH * TOPK], BF16)
                IO = sb(st, "iota_b", [P, TOPK], BF16)
                EQ = sb(st, "is_digit", [P, PH * TOPK, TOPK], BF16)
                GS = sb(st, "picked", [P, TT, 3, PH * TOPK])
                SUM = sb(st, "gate_sum", [P, PH])
                PJ = ps(st, "q_ps", [P, 2, CH])
                PS = ps(st, "score_ps", [P, 2, CH])
                PT = ps(st, "pick_ps", [P, 2, CH])
                (q_done, q_taken, s_done, s_taken, s_used, v_step, e_in, e_out, picked, turned, gi_done) = (
                    sem(st, n) for n in ("q_done", "q_taken", "s_done", "s_taken", "s_used", "v_step", "e_in", "e_out",
                                         "picked", "turned", "gi_done"))
                block = st.enter_context(nc.Block())

                NG = 4

                @block.tensor
                def _(pe):
                    def scores(g):
                        pe.wait_ge(q_taken, g + 1)
                        if g >= 2:
                            pe.wait_ge(s_taken, g - 1)
                        for i in range(4):
                            mm = pe.matmul(PS[:, g % 2, i * P:(i + 1) * P], QT[:, g % 2, i, :], KEY[:, i % 2, :], start=True, stop=True)
                        mm.then_inc(s_done, 1)

                    def picks(t):
                        pe.wait_ge(picked, t + 1)
                        if t >= 2:
                            pe.wait_ge(gi_done, t - 1)
                        for kind in range(3):
                            mm = pe.transpose(PT[:, t % 2, kind * P:(kind + 1) * P], GS[:, t, kind, :], ident)
                        mm.then_inc(turned, 1)

                    for g in range(TT * NG):
                        t, c = divmod(g, NG)
                        if t == 0:
                            pe.wait_ge(w_in[c], 16)
                        if g >= 2:
                            pe.wait_ge(q_taken, g - 1)
                        for i in range(4):
                            for k in range(KB):
                                mm = pe.matmul(PJ[:, g % 2, i * P:(i + 1) * P], W[:, c, k, i * P:(i + 1) * P],
                                               HT[:, k, t * P:(t + 1) * P], start=(k == 0), stop=(k == KB - 1))
                        mm.then_inc(q_done, 1)
                        if g == 0:
                            pe.wait_ge(key_in, 16)
                        else:
                            scores(g - 1)
                    scores(TT * NG - 1)
                    for t in range(TT):
                        picks(t)

                @block.scalar
                def _(act):
                    def scores(g):
                        act.wait_ge(s_done, g + 1)
                        if g >= 2:
                            act.wait_ge(s_used, g - 1)
                        act.activation(S[:, g % 2, :, :], PS[:, g % 2, :].rearrange("p (i k) -> p i k", i=4), ACT.Copy).then_inc(s_taken, 1)
                        if g % NG == NG - 1:
                            t = g // NG
                            act.wait_ge(e_in, t + 1)
                            act.activation(TV[:, :, :], TV[:, :, :], ACT.Exp).then_inc(e_out, 1)

                    for g in range(TT * NG):
                        act.wait_ge(q_done, g + 1)
                        if g >= 2:
                            act.wait_ge(s_done, g - 1)
                        act.activation(QT[:, g % 2, :, :], PJ[:, g % 2, :].rearrange("p (i l) -> p i l", i=4), ACT.Copy).then_inc(q_taken, 1)
                        if g:
                            scores(g - 1)
                    scores(TT * NG - 1)
                    for t in range(TT):
                        act.wait_ge(turned, t + 1)
                        act.activation(GI[:, :, t * P:(t + 1) * P], PT[:, t % 2, 0:3 * P].rearrange("p (k t) -> p k t", k=3),
                                       ACT.Copy).then_inc(gi_done, 1)
                    act.wait_ge(gi_done, TT)

                @block.vector
                def _(dve):
                    v = Steps(dve, v_step)
                    v.seq(dve.tensor_copy(IO[:, :], iota[:, 0:TOPK]))

                    def top16(many):
                        for x, rest, top, at in many:
                            v.mark(dve.max(top[:, 0:8], x))
                        v.wait()
                        for x, rest, top, at in many:
                            v.mark(dve.max_index(at[:, 0:8], top[:, 0:8], x))
                        for x, rest, top, at in many:
                            v.mark(dve.match_replace(rest, top[:, 0:8], x, NEG))
                        v.wait()
                        for x, rest, top, at in many:
                            v.mark(dve.max(top[:, 8:16], rest))
                        v.wait()
                        for x, rest, top, at in many:
                            v.mark(dve.max_index(at[:, 8:16], top[:, 8:16], rest))
                        v.wait()

                    for t in range(TT):
                        for c in range(NG):
                            g = t * NG + c
                            dve.wait_ge(s_taken, g + 1)
                            top16([(S[:, g % 2, i, :], SR[:, i, :], V[:, t, 4 * c + i, :], IX[:, t, 4 * c + i, :]) for i in range(4)])
                            dve.sem_inc(s_used, 1)
                        v1, v2 = V[:, t, 0:NQ:2, :], V[:, t, 1:NQ:2, :]
                        v.mark(dve.tensor_copy(IB[:, :, :], IX[:, t, :, :]))
                        v.mark(dve.tensor_tensor(CA[:, :, 0:64].rearrange("p h (a b) -> p h a b", a=4),
                                                 v1[:, :, 0:4].unsqueeze(3).broadcast_to([P, PH, 4, 16]),
                                                 v2.unsqueeze(2).broadcast_to([P, PH, 4, 16]), ALU.add))
                        v.mark(dve.tensor_tensor(CA[:, :, 64:NC].rearrange("p h (a b) -> p h a b", a=12),
                                                 v1[:, :, 4:16].unsqueeze(3).broadcast_to([P, PH, 12, 4]),
                                                 v2[:, :, 0:4].unsqueeze(2).broadcast_to([P, PH, 12, 4]), ALU.add))
                        v.wait()
                        top16([(CA[:, h, :], CB[:, h, :], TV[:, h, :], TP[:, h, :]) for h in range(PH)])
                        g = GS[:, t, 0, :].rearrange("p (h k) -> p h k", h=PH)
                        v.seq(dve.tensor_copy(SUM[:, :], TV[:, :, 0]))
                        dve.tensor_tensor(TV[:, :, :], TV[:, :, :], SUM[:, :].unsqueeze(2).broadcast_to([P, PH, TOPK]),
                                          ALU.subtract).then_inc(e_in, 1)
                        tp = TP[:, :, :].rearrange("p h k -> p (h k)")
                        v.mark(dve.tensor_single_scalar(DI[:, 0, :], tp, 4, ALU.logical_shift_right))
                        v.mark(dve.tensor_single_scalar(DI[:, 1, :], tp, 15, ALU.bitwise_and))
                        v.mark(dve.tensor_single_scalar(DI[:, 2, :], tp, 2, ALU.logical_shift_right))
                        v.mark(dve.tensor_single_scalar(DI[:, 3, :], tp, 3, ALU.bitwise_and))
                        v.mark(dve.tensor_scalar(HI[:, :], tp, 64.0, None, ALU.is_ge))
                        v.wait()
                        v.mark(dve.scalar_tensor_tensor(DF[:, 0, :], DI[:, 2, :], -12.0, DI[:, 0, :], ALU.add, ALU.subtract))
                        v.mark(dve.tensor_tensor(DF[:, 1, :], DI[:, 3, :], DI[:, 1, :], ALU.subtract))
                        v.wait()
                        v.seq(dve.tensor_tensor(DF[:, :, :], DF[:, :, :], HI[:, :].unsqueeze(1).broadcast_to([P, 2, PH * TOPK]), ALU.mult))
                        v.seq(dve.tensor_tensor(AB[:, :, :], DF[:, :, :], DI[:, 0:2, :], ALU.add))
                        for c in range(2):
                            v.seq(dve.tensor_tensor(EQ[:, :, :], AB[:, c, :].unsqueeze(2).broadcast_to([P, PH * TOPK, TOPK]),
                                                    IO[:, :].unsqueeze(1).broadcast_to([P, PH * TOPK, TOPK]), ALU.is_equal))
                            eq = EQ[:, :, :].rearrange("p (h k) a -> p h k a", h=PH)
                            v.seq(dve.tensor_tensor(eq, eq, IB[:, c:NQ:2, :].unsqueeze(2).broadcast_to([P, PH, TOPK, TOPK]), ALU.mult))
                            v.seq(dve.tensor_reduce(GS[:, t, 1 + c, :], EQ[:, :, :], mybir.AxisListType.X, ALU.add))
                        dve.wait_ge(e_out, t + 1)
                        v.seq(dve.tensor_reduce(SUM[:, :], TV[:, :, :], mybir.AxisListType.X, ALU.add))
                        v.seq(dve.reciprocal(SUM[:, :], SUM[:, :]))
                        dve.tensor_tensor(g, TV[:, :, :], SUM[:, :].unsqueeze(2).broadcast_to([P, PH, TOPK]),
                                          ALU.mult).then_inc(picked, 1)
                        dve.wait_ge(picked, t + 1)

        def peer_gates(GI, WD, ada):
            with ExitStack() as st:
                QUADS = 2 * TG // 4
                HALF = QUADS // 2
                TURNS = T // (2 * TG)
                RB = 4
                LT = sb(st, "first_one_hot", [P, RB, 4, P])
                RT = sb(st, "second_gated", [P, RB, 4, P])
                WS = sb(st, "spread", [P, 2, P, TG])
                PW = ps(st, "spread_ps", [P, 4, CH])
                lr_ready, w_done, w_taken, v_step = (sem(st, n) for n in ("lr_ready", "w_done", "w_taken", "v_step"))
                w_out = [sem(st, f"w_stored{n}") for n in range(2)]
                if ada is not None:
                    assert ADA_CH == 2 * TURNS and HALF == KB
                    AW = sb(st, "ada_w_ring", [P, 2, KB, CH])
                    ROW = sb(st, "mod_rows", [2, 2, CH])
                    PR = ps(st, "mod_row_ps", [P, 2, CH])
                    PM = ps(st, "mod_ps", [P, N_MOD * KB * 2])
                    ada_in = [sem(st, f"ada_w_in{n}") for n in range(2)]
                    ada_used, row_ready, turned = (sem(st, n) for n in ("ada_w_used", "row_ready", "turned"))
                block = st.enter_context(nc.Block())

                @block.sync
                def _(sp):
                    def ada_load(it, e):
                        sp.dma_start(AW[:, e].rearrange("p k n -> p (k n)"),
                                     I["ada_w"][bass.ds(it * 2 + (ada * ADA_CH + e), 1)].rearrange("a p k n -> p (a k n)")).then_inc(ada_in[e], 16)

                    def turn(it, more):
                        for g in range(2):
                            if more:
                                sp.wait_ge(ada_used, it * 2 + (g + 1))
                                ada_load(it + 1, g)
                            sp.wait_ge(w_taken, it * QUADS + (g + 1) * HALF)
                            sp.dma_start(WD[:, bass.ds(it * 2 + g, 1)].rearrange("p a j t -> p (a j t)"),
                                         WS[:, g].rearrange("p j t -> p (j t)")).then_inc(w_out[g], 16)

                    if ada is not None:
                        ada_load(0, 0)
                        ada_load(0, 1)
                    with sp.Fori(0, TURNS - 1) as it:
                        turn(it, ada is not None)
                    turn(TURNS - 1, False)
                    for g in range(2):
                        sp.wait_ge(w_out[g], 16 * TURNS)

                @block.vector
                def _(dve):
                    v = Steps(dve, v_step)

                    def quad(it, q, buffer_wait):
                        if buffer_wait:
                            dve.wait_ge(w_done, it * QUADS + (q - RB + 1))
                        tok = it * (2 * TG) + 4 * q
                        dve.tensor_tensor(LT[:, q % RB, :, :], iota.unsqueeze(1).broadcast_to([P, 4, P]),
                                          GI[:, 1, bass.ds(tok, 4)].unsqueeze(2).broadcast_to([P, 4, P]), ALU.is_equal)
                        for k in range(4):
                            ins = dve.tensor_scalar(RT[:, q % RB, k, :], iota, GI[:, 2, bass.ds(tok + k, 1)],
                                                    GI[:, 0, bass.ds(tok + k, 1)], ALU.is_equal, ALU.mult)
                        ins.then_inc(lr_ready, 1)

                    for q in range(QUADS):
                        quad(0, q, q >= RB)
                    with dve.Fori(1, TURNS) as it:
                        for q in range(QUADS):
                            quad(it, q, True)
                    if ada is not None:
                        dve.wait_ge(turned, ADA_CH)
                        finish_modulation(dve, v, ada, PM)

                @block.tensor
                def _(pe):
                    def ada_turn(it, e):
                        pe.wait_ge(row_ready, it * 2 + (e + 1))
                        for c in range(CH // P):
                            mm = pe.matmul(PM[:, bass.ds(it * (2 * ADA_COLS) + (e * ADA_COLS + c * 2), 2)],
                                           ROW[:, e, c * P:(c + 1) * P], CST[0:2, C_IDENT:C_IDENT + 2], start=True, stop=True)
                        mm.then_inc(turned, 1)

                    def quad(it, q, bank_wait):
                        pe.wait_ge(lr_ready, it * QUADS + (q + 1))
                        if bank_wait:
                            pe.wait_ge(w_taken, it * QUADS + (q - 3))
                        for k in range(4):
                            mm = pe.matmul(PW[:, q % 4, k * P:(k + 1) * P], LT[:, q % RB, k, :], RT[:, q % RB, k, :],
                                           start=True, stop=True)
                        mm.then_inc(w_done, 1)
                        if ada is not None:
                            e, k = divmod(q, HALF)
                            if k == 0:
                                pe.wait_ge(ada_in[e], it * 16 + 16)
                            mm = pe.matmul(PR[0:2, e, :], CT[:, k, :], AW[:, e, k, :], start=(k == 0), stop=(k == KB - 1))
                            if k == KB - 1:
                                mm.then_inc(ada_used, 1)
                            if q == HALF + 3:
                                ada_turn(it, 0)
                            if q == QUADS - 1:
                                ada_turn(it, 1)

                    for q in range(QUADS):
                        quad(0, q, q >= 4)
                    with pe.Fori(1, TURNS) as it:
                        for q in range(QUADS):
                            quad(it, q, True)

                @block.scalar
                def _(act):
                    def quad(it, q, later):
                        if later and q % HALF == 0:
                            act.wait_ge(w_out[q // HALF], it * 16)
                        act.wait_ge(w_done, it * QUADS + (q + 1))
                        g, k = divmod(q, HALF)
                        act.activation(WS[:, g, :, 4 * k:4 * k + 4].rearrange("p j t -> p t j"),
                                       PW[:, q % 4, :].rearrange("p (t j) -> p t j", t=4), ACT.Copy).then_inc(w_taken, 1)
                        if ada is not None and q in (HALF + 1, QUADS - 1):
                            e = q // (QUADS - 1)
                            act.wait_ge(ada_used, it * 2 + (e + 1))
                            if later:
                                act.wait_ge(turned, it * 2 + (e - 1))
                            act.activation(ROW[:, e, :], PR[0:2, e, :], ACT.Copy).then_inc(row_ready, 1)

                    for q in range(QUADS):
                        quad(0, q, False)
                    with act.Fori(1, TURNS) as it:
                        for q in range(QUADS):
                            quad(it, q, True)

        def peer_experts(l, HH, HL, WD, out=None):
            with ExitStack() as st:
                NCHK, BODY = N_KEYS // JC, 2 * JC
                TURNS = N_KEYS // BODY
                U = sb(st, "u_ring", [P, 2, JC, KB * P])
                V = sb(st, "v_ring", [P, 2, JC, D])
                W = sb(st, "w_ring", [P, 2, T // TG, JC * TG])
                UH, UL = (sb(st, n, [P, 2, KB * P], F32R) for n in ("u_hi", "u_lo"))
                VH, VL = (sb(st, n, [P, 2, D], F32R) for n in ("v_hi", "v_lo"))
                G = sb(st, "gelu", [P, 2, T])
                A = sb(st, "act", [P, 2, T])
                AH, AL = (sb(st, n, [P, 2, T], F32R) for n in ("act_hi", "act_lo"))
                LN = sb(st, "ln_rows", [P, 2, D])
                S = norm_tiles(st)
                PO = ps(st, "out_ps", [P, TT, 2, CH])
                PH_ = ps(st, "hidden_ps", [P, 2, CH])
                u_in, v_in, w_in = ([sem(st, f"{n}{s}") for s in range(2)] for n in ("u_in", "v_in", "w_in"))
                x_ready = sem(st, "x_ready")
                (row_in, v_step, uh, ul, vh, vl, h_done, g_done, a_done, o_done, root_in, root_out, x_out) = (
                    sem(st, n) for n in ("row_in", "v_step", "uh_ready", "ul_ready", "vh_ready", "vl_ready", "h_done", "g_done",
                                         "a_done", "o_done", "root_in", "root_out", "x_out"))
                block = st.enter_context(nc.Block())
                LAST = TURNS - 1

                def turns(eng, step):
                    for jj in range(BODY):
                        step(0, jj, True, False)
                    with eng.Fori(1, LAST) as it:
                        for jj in range(BODY):
                            step(it, jj, False, False)
                    for jj in range(BODY):
                        step(LAST, jj, False, True)

                @block.sync
                def _(sp):
                    def load(it, s, wait):
                        if wait:
                            sp.wait_ge(ul, it * BODY + (JC * (s - 1)))
                        sp.dma_start(U[:, s].rearrange("p j n -> p (j n)"), I["peer_u"][l, bass.ds(it * 2 + s, 1)].rearrange("c p j k i -> p (c j k i)")).then_inc(u_in[s], 16)
                        if wait:
                            sp.wait_ge(vl, it * BODY + (JC * (s - 1)))
                        sp.dma_start(V[:, s].rearrange("p j n -> p (j n)"), I["peer_v"][l, bass.ds(it * 2 + s, 1)].rearrange("c p j d -> p (c j d)")).then_inc(v_in[s], 16)
                        if wait:
                            sp.wait_ge(a_done, it * BODY + (JC * (s - 1)))
                        sp.dma_start(W[:, s], WD[:, :, bass.ds(it * BODY + JC * s, JC), :].rearrange("p g j t -> p g (j t)")).then_inc(w_in[s], 16)

                    load(0, 0, False)
                    load(0, 1, False)
                    with sp.Fori(1, TURNS) as it:
                        load(it, 0, True)
                        load(it, 1, True)
                    sp.dma_start(LN[:, 0, :], spread(I["ln_g"][l, 1:2, :], D)).then_inc(row_in, 16)
                    sp.dma_start(LN[:, 1, :], spread(I["ln_b"][l, 1:2, :], D)).then_inc(row_in, 16)
                    if out is not None:
                        for t in range(TT):
                            sp.wait_ge(x_ready, t + 1)
                            sp.dma_start(out[t], X[:, t, :]).then_inc(x_out, 16)
                        sp.wait_ge(x_out, 16 * TT)

                @block.tensor
                def _(pe):
                    def hidden(it, jj):
                        b = jj % 2
                        pe.wait_ge(uh, it * BODY + (jj + 1))
                        pe.wait_ge(ul, it * BODY + (jj + 1))
                        for k in range(KB):
                            for n, (u, x) in enumerate(((UH, HH), (UH, HL), (UL, HH))):
                                mm = pe.matmul(PH_[:, b, 0:T], u[:, b, k * P:(k + 1) * P], x[:, k, :],
                                               start=(k == 0 and n == 0), stop=(k == KB - 1 and n == 2))
                        mm.then_inc(h_done, 1)

                    def step(it, jj, first, last):
                        if not (last and jj == BODY - 1):
                            if not first or jj >= 1:
                                pe.wait_ge(g_done, it * BODY + jj)
                            hidden(it, jj + 1)
                        b = jj % 2
                        pe.wait_ge(a_done, it * BODY + (jj + 1))
                        pe.wait_ge(vl, it * BODY + (jj + 1))
                        for t in range(TT):
                            for c in range(2):
                                for n, (a, x) in enumerate(((AH, VH), (AH, VL), (AL, VH))):
                                    mm = pe.matmul(PO[:, t, c, :], a[:, b, t * P:(t + 1) * P], x[:, b, c * CH:(c + 1) * CH],
                                                   start=(first and jj == 0 and n == 0), stop=(last and jj == BODY - 1 and n == 2),
                                                   skip_group_check=True)
                        mm.then_inc(o_done, 1)

                    hidden(0, 0)
                    turns(pe, step)

                @block.scalar
                def _(act):
                    def u_part(it, jj):
                        s = jj // JC % 2
                        if jj % JC == 0:
                            act.wait_ge(u_in[s], it * 16 + 16 * (jj // BODY + 1))
                        act.activation(UH[:, jj % 2, :], U[:, s, jj % JC, :], ACT.Copy).then_inc(uh, 1)

                    def v_part(it, jj):
                        s = jj // JC % 2
                        if jj % JC == 0:
                            act.wait_ge(v_in[s], it * 16 + 16 * (jj // BODY + 1))
                        act.activation(VH[:, jj % 2, :], V[:, s, jj % JC, :], ACT.Copy).then_inc(vh, 1)

                    def step(it, jj, first, last):
                        act.wait_ge(h_done, it * BODY + (jj + 1))
                        if not first or jj >= 2:
                            act.wait_ge(a_done, it * BODY + (jj - 1))
                        act.activation(G[:, jj % 2, :], PH_[:, jj % 2, 0:T], ACT.Gelu_apprx_tanh).then_inc(g_done, 1)
                        if not last or jj + 2 < BODY:
                            u_part(it, jj + 2)
                        if not last or jj + 1 < BODY:
                            if not first or jj >= 1:
                                act.wait_ge(o_done, it * BODY + jj)
                            v_part(it, jj + 1)

                    u_part(0, 0)
                    u_part(0, 1)
                    v_part(0, 0)
                    turns(act, step)
                    for t in range(TT):
                        norm_root(act, root_in, root_out, S, t, t + 1)

                @block.vector
                def _(dve):
                    v = Steps(dve, v_step)

                    def u_part(it, jj):
                        dve.wait_ge(uh, it * BODY + (jj + 1))
                        dve.tensor_tensor(UL[:, jj % 2, :], U[:, jj // JC % 2, jj % JC, :], UH[:, jj % 2, :].bitcast(F32),
                                          ALU.subtract).then_inc(ul, 1)

                    def v_part(it, jj):
                        dve.wait_ge(vh, it * BODY + (jj + 1))
                        dve.tensor_tensor(VL[:, jj % 2, :], V[:, jj // JC % 2, jj % JC, :], VH[:, jj % 2, :].bitcast(F32),
                                          ALU.subtract).then_inc(vl, 1)

                    def step(it, jj, first, last):
                        b = jj % 2
                        dve.wait_ge(g_done, it * BODY + (jj + 1))
                        if jj % JC == 0:
                            dve.wait_ge(w_in[jj // JC], it * 16 + 16)
                        if not first or jj >= 2:
                            dve.wait_ge(o_done, it * BODY + (jj - 1))
                        dve.tensor_tensor(A[:, b, :].rearrange("p (g t) -> p g t", t=TG), G[:, b, :].rearrange("p (g t) -> p g t", t=TG),
                                          W[:, jj // JC, :, (jj % JC) * TG:(jj % JC + 1) * TG], ALU.mult).then_inc(v_step, 1)
                        dve.wait_ge(v_step, it * (2 * BODY) + (2 * jj + 1))
                        dve.tensor_copy(AH[:, b, :], A[:, b, :]).then_inc(v_step, 1)
                        dve.wait_ge(v_step, it * (2 * BODY) + (2 * jj + 2))
                        dve.tensor_tensor(AL[:, b, :], A[:, b, :], AH[:, b, :].bitcast(F32), ALU.subtract).then_inc(a_done, 1)
                        if not last or jj + 2 < BODY:
                            u_part(it, jj + 2)
                        if not last or jj + 1 < BODY:
                            v_part(it, jj + 1)

                    u_part(0, 0)
                    u_part(0, 1)
                    v_part(0, 0)
                    turns(dve, step)
                    v.n = 2 * N_KEYS
                    dve.wait_ge(row_in, 32)
                    dve.wait_ge(o_done, N_KEYS)
                    for t in range(TT):
                        norm_rows(dve, v, root_in, root_out, x_ready, PO[:, t].rearrange("p a n -> p (a n)"), t, LN, S, t + 1)
                    dve.wait_ge(x_ready, TT)

        def peer(l, out=None):
            with ExitStack() as st:
                HH = sb(st, "h_hi", [P, KB, T], F32R)
                HL = sb(st, "h_lo", [P, KB, T], F32R)
                GI = sb(st, "picks", [P, 3, T])
                with ExitStack() as inner:
                    HT = sb(inner, "HT", [P, KB, T])
                    W = sb(inner, "peer_wq", [P, 4, KB, CH])
                    KEY = sb(inner, "keys_t", [P, 2, N_KEYS])
                    w_in = [sem(inner, f"peer_w_in{n}") for n in range(4)]
                    key_in = sem(inner, "key_in")
                    loads = [(W[:, n], I["peer_w_q"][l, n], w_in[n]) for n in range(4)]
                    loads.insert(1, (KEY[:, :, :], I["peer_keys"][l], key_in))
                    transpose_modulate(HT, l, 3, (HH, HL), loads)
                    peer_select(HT, W, w_in, KEY, key_in, GI)
                peer_gates(GI, WD, 1 if l == 0 else None)
                peer_experts(l, HH, HL, WD, out)

        def odd_project(HT, W, w_in, Z, GS):
            with ExitStack() as st:
                NCH, NW = len(w_in), W.shape[-1]
                NN = GQ_HEADS + KV_HEADS
                QG = sb(st, "qk_gain", [P, 2 * HD])
                SQ = sb(st, "squares", [P, NN, HD])
                MS = sb(st, "mean_square", [P, TT, NN])
                RO = sb(st, "rotated", [P, 4, ROPE_HEADS, 32])
                PJ = ps(st, "proj_ps", [P, 4, CH])
                g_in, done, taken, v_step, root_in, root_out, rows_ready, out_st = (
                    sem(st, n) for n in ("gain_in", "proj_done", "proj_taken", "v_step", "root_in", "root_out", "rows_ready", "rows_out"))
                block = st.enter_context(nc.Block())
                ORDER = (0, 1, 2)

                @block.sync
                def _(sp):
                    sp.wait_ge(rows_ready, 1)
                    sp.dma_start(O["new_gk"], Z[:, 0, 512:640]).then_inc(out_st, 16)
                    sp.dma_start(O["new_dk"], Z[:, 0, 1152:1664]).then_inc(out_st, 16)
                    sp.dma_start(O["new_gv"], Z[:, 0, 1664:1792]).then_inc(out_st, 16)
                    sp.dma_start(O["new_dv"], Z[:, 0, 1792:2304]).then_inc(out_st, 16)
                    sp.wait_ge(out_st, 64)

                @block.tensor
                def _(pe):
                    for i, t in enumerate(ORDER):
                        for n in range(NCH):
                            item = i * NCH + n
                            pe.wait_ge(w_in[n], 16)
                            if item >= 4:
                                pe.wait_ge(taken, item - 3)
                            for k in range(KB):
                                mm = pe.matmul(PJ[:, item % 4, 0:NW], HT[:, k, t * P:(t + 1) * P], W[:, n, k, :],
                                               start=(k == 0), stop=(k == KB - 1))
                            mm.then_inc(done, 1)

                @block.scalar
                def _(act):
                    act.dma_start(QG[:, :], spread(I["qk_norm_g"], 2 * HD)).then_inc(g_in, 16)
                    for i, t in enumerate(ORDER):
                        for n in range(NCH):
                            item = i * NCH + n
                            act.wait_ge(done, item + 1)
                            act.activation(Z[:, t, n * NW:(n + 1) * NW], PJ[:, item % 4, 0:NW], ACT.Copy).then_inc(taken, 1)
                        act.wait_ge(root_in, i + 1)
                        act.activation(MS[:, t, :], MS[:, t, :], ACT.Sqrt).then_inc(root_out, 1)

                @block.vector
                def _(dve):
                    v = Steps(dve, v_step)
                    dve.wait_ge(g_in, 16)
                    for i, t in enumerate(ORDER):
                        z = Z[:, t, 0:NN * HD].rearrange("p (h e) -> p h e", h=NN)
                        dve.wait_ge(taken, i * NCH + 2)
                        v.seq(dve.tensor_tensor(SQ[:, :, :], z, z, ALU.mult))
                        v.seq(dve.tensor_reduce(MS[:, t, :], SQ[:, :, :], AX, ALU.add))
                        dve.tensor_scalar(MS[:, t, :], MS[:, t, :], 1.0 / HD, RMS_EPS, ALU.mult, ALU.add).then_inc(root_in, 1)
                        dve.wait_ge(root_out, i + 1)
                        v.seq(dve.reciprocal(MS[:, t, :], MS[:, t, :]))
                        v.seq(dve.tensor_tensor(z, z, MS[:, t, :].unsqueeze(2).broadcast_to([P, NN, HD]), ALU.mult))
                        for a, b, g in ((0, GQ_HEADS, 0), (GQ_HEADS, NN, 1)):
                            v.mark(dve.tensor_tensor(z[:, a:b, :], z[:, a:b, :],
                                                     QG[:, g * HD:(g + 1) * HD].unsqueeze(1).broadcast_to([P, b - a, HD]), ALU.mult))
                        v.wait()
                        dve.wait_ge(taken, (i + 1) * NCH)
                        if t:
                            x = Z[:, t, 0:ROPE_HEADS * HD].rearrange("p (h a n f) -> p h a n f", h=ROPE_HEADS, a=2, n=2)
                            o = (t - 1) * 32
                            cos, sin = (CST[:, c + o:c + o + 32].rearrange("p (a f) -> p a f", a=2).unsqueeze(1)
                                        .broadcast_to([P, ROPE_HEADS, 2, 16]) for c in (C_COS, C_SIN))
                            r = [RO[:, k].rearrange("p h (a f) -> p h a f", a=2) for k in range(4)]
                            for k, (half, table) in enumerate(((0, cos), (1, sin), (0, sin), (1, cos))):
                                v.mark(dve.tensor_tensor(r[k], x[:, :, :, half, :], table, ALU.mult))
                            v.wait()
                            v.mark(dve.tensor_tensor(x[:, :, :, 0, :], r[0], r[1], ALU.subtract))
                            v.mark(dve.tensor_tensor(x[:, :, :, 1, :], r[2], r[3], ALU.add))
                            v.wait()
                        for g in range(2):
                            ins = dve.tensor_copy(GS[:, t, g * HD:(g + 1) * HD], Z[:, t, 512 + (1 - g) * HD:512 + (2 - g) * HD])
                            if g == 0:
                                v.mark(ins)
                        ins.then_inc(rows_ready, 1)
                        dve.wait_ge(rows_ready, i + 1)

        def attend(Z, GS, MIX, ahead):
            with ExitStack() as st:
                QT = sb(st, "q_t", [P, 8, T])
                KT = sb(st, "k_t", [P, 6, 4 * P])
                CK = sb(st, "ctx_k", [P, 6, P])
                CV = sb(st, "ctx_v", [P, 5 * P])
                E = sb(st, "exp_s", [P, 2, 2, 3 * P])
                ET = sb(st, "exp_t", [P, 2, 2, 3 * P])
                MX = sb(st, "row_max", [P, 2, 2])
                SB = 4
                SU = sb(st, "row_sum", [P, SB, 2])
                TMP = sb(st, "diff_tmp", [P, 2, P])
                LB = sb(st, "lambda_rows", [P, 4 * HD])
                NL = sb(st, "minus_lambda", [P, 4])
                SG = sb(st, "subln_gain", [P, P])
                SQ = sb(st, "squares", [P, TT, H, P])
                MS = sb(st, "mean_square", [P, TT, H])
                PS = ps(st, "score_ps", [P, 2, 2, CH])
                PT = ps(st, "exp_t_ps", [P, 2, CH])
                PO = ps(st, "o_ps", [P, 2, CH])
                (c_in, l_in, v_step, turned, turn_taken, l_sum, l_exp, s_done, m_ready, e_done, t_done, t_taken, o_done, o_taken,
                 root_in, root_out, neg_l, swapped) = (
                    sem(st, n) for n in ("cache_in", "lambda_in", "v_step", "turned", "turn_taken", "l_sum", "l_exp", "s_done",
                                         "m_ready", "e_done", "t_done", "t_taken", "o_done", "o_taken", "root_in", "root_out", "neg_l", "swapped"))
                block = st.enter_context(nc.Block())
                UNITS = [(t, u) for t in (0, 1, 2) for u in range(8)]
                TURNS = ([(QT[:, b, :], [Z[:, t, b * P:(b + 1) * P] for t in range(TT)]) for b in range(4)]
                         + [(QT[:, 4 + b, :], [Z[:, t, 640 + b * P:640 + (b + 1) * P] for t in range(TT)]) for b in range(4)]
                         + [(KT[:, 0, :], [Z[:, t, 512:640] for t in range(TT)] + [CK[:, 0, :]])]
                         + [(KT[:, 1, :], [GS[:, t, :] for t in range(TT)] + [CK[:, 1, :]])]
                         + [(KT[:, 2 + b, :], [Z[:, t, 1152 + b * P:1152 + (b + 1) * P] for t in range(TT)] + [CK[:, 2 + b, :]])
                            for b in range(4)])

                def banks(n):
                    return PS[:, n // 2 % 2, n % 2, :]

                @block.sync
                def _(sp):
                    sp.dma_start(CK[:, 0, :], I["cache_gk"]).then_inc(c_in, 16)
                    for g in range(2):
                        sp.dma_start(CK[:, 1, g * HD:(g + 1) * HD], I["cache_gk"][:, (1 - g) * HD:(2 - g) * HD]).then_inc(c_in, 16)
                    sp.dma_start(CK[:, 2:6, :].rearrange("p b n -> p (b n)"), I["cache_dk"]).then_inc(c_in, 16)
                    sp.dma_start(CV[:, 0:P], I["cache_gv"]).then_inc(c_in, 16)
                    sp.dma_start(CV[:, P:5 * P], I["cache_dv"]).then_inc(c_in, 16)
                    sp.dma_start(LB[:, :], spread(I["diff_lambda"], 4 * HD)).then_inc(l_in, 16)
                    sp.dma_start(SG[:, :], spread(I["diff_subln_g"], P)).then_inc(l_in, 16)
                    load_ahead(sp, ahead)

                @block.tensor
                def _(pe):
                    for n, (dst, src) in enumerate(TURNS):
                        if n >= 4:
                            pe.wait_ge(turn_taken, n - 3)
                        if n == 8:
                            pe.wait_ge(c_in, 96)
                        for k, x in enumerate(src):
                            mm = pe.transpose(banks(n)[:, k * P:(k + 1) * P], x, ident)
                        mm.then_inc(turned, 1)
                    pe.wait_ge(turn_taken, len(TURNS))

                    def scores(n):
                        t, u = UNITS[n]
                        a, b = (0, P) if t == 0 else (P, 4 * P)
                        if n >= 2:
                            pe.wait_ge(e_done, n - 1)
                        for c in range(2):
                            r = slice(c * HD, (c + 1) * HD)
                            kb = (0 if u // 2 == c else 1) if u < 4 else 2 + u - 4
                            mm = pe.matmul(PS[:, n % 2, c, 0:b - a], QT[r, u, t * P:(t + 1) * P], KT[r, kb, a:b], start=True, stop=True)
                        mm.then_inc(s_done, 1)

                    def weighted(n):
                        t, u = UNITS[n]
                        m = 1 if t == 0 else 3
                        pe.wait_ge(t_taken, n + 1)
                        if n >= 2:
                            pe.wait_ge(o_taken, n - 1)
                        for c in range(2):
                            w = HD if u < 4 else P
                            for i in range(m):
                                off = (u // 2) * HD if u < 4 else P + (u - 4) * P
                                src = Z[:, 0, 1664 + off:1664 + off + w] if t == 0 else (
                                    Z[:, 1 + i, 1664 + off:1664 + off + w] if i < 2 else CV[:, off:off + w])
                                mm = pe.matmul(PO[:, n % 2, c * P:c * P + w], ET[:, n % 2, c, i * P:(i + 1) * P], src,
                                               start=(i == 0), stop=(i == m - 1))
                        mm.then_inc(o_done, 1)

                    scores(0)
                    for n, (t, u) in enumerate(UNITS):
                        if n + 1 < len(UNITS):
                            scores(n + 1)
                        m = 1 if t == 0 else 3
                        pe.wait_ge(e_done, n + 1)
                        if n >= 1:
                            pe.wait_ge(t_taken, n)
                        for c in range(2):
                            for i in range(m):
                                mm = pe.transpose(PT[:, c, i * P:(i + 1) * P], E[:, n % 2, c, i * P:(i + 1) * P], ident)
                        mm.then_inc(t_done, 1)
                        if n:
                            weighted(n - 1)
                    weighted(len(UNITS) - 1)

                @block.scalar
                def _(act):
                    for n, (dst, src) in enumerate(TURNS):
                        act.wait_ge(turned, n + 1)
                        act.activation(dst, banks(n)[:, 0:len(src) * P], ACT.Copy).then_inc(turn_taken, 1)
                    act.wait_ge(l_sum, 1)
                    act.activation(NL[:, 0:2], NL[:, 0:2], ACT.Exp).then_inc(l_exp, 1)

                    def exps(n):
                        t, u = UNITS[n]
                        m = P if t == 0 else 3 * P
                        act.wait_ge(m_ready, n + 1)
                        if n >= 2:
                            act.wait_ge(t_done, n - 1)
                        if n >= SB:
                            act.wait_ge(o_taken, n - SB + 1)
                        for c in range(2):
                            ins = act.activation(E[:, n % 2, c, 0:m], PS[:, n % 2, c, 0:m], ACT.Exp, scale=HD ** -0.5,
                                                 bias=MX[:, n % 2, c:c + 1], accum_out=SU[:, n % SB, c:c + 1])
                        ins.then_inc(e_done, 1)

                    exps(0)
                    for n, (t, u) in enumerate(UNITS):
                        if n + 1 < len(UNITS):
                            exps(n + 1)
                        m = P if t == 0 else 3 * P
                        act.wait_ge(t_done, n + 1)
                        if n >= 2:
                            act.wait_ge(o_done, n - 1)
                        act.activation(ET[:, n % 2, :, 0:m], PT[:, :, 0:m], ACT.Copy).then_inc(t_taken, 1)
                    act.wait_ge(root_in, 1)
                    act.activation(MS[:, :, :], MS[:, :, :], ACT.Sqrt).then_inc(root_out, 1)

                @block.vector
                def _(dve):
                    v = Steps(dve, v_step)
                    dve.wait_ge(l_in, 32)
                    l = LB[:, :].rearrange("p (a b e) -> p a b e", a=2, b=2)
                    v.seq(dve.tensor_tensor(TMP[:, 0, :].rearrange("p (a e) -> p a e", a=2), l[:, :, 0, :], l[:, :, 1, :], ALU.mult))
                    dve.tensor_reduce(NL[:, 0:2], TMP[:, 0, :].rearrange("p (a e) -> p a e", a=2), AX, ALU.add).then_inc(l_sum, 1)
                    dve.wait_ge(l_exp, 1)
                    v.seq(dve.tensor_tensor(NL[:, 2:3], NL[:, 1:2], NL[:, 0:1], ALU.subtract))
                    v.seq(dve.tensor_scalar_add(NL[:, 2:3], NL[:, 2:3], -LAM_INIT))
                    dve.wait_ge(turn_taken, len(TURNS))

                    def maxes(n):
                        t, u = UNITS[n]
                        m = P if t == 0 else 3 * P
                        dve.wait_ge(s_done, n + 1)
                        if n >= 2:
                            dve.wait_ge(e_done, n - 1)
                        v.seq(dve.tensor_reduce(MX[:, n % 2, :], PS[:, n % 2, :, 0:m], AX, ALU.max))
                        dve.tensor_scalar_mul(MX[:, n % 2, :], MX[:, n % 2, :], -HD ** -0.5).then_inc(m_ready, 1)

                    def heads(n):
                        t, u = UNITS[n]
                        b, su = n % 2, SU[:, n % SB, :]
                        dve.wait_ge(e_done, n + 1)
                        v.seq(dve.reciprocal(su, su))
                        if u >= 4:
                            v.seq(dve.tensor_tensor(su[:, 1:2], su[:, 1:2], NL[:, 2:3], ALU.mult))
                        dve.wait_ge(o_done, n + 1)
                        if u < 4:
                            v.mark(dve.tensor_scalar(MIX[:, t, u, 0:HD], PO[:, b, 0:HD], su[:, 0:1], None, ALU.mult))
                            dve.tensor_scalar(MIX[:, t, u, HD:P], PO[:, b, P:P + HD], su[:, 1:2], None, ALU.mult).then_inc(o_taken, 1)
                        else:
                            v.seq(dve.tensor_scalar(TMP[:, b, :], PO[:, b, P:2 * P], su[:, 1:2], None, ALU.mult))
                            dve.scalar_tensor_tensor(MIX[:, t, u, :], PO[:, b, 0:P], su[:, 0:1], TMP[:, b, :],
                                                     ALU.mult, ALU.add).then_inc(o_taken, 1)

                    maxes(0)
                    for n in range(1, len(UNITS)):
                        maxes(n)
                        if n >= 2:
                            heads(n - 2)
                    heads(len(UNITS) - 2)
                    heads(len(UNITS) - 1)
                    dve.wait_ge(o_taken, len(UNITS))
                    for t in range(TT):
                        v.mark(dve.tensor_tensor(SQ[:, t], MIX[:, t, 4:8, :], MIX[:, t, 4:8, :], ALU.mult))
                    v.wait()
                    v.seq(dve.tensor_reduce(MS[:, :, :], SQ[:, :, :, :], AX, ALU.add))
                    dve.tensor_scalar(MS[:, :, :], MS[:, :, :], 1.0 / P, RMS_EPS, ALU.mult, ALU.add).then_inc(root_in, 1)
                    dve.wait_ge(root_out, 1)
                    v.seq(dve.reciprocal(MS[:, :, :], MS[:, :, :]))
                    v.seq(dve.tensor_scalar_mul(SG[:, :], SG[:, :], 1.0 - LAM_INIT))
                    for t in range(TT):
                        v.seq(dve.tensor_tensor(MIX[:, t, 4:8, :], MIX[:, t, 4:8, :], MS[:, t, :].unsqueeze(2).broadcast_to([P, H, P]), ALU.mult))
                        v.seq(dve.tensor_tensor(MIX[:, t, 4:8, :], MIX[:, t, 4:8, :], SG[:, :].unsqueeze(1).broadcast_to([P, H, P]), ALU.mult))

        def mlstm(QKT, MVA, MO, LI, FF, MIX, ahead):
            with ExitStack() as st:
                R = 64
                C0 = sb(st, "mstate0", [P, 2, H, P + 1])
                CU = sb(st, "mstate1", [P, 2, H, P + 1])
                NC = sb(st, "prompt_mstate", [P, 2, H, P + 1])
                LF, BB, CR, NM, EM = (sb(st, n, [R, T]) for n in ("log_f", "b_sum", "c_rows", "m_rows", "exp_m_rows"))
                MM = sb(st, "run_max", [R, T])
                ONE = sb(st, "ones", [R, P])
                SM = sb(st, "m_ends", [R, TT, 2])
                M0 = sb(st, "m0", [R, 1])
                COL = sb(st, "cols", [P, 2, TT, R])
                MC = sb(st, "m_cols", [P, 2 * H, TT, 2])
                WIN = sb(st, "w_in", [P, 4, H])
                WOLD = sb(st, "w_old", [P, 2, H])
                AM = sb(st, "att_masked", [P, 2, H, TT, P])
                EE = sb(st, "exp_w", [P, TT, 2, H, P])
                QS = sb(st, "q_scaled", [P, 2, 2, H, P])
                KW = sb(st, "k_weighed", [P, 2, 4, P])
                DEN = sb(st, "den", [P, 2, 2])
                HB = sb(st, "h_tmp", [P, 2, P])
                PB = ps(st, "m_ps", [P, 2, CH])
                PA = ps(st, "att_ps", [P, CH])
                PK = ps(st, "k_ps", [P, CH])
                PC = ps(st, "c_ps", [P, 2, CH])
                PN = ps(st, "num_ps", [P, 2, CH])
                (s_in, m_in, zeroed, a_step, v_step, absf, ln_done, c_ready, m_ready, em_ready, cols_done, small_done,
                 cols_ready, small_ready, mb_done, mb_taken, e_sub, e_exp, att_done, att_taken, kt_done, k_rows, win_sub, win_exp,
                 wt_ready, q_sub, q_exp, q_ready, cu_done, cu_taken, num_done, num_taken, out_st) = (
                    sem(st, n) for n in (
                        "state_in", "m_in", "zeroed", "a_step", "v_step", "absf", "ln_done", "c_ready", "m_ready", "em_ready",
                        "cols_done", "small_done", "cols_ready", "small_ready", "mb_done", "mb_taken", "e_sub", "e_exp",
                        "att_done", "att_taken", "kt_done", "k_rows", "win_sub", "win_exp", "wt_ready", "q_sub", "q_exp",
                        "q_ready", "cu_done", "cu_taken", "num_done", "num_taken", "out_st"))
                block = st.enter_context(nc.Block())
                KINDS = ((0, 0), (0, 1), (1, 0), (2, 1))
                UNITS = [(t, d) for t in range(TT) for d in range(2)]
                scale_in = [(t, d) for t, d in UNITS if t]

                @block.sync
                def _(sp):
                    sp.dma_start(C0[:, :, :, :], I["state_mlstm"]).then_inc(s_in, 16)
                    sp.wait_ge(zeroed, 1)
                    for d in range(2):
                        sp.dma_start(M0[32 * d:32 * d + H, :], I["state_m"][d]).then_inc(m_in, 16)
                    load_ahead(sp, ahead)
                    sp.wait_ge(m_ready, 1)
                    sp.dma_start(O["new_m"][0], NM[0:H, P - 1:P]).then_inc(out_st, 16)
                    sp.dma_start(O["new_m"][1], NM[32:32 + H, 0:1]).then_inc(out_st, 16)
                    sp.wait_ge(cu_taken, H)
                    sp.dma_start(O["new_mlstm"], NC[:, :, :, :]).then_inc(out_st, 16)
                    sp.wait_ge(out_st, 48)

                @block.gpsimd
                def _(pool):
                    pool.memset(M0[:, :], 0.0).then_inc(zeroed, 1)
                    pool.memset(ONE[:, :], 1.0).then_inc(zeroed, 1)
                    pool.memset(MM[:, :], 0.0).then_inc(zeroed, 1)
                    pool.memset(BB[:, :], 0.0).then_inc(zeroed, 1)
                    pool.memset(SM[:, :, :], 0.0).then_inc(zeroed, 1)

                @block.tensor
                def _(pe):
                    pe.wait_ge(m_ready, 1)
                    pe.wait_ge(em_ready, 1)
                    for n, src in enumerate((CR, EM)):
                        for t in range(TT):
                            mm = pe.transpose(PK[:, (n * TT + t) * R:(n * TT + t + 1) * R], src[:, t * P:(t + 1) * P],
                                              CST[0:R, C_IDENT:C_IDENT + R])
                    mm.then_inc(cols_done, 1)
                    for n in range(2 * H):
                        mm = pe.matmul(PA[:, n * 6:(n + 1) * 6], CST[0:R, C_SEL + n * P:C_SEL + (n + 1) * P],
                                       SM[:, :, :].rearrange("p t j -> p (t j)"), start=True, stop=True)
                    mm.then_inc(small_done, 1)
                    for u, (t, d) in enumerate(UNITS):
                        if u >= 2:
                            pe.wait_ge(mb_taken, u - 1)
                        for h in range(H):
                            n = d * H + h
                            mm = pe.matmul(PB[:, u % 2, h * P:(h + 1) * P], CST[0:R, C_SEL + n * P:C_SEL + (n + 1) * P],
                                           MM[:, t * P:(t + 1) * P], start=True, stop=True)
                        mm.then_inc(mb_done, 1)
                    pe.wait_ge(small_ready, 1)
                    for h in range(H):
                        if h:
                            pe.wait_ge(att_taken, h)
                        for t in range(TT):
                            mm = pe.matmul(PA[:, t * P:(t + 1) * P], QKT[:, 3 * H + h, t * P:(t + 1) * P],
                                           QKT[:, 2 * H + h, t * P:(t + 1) * P], start=True, stop=True)
                        mm.then_inc(att_done, 1)
                    pe.wait_ge(cols_ready, 1)
                    pe.wait_ge(s_in, 16)
                    for h in range(H):
                        if h:
                            pe.wait_ge(k_rows, h)
                            pe.wait_ge(cu_taken, h)
                        for t in range(TT):
                            mm = pe.transpose(PK[:, t * P:(t + 1) * P], QKT[:, 3 * H + h, t * P:(t + 1) * P], ident)
                        mm.then_inc(kt_done, 1)
                        pe.wait_ge(k_rows, h + 1)
                        for n, (t, d) in enumerate(KINDS):
                            mm = pe.matmul(PC[:, n // 2, n % 2 * (P + 1):(n % 2 + 1) * (P + 1)], KW[:, h % 2, n, :],
                                           MVA[:, t, h, :], start=True, stop=True)
                        mm.then_inc(cu_done, 1)
                    pe.wait_ge(cu_taken, H)
                    pe.wait_ge(wt_ready, 6)
                    pe.wait_ge(q_ready, 4)
                    for n in range(TT * H):
                        t, h = divmod(n, H)
                        if n >= 2:
                            pe.wait_ge(num_taken, n - 1)
                        for d in range(2):
                            o = PN[:, n % 2, d * 256:d * 256 + P + 1]
                            mm = pe.matmul(o, EE[:, t, d, h, :], MVA[:, t, h, :], start=True, stop=(t == 0))
                            if t:
                                c = C0 if (t == 1) == (d == 0) else CU
                                mm = pe.matmul(o, QS[:, t - 1, d, h, :], c[:, d, h, :], start=False, stop=True)
                        mm.then_inc(num_done, 1)

                @block.scalar
                def _(act):
                    a = Steps(act, a_step)
                    a.seq(act.activation(LF[:, :], FF[:, :], ACT.Abs))
                    a.seq(act.activation(LF[:, :], LF[:, :], ACT.Exp, scale=-1.0))
                    act.activation(LF[:, :], LF[:, :], ACT.Ln, bias=1.0).then_inc(ln_done, 1)
                    act.wait_ge(m_ready, 1)
                    act.activation(EM[:, :], NM[:, :], ACT.Exp, scale=-1.0).then_inc(em_ready, 1)
                    act.wait_ge(win_sub, 6)
                    a.mark(act.activation(WOLD[:, :, :], WOLD[:, :, :], ACT.Exp))
                    act.activation(WIN[:, :, :], WIN[:, :, :], ACT.Exp).then_inc(win_exp, 1)
                    a.wait()
                    u4 = 0
                    for u, (t, d) in enumerate(UNITS):
                        if t:
                            act.wait_ge(q_sub, u4 + 1)
                            q = QS[:, t - 1, d, :, :]
                            act.activation(q, q, ACT.Exp, scale=-1.0).then_inc(q_exp, 1)
                            u4 += 1
                        act.wait_ge(e_sub, u + 1)
                        e = EE[:, t, d, :, :]
                        act.activation(e, e, ACT.Exp, scale=-1.0).then_inc(e_exp, 1)
                    act.wait_ge(win_exp, 1)
                    for h in range(H):
                        act.wait_ge(kt_done, h + 1)
                        if h >= 2:
                            act.wait_ge(cu_done, h - 1)
                        for n, (t, d) in enumerate(KINDS):
                            ins = act.activation(KW[:, h % 2, n, :], PK[:, t * P:(t + 1) * P], ACT.Copy, scale=WIN[:, n, h:h + 1])
                        ins.then_inc(k_rows, 1)

                @block.vector
                def _(dve):
                    v = Steps(dve, v_step)
                    dve.wait_ge(ln_done, 1)
                    v.seq(dve.scalar_tensor_tensor(LF[:, :], FF[:, :], 0.0, LF[:, :], ALU.min, ALU.subtract))
                    dve.wait_ge(zeroed, 5)
                    dve.wait_ge(m_in, 32)

                    def rows(x, t, d):
                        a = x[32 * d:32 * d + H, t * P:(t + 1) * P]
                        return a[:, ::-1] if d else a

                    for t, d in UNITS:
                        v.mark(dve.tensor_tensor_scan(rows(BB, t, d), ONE[32 * d:32 * d + H, :], rows(LF, t, d), 0.0, ALU.mult, ALU.add))
                    v.wait()
                    v.seq(dve.tensor_tensor(CR[:, :], LI[:, :], BB[:, :], ALU.subtract))
                    for t, d in ((0, 0), (0, 1), (1, 0), (2, 1), (2, 0), (1, 1)):
                        r = slice(32 * d, 32 * d + H)
                        last = lambda x, t: x[r, t * P + (0 if d else P - 1):t * P + (1 if d else P)]
                        if t:
                            first = (t == 1) == (d == 0)
                            before = 3 - t
                            v.seq(dve.tensor_copy(SM[r, t, 1:2], M0[r, :]) if first else
                                  dve.tensor_tensor(SM[r, t, 1:2], last(BB, before), last(MM, before), ALU.add))
                        v.seq(dve.tensor_tensor_scan(rows(MM, t, d), rows(CR, t, d), rows(CR, t, d), SM[r, t, 1:2], ALU.max, ALU.max))
                        v.mark(dve.tensor_copy(SM[r, t, 0:1], last(MM, t)))
                    v.wait()
                    dve.tensor_tensor(NM[:, :], BB[:, :], MM[:, :], ALU.add).then_inc(m_ready, 1)
                    dve.wait_ge(cols_done, 1)
                    dve.tensor_copy(COL[:, :, :, :], PK[:, 0:6 * R].rearrange("p (n t r) -> p n t r", n=2, t=TT)).then_inc(cols_ready, 1)
                    dve.wait_ge(small_done, 1)
                    dve.tensor_copy(MC[:, :, :, :], PA[:, 0:48].rearrange("p (n t j) -> p n t j", n=2 * H, t=TT)).then_inc(small_ready, 1)
                    dve.wait_ge(cols_ready, 1)
                    dve.wait_ge(small_ready, 1)
                    for j, (t, d) in enumerate(KINDS[2:]):
                        m = MC[:, d * H:(d + 1) * H, t, :]
                        dve.tensor_tensor(WOLD[:, j, :], m[:, :, 1], m[:, :, 0], ALU.subtract).then_inc(win_sub, 1)
                    for n, (t, d) in enumerate(KINDS):
                        dve.tensor_tensor(WIN[:, n, :], COL[:, 0, t, 32 * d:32 * d + H], MC[:, d * H:(d + 1) * H, t, 0],
                                          ALU.subtract).then_inc(win_sub, 1)
                    for u, (t, d) in enumerate(UNITS):
                        dve.wait_ge(mb_done, u + 1)
                        mb = PB[:, u % 2, :].rearrange("p (h l) -> p h l", h=H)
                        if t:
                            dve.tensor_tensor(QS[:, t - 1, d, :, :], mb, MC[:, d * H:(d + 1) * H, t, 1:2].broadcast_to([P, H, P]),
                                              ALU.subtract).then_inc(q_sub, 1)
                        e = EE[:, t, d, :, :]
                        dve.tensor_tensor(e, mb, COL[:, 0, t, 32 * d:32 * d + H].unsqueeze(2).broadcast_to([P, H, P]),
                                          ALU.subtract).then_inc(mb_taken, 1)
                        dve.wait_ge(mb_taken, u + 1)
                        dve.tensor_scalar_max(e, e, 0.0).then_inc(e_sub, 1)
                    for h in range(H):
                        dve.wait_ge(att_done, h + 1)
                        for d in range(2):
                            keep = CST[:, (C_KEEPB if d else C_KEEPF):(C_KEEPB if d else C_KEEPF) + P]
                            ins = dve.tensor_tensor(AM[:, d, h, :, :], PA[:, 0:T].rearrange("p (t l) -> p t l", t=TT),
                                                    keep.unsqueeze(1).broadcast_to([P, TT, P]), ALU.mult)
                        ins.then_inc(att_taken, 1)
                    dve.wait_ge(att_taken, H)
                    for u, (t, d) in enumerate(UNITS):
                        dve.wait_ge(e_exp, u + 1)
                        e = EE[:, t, d, :, :]
                        dve.tensor_tensor(e, e, AM[:, d, :, t, :], ALU.mult).then_inc(wt_ready, 1)
                    for n, (t, d) in enumerate(scale_in):
                        dve.wait_ge(q_exp, n + 1)
                        q = QS[:, t - 1, d, :, :]
                        dve.tensor_tensor(q, q, QKT[:, 2 * H:3 * H, t * P:(t + 1) * P], ALU.mult).then_inc(q_ready, 1)
                    dve.wait_ge(win_exp, 1)
                    dve.wait_ge(a_step, 3)
                    dve.wait_ge(s_in, 16)
                    for h in range(H):
                        dve.wait_ge(cu_done, h + 1)
                        dve.tensor_copy(NC[:, :, h, :], PC[:, 0, 0:2 * (P + 1)].rearrange("p (d e) -> p d e", d=2))
                        for d in range(2):
                            ins = dve.scalar_tensor_tensor(CU[:, d, h, :], C0[:, d, h, :], WOLD[:, d, h:h + 1],
                                                           PC[:, 1, d * (P + 1):(d + 1) * (P + 1)], ALU.mult, ALU.add)
                        ins.then_inc(cu_taken, 1)
                    for n in range(TT * H):
                        t, h = divmod(n, H)
                        b = n % 2
                        dve.wait_ge(num_done, n + 1)
                        num = PN[:, b, :].rearrange("p (d e) -> p d e", d=2)
                        v.seq(dve.scalar_tensor_tensor(DEN[:, b, :], num[:, :, P], -1.0, COL[:, 1, t, h:h + 33:32], ALU.mult, ALU.max))
                        v.seq(dve.tensor_tensor(DEN[:, b, :], num[:, :, P], DEN[:, b, :], ALU.max))
                        v.seq(dve.reciprocal(DEN[:, b, :], DEN[:, b, :]))
                        v.seq(dve.tensor_scalar(HB[:, b, :], num[:, 0, 0:P], DEN[:, b, 0:1], None, ALU.mult))
                        dve.scalar_tensor_tensor(HB[:, b, :], num[:, 1, 0:P], DEN[:, b, 1:2], HB[:, b, :],
                                                 ALU.mult, ALU.add).then_inc(num_taken, 1)
                        dve.wait_ge(num_taken, n + 1)
                        v.mark(dve.tensor_tensor(MIX[:, t, H + h, :], HB[:, b, :], MO[:, t, h * P:(h + 1) * P], ALU.mult))
                    v.wait()

        modulation(0)
        with ExitStack() as ev:
            HT = sb(ev, "HT", [P, KB, T])
            QKT = sb(ev, "qk_t", [P, 4 * H, T])
            RV = sb(ev, "ret_v", [P, TT, H, P])
            RG = sb(ev, "ret_gate", [P, TT, HW])
            MVA = sb(ev, "ml_v", [P, TT, H, P + 1])
            MO = sb(ev, "ml_gate", [P, TT, HW])
            LI = sb(ev, "log_i", [64, T])
            FF = sb(ev, "forget", [64, T])
            RT = (sb(ev, "ret_dt", [P, H, P]), sb(ev, "ret_qd", [P, 2 * H, P]), sb(ev, "ret_kd", [P, 2 * H]),
                  sb(ev, "ret_cd", [P, 2 * H]))
            with ExitStack() as pr:
                SLOTS = 4
                W = sb(pr, "even_w_ring", [P, SLOTS, KB, CH])
                w_in = [sem(pr, f"even_w_in{n}") for n in range(SLOTS)]
                transpose_modulate(HT, 0, 0, ahead=[(W[:, n], I["even_w"][n], w_in[n]) for n in range(SLOTS)])
                even_project(HT, W, w_in, QKT, RV, RG, MVA, MO, LI, FF, RT)
            MIX = sb(ev, "mix", [P, TT, 2 * H, P])
            retention(QKT, RV, MIX, RT)
            WO = sb(ev, "w_out", [P, 2, KB, CH])
            wo_in = sem(ev, "w_out_in")
            mlstm(QKT, MVA, MO, LI, FF, MIX, [(WO[:, n], I["even_w_out"][n], wo_in) for n in range(2)])
            out_project(MIX, HT, WO, wo_in, 0, RG)
        peer(0)
        renew_semaphores()
        with ExitStack() as od:
            HT = sb(od, "HT", [P, KB, T])
            Z = sb(od, "odd_rows", [P, TT, 2304])
            GS = sb(od, "gk_swapped", [P, TT, P])
            MIX = sb(od, "mix", [P, TT, 2 * H, P])
            with ExitStack() as pr:
                NW, NCH = 384, 6
                W = sb(pr, "odd_w", [P, NCH, KB, NW])
                w_in = [sem(pr, f"odd_w_in{n}") for n in range(NCH)]
                transpose_modulate(HT, 1, 0, ahead=[(W[:, n], I["odd_w"][n], w_in[n]) for n in range(NCH)])
                odd_project(HT, W, w_in, Z, GS)
            WO = sb(od, "w_out", [P, 2, KB, CH])
            wo_in = sem(od, "w_out_in")
            attend(Z, GS, MIX, [(WO[:, n], I["odd_w_out"][n], wo_in) for n in range(2)])
            out_project(MIX, HT, WO, wo_in, 1)
        peer(1, O["y"])


def constants():
    c = np.zeros((P, C_ALL), np.float32)
    i = np.arange(P, dtype=np.float32)
    c[:, C_IDENT:C_IDENT + P] = np.eye(P)
    c[:, C_IOTA:C_IOTA + P] = i
    rel = i[None, :] - i[:, None]
    c[:, C_KEEPF:C_KEEPF + P] = rel >= 0
    c[:, C_KEEPB:C_KEEPB + P] = rel <= 0
    c[:, C_RELF:C_RELF + P] = np.maximum(rel, 0)
    c[:, C_RELB:C_RELB + P] = np.maximum(-rel, 0)
    c[:, C_IDX] = i
    c[:, C_IDX + 1] = P - 1 - i
    for n in range(8):
        c[32 * (n // H) + n % H, C_SEL + n * P:C_SEL + (n + 1) * P] = 1
    nf = HD // 4
    inv = (np.float32(10000.0) ** (-np.arange(nf, dtype=np.float32) / np.float32(nf))).astype(np.float32)
    pos = np.arange(2 * P)
    for t in range(2):
        at = pos[t * P:(t + 1) * P]
        for axis, where in enumerate((at // 64, at % 64)):
            ang = where.astype(np.float32)[:, None] * inv[None, :]
            o = t * 32 + axis * nf
            c[:, C_COS + o:C_COS + o + nf] = np.cos(ang)
            c[:, C_SIN + o:C_SIN + o + nf] = np.sin(ang)
    return c


def chunked(w, n=CH):
    k, cols = w.shape
    return np.ascontiguousarray(w.reshape(k // P, P, cols // n, n).transpose(2, 1, 0, 3))


def layout(**a):
    a = {k: np.asarray(v) for k, v in a.items()}
    w = a["even_w_in"][0]
    part = [w[:, n * HW:(n + 1) * HW] for n in range(8)]
    wo = a["odd_w_in"][0]
    gq, gk, gv, dq, dk, dv = np.split(wo, np.cumsum([512, 128, 128, 512, 512]), axis=1)
    cols = lambda v: np.ascontiguousarray(v.reshape(-1, P).T)
    d = {
        "x": np.concatenate([a["x_prompt"].reshape(1, P, D), a["x_sample"].reshape(2, P, D)]),
        "consts": constants(),
        "cond_t": np.ascontiguousarray(np.stack([cols(a["c_ctx"]), cols(a["c"][0])], axis=2)),
        "ada_w": np.concatenate([chunked(a["ada_w"][l]) for l in range(DEPTH)]),
        "ada_b_t": cols(a["ada_b"].reshape(-1)),
        "ln_g": a["ln_g"], "ln_b": a["ln_b"],
        "even_w": chunked(np.concatenate([part[n] for n in (0, 1, 4, 5, 2, 3, 6, 7)], axis=1)),
        "even_w_gate": np.ascontiguousarray(w[:, 8 * HW:].reshape(KB, P, 4, H).transpose(2, 1, 0, 3)),
        "even_b_gate": a["even_b_gate"].reshape(4, H, 1),
        "ret_logit": a["ret_decay_logit"].reshape(1, 2 * H),
        "gn_g": np.concatenate([a["ret_gn_g"], a["ml_gn_g"]]).reshape(1, 2 * HW),
        "even_w_out": chunked(a["even_w_out"][0]),
        "state_ret": np.ascontiguousarray(a["state_ret"][0, 0].transpose(2, 0, 1, 3)),
        "state_mlstm": np.ascontiguousarray(np.concatenate(
            [a["state_mlstm_C"][0, 0], a["state_mlstm_n"][0, 0][..., None]], axis=-1).transpose(2, 0, 1, 3)),
        "state_m": a["state_mlstm_m"].reshape(2, H, 1),
        "odd_w": chunked(np.concatenate([gq, gk, dq, dk, gv, dv], axis=1), 384),
        "qk_norm_g": np.stack([a["q_norm_g"][0], a["k_norm_g"][0]]).reshape(1, 2 * HD),
        "diff_lambda": a["diff_lambda"].reshape(1, 4 * HD),
        "diff_subln_g": a["diff_subln_g"].reshape(1, P),
        "odd_w_out": chunked(a["odd_w_out"][0]),
        "cache_gk": a["cache_gqa_k"].reshape(P, P), "cache_gv": a["cache_gqa_v"].reshape(P, P),
        "cache_dk": a["cache_diff_k"].reshape(P, HW), "cache_dv": a["cache_diff_v"].reshape(P, HW),
        "peer_w_q": np.stack([chunked(a["peer_w_q"][l]) for l in range(DEPTH)]),
        "peer_keys": np.ascontiguousarray(a["peer_sub_keys"].transpose(0, 3, 1, 2)),
        "peer_u": np.ascontiguousarray(a["peer_u"].reshape(DEPTH, N_KEYS, N_KEYS // JC, JC, KB, P)
                                       .transpose(0, 2, 5, 3, 4, 1)),
        "peer_v": np.ascontiguousarray(a["peer_v"].reshape(DEPTH, N_KEYS, N_KEYS // JC, JC, D)
                                       .transpose(0, 2, 1, 3, 4)),
    }
    return {k: np.ascontiguousarray(v) for k, v in d.items()}


OUTS = {
    "y": (TT, P, D),
    "new_ret": (P, 2, H, P),
    "new_mlstm": (P, 2, H, P + 1),
    "new_m": (2, H, 1),
    "new_gk": (P, P), "new_gv": (P, P), "new_dk": (P, HW), "new_dv": (P, HW),
}


def kernel(**inputs):
    import concourse.bacc as bacc
    from concourse.bass_utils import run_bass_kernel_spmd

    nc = bacc.Bacc("TRN2", target_bir_lowering=False, num_devices=1)
    arrays = layout(**inputs)
    I = {n: nc.dram_tensor(f"in_{n}", v.shape, mybir.dt.from_np(v.dtype), kind="ExternalInput").ap()
         for n, v in arrays.items()}
    O = {n: nc.dram_tensor(f"out_{n}", s, F32, kind="ExternalOutput").ap() for n, s in OUTS.items()}
    build(nc, I, O)
    r = run_bass_kernel_spmd(nc, [{f"in_{n}": v for n, v in arrays.items()}], core_ids=[0]).results[0]
    got = {n: r[f"out_{n}"] for n in OUTS}
    state = lambda s: s.transpose(1, 2, 0, 3)[None, None]
    return (got["y"][0:1], got["y"][1:3].reshape(1, 2 * P, D), state(got["new_ret"]),
            state(got["new_mlstm"][..., :P]), state(got["new_mlstm"])[..., P], got["new_m"].reshape(1, 1, 2, H),
            got["new_gk"].reshape(1, 1, P, KV_HEADS, HD), got["new_gv"].reshape(1, 1, P, KV_HEADS, HD),
            got["new_dk"].reshape(1, 1, P, H, 2, HD), got["new_dv"].reshape(1, 1, P, H, P))
```
